# Optimizing a Trainium2 kernel written in Bass

```python
import math
import jax
import jax.numpy as jnp
from jax import lax
import numpy as np

D_MODEL = 1024
BATCH = 1
SEQ = 256
DEPTH = 1

N_MEM = 256
N_GROUPS = 4
GW = D_MODEL // N_GROUPS
D_MIX = N_GROUPS * GW
HEAD_DIM = 64
S5_GROUP = 16
S5_GROUPS = GW // S5_GROUP
S5_STATE = 64
ML_HEADS = GW // HEAD_DIM
ML_CHUNK = 64
CONV_K = 4
RW_HEADS = GW // HEAD_DIM
RW_DECAY_RANK = 64
RW_A_RANK = 64
RW_GATE_RANK = 128
RW_GN_EPS = 64e-5
MB_HEADS = GW // HEAD_DIM
MOBA_BLOCK = 256
MOBA_TOPK = 3
MOBA_QCHUNK = 16
REL_BUCKETS = 32
REL_MAX_DIST = 128
XA_HEADS = 4
XA_HEAD_DIM = D_MODEL // XA_HEADS
D_FF = ((8 * D_MODEL + 3 * 256 - 1) // (3 * 256)) * 256
ML_COLS = 4 * GW + 2 * ML_HEADS
RW_COLS = 3 * GW + RW_DECAY_RANK + RW_A_RANK + RW_GATE_RANK
MB_COLS = 3 * GW
D_IN = GW + ML_COLS + RW_COLS + MB_COLS
RMS_EPS = 1e-6

kernel_name = 'hybrid_s5_mlstm_rwkv7_moba_trunk'

def rms_norm(x, g):
    xf = x.astype(jnp.float32)
    y = xf * lax.rsqrt(jnp.mean(xf * xf, axis=-1, keepdims=True) + RMS_EPS)
    return (y * g.astype(jnp.float32)).astype(x.dtype)

def split_cols(t, sizes):
    out, start = [], 0
    for s in sizes:
        out.append(t[..., start:start + s])
        start += s
    return out

def causal_dwconv(x, w):
    k, c = w.shape
    return lax.conv_general_dilated(x, w[:, None, :].astype(x.dtype), window_strides=(1,),
                                    padding=[(k - 1, 0)], dimension_numbers=('NWC', 'WIO', 'NWC'),
                                    feature_group_count=c)

def t5_bucket(rel):
    n = jnp.maximum(rel, 0)
    max_exact = REL_BUCKETS // 2
    nf = jnp.maximum(n, 1).astype(jnp.float32)
    large = max_exact + (jnp.log(nf / max_exact) / math.log(REL_MAX_DIST / max_exact)
                         * (REL_BUCKETS - max_exact)).astype(jnp.int32)
    return jnp.where(n < max_exact, n, jnp.minimum(large, REL_BUCKETS - 1))

def _complex_affine_combine(e1, e2):
    a1r, a1i, b1r, b1i = e1
    a2r, a2i, b2r, b2i = e2
    return (a2r * a1r - a2i * a1i, a2r * a1i + a2i * a1r,
            a2r * b1r - a2i * b1i + b2r, a2r * b1i + a2i * b1r + b2i)

def s5_mixer(u, lam_re, lam_im, log_step, b_re, b_im, c_re, c_im, d_skip, w_glu, b_glu):
    f32 = jnp.float32
    bsz, seq, _ = u.shape
    ug = u.astype(f32).reshape(bsz, seq, S5_GROUPS, S5_GROUP)
    lr, li = lam_re.astype(f32), lam_im.astype(f32)
    step = jnp.exp(log_step.astype(f32))[:, None]
    mag = jnp.exp(lr * step)
    ang = li * step
    ab_re, ab_im = mag * jnp.cos(ang), mag * jnp.sin(ang)
    den = lr * lr + li * li
    co_re = ((ab_re - 1.0) * lr + ab_im * li) / den
    co_im = (ab_im * lr - (ab_re - 1.0) * li) / den
    br, bi = b_re.astype(f32), b_im.astype(f32)
    bb_re = co_re[..., None] * br - co_im[..., None] * bi
    bb_im = co_re[..., None] * bi + co_im[..., None] * br
    bu_re = jnp.einsum('blgh,gph->blgp', ug, bb_re)
    bu_im = jnp.einsum('blgh,gph->blgp', ug, bb_im)
    a_re = jnp.broadcast_to(ab_re, (1, seq) + ab_re.shape)
    a_im = jnp.broadcast_to(ab_im, (1, seq) + ab_im.shape)
    _, _, xs_re, xs_im = lax.associative_scan(_complex_affine_combine,
                                              (a_re, a_im, bu_re, bu_im), axis=1)
    y = (jnp.einsum('blgp,ghp->blgh', xs_re, c_re.astype(f32))
         - jnp.einsum('blgp,ghp->blgh', xs_im, c_im.astype(f32)))
    y = y.reshape(bsz, seq, GW) + d_skip.astype(f32) * u.astype(f32)
    z = jax.nn.gelu(y)
    return z * jax.nn.sigmoid(z @ w_glu.astype(f32) + b_glu.astype(f32))

def mlstm_mixer(p, conv_w, i_bias, f_bias):
    f32 = jnp.float32
    bsz, seq, _ = p.shape
    nc, cl, nh, dh = seq // ML_CHUNK, ML_CHUNK, ML_HEADS, HEAD_DIM
    q, k, v, o, i_pre, f_pre = split_cols(p, (GW, GW, GW, GW, nh, nh))
    qk = jax.nn.silu(causal_dwconv(jnp.concatenate([q, k], axis=-1), conv_w))
    q, k = qk[..., :GW], qk[..., GW:]

    def heads(t):
        return t.astype(f32).reshape(bsz, nc, cl, nh, dh).transpose(0, 3, 1, 2, 4)

    def gate(t, bias):
        return (t.astype(f32) + bias.astype(f32)).reshape(bsz, nc, cl, nh).transpose(0, 3, 1, 2)

    qh, kh, vh = heads(q), heads(k) * dh ** -0.5, heads(v)
    log_i = gate(i_pre, i_bias)
    bcum = jnp.cumsum(jax.nn.log_sigmoid(gate(f_pre, f_bias)), axis=-1)
    causal = jnp.tril(jnp.ones((cl, cl), dtype=bool))
    dmat = jnp.where(causal, bcum[..., :, None] - bcum[..., None, :] + log_i[..., None, :], -jnp.inf)
    b_last = bcum[..., -1]
    w_st = b_last[..., None] - bcum + log_i
    m_in = jnp.max(w_st, axis=-1)
    e_st = jnp.exp(w_st - m_in[..., None])
    kv_ch = jnp.einsum('bhcs,bhcsk,bhcsv->bhckv', e_st, kh, vh)
    k_ch = jnp.einsum('bhcs,bhcsk->bhck', e_st, kh)

    def chunk_step(carry, xs):
        c_st, n_st, m_st = carry
        bl, mi, kv, ks = xs
        m_new = jnp.maximum(bl + m_st, mi)
        a = jnp.exp(bl + m_st - m_new)
        e = jnp.exp(mi - m_new)
        c_new = a[..., None, None] * c_st + e[..., None, None] * kv
        n_new = a[..., None] * n_st + e[..., None] * ks
        return (c_new, n_new, m_new), (c_st, n_st, m_st)

    init = (jnp.zeros((bsz, nh, dh, dh), f32), jnp.zeros((bsz, nh, dh), f32), jnp.zeros((bsz, nh), f32))
    xs = tuple(jnp.moveaxis(t, 2, 0) for t in (b_last, m_in, kv_ch, k_ch))
    _, (c_prev, n_prev, m_prev) = lax.scan(chunk_step, init, xs)
    c_prev = jnp.moveaxis(c_prev, 0, 2)
    n_prev = jnp.moveaxis(n_prev, 0, 2)
    m_prev = jnp.moveaxis(m_prev, 0, 2)
    b_inter = bcum + m_prev[..., None]
    m_comb = jnp.maximum(b_inter, jnp.max(dmat, axis=-1))
    w_inter = jnp.exp(b_inter - m_comb)
    s = jnp.exp(dmat - m_comb[..., None]) * jnp.einsum('bhctd,bhcsd->bhcts', qh, kh)
    num = (jnp.einsum('bhcts,bhcsv->bhctv', s, vh)
           + w_inter[..., None] * jnp.einsum('bhctk,bhckv->bhctv', qh, c_prev))
    den = jnp.sum(s, axis=-1) + w_inter * jnp.einsum('bhctk,bhck->bhct', qh, n_prev)
    h = num / jnp.maximum(jnp.abs(den), jnp.exp(-m_comb))[..., None]
    h = h.transpose(0, 2, 3, 1, 4).reshape(bsz, seq, GW)
    return jax.nn.sigmoid(o.astype(f32)) * h

def rwkv7_mixer(p, mu, w0, w2, a0, a2, g2, k_k, k_a, r_k, ln_w, ln_b):
    f32 = jnp.float32
    bsz, seq, _ = p.shape
    nh, dh = RW_HEADS, HEAD_DIM
    p = p.astype(f32)
    prev = jnp.pad(p, ((0, 0), (1, 0), (0, 0)))[:, :-1]
    p = p + (prev - p) * mu.astype(f32)
    r, k, v, w_lo, a_lo, g_lo = split_cols(p, (GW, GW, GW, RW_DECAY_RANK, RW_A_RANK, RW_GATE_RANK))
    w = -jax.nn.softplus(-(w0.astype(f32) + jnp.tanh(w_lo) @ w2.astype(f32))) - 0.5
    decay = jnp.exp(-jnp.exp(w))
    a = jax.nn.sigmoid(a0.astype(f32) + a_lo @ a2.astype(f32))
    g = jax.nn.sigmoid(g_lo) @ g2.astype(f32)

    def heads(t):
        return t.reshape(bsz, seq, nh, dh)

    kk = heads(k * k_k.astype(f32))
    kk = kk * lax.rsqrt(jnp.sum(kk * kk, axis=-1, keepdims=True) + 1e-12)
    k = k * (1.0 + (a - 1.0) * k_a.astype(f32))
    rh, kh, vh, wh, ah = heads(r), heads(k), heads(v), heads(decay), heads(a)

    def time_step(state, xs):
        r_t, w_t, k_t, v_t, kk_t, kka_t = xs
        sa = jnp.einsum('bhvk,bhk->bhv', state, -kk_t)
        state = (state * w_t[:, :, None, :] + sa[..., None] * kka_t[:, :, None, :]
                 + v_t[..., None] * k_t[:, :, None, :])
        return state, jnp.einsum('bhvk,bhk->bhv', state, r_t)

    xs = tuple(jnp.moveaxis(t, 1, 0) for t in (rh, wh, kh, vh, kk, kk * ah))
    _, y = lax.scan(time_step, jnp.zeros((bsz, nh, dh, dh), f32), xs)
    y = jnp.moveaxis(y, 0, 1)
    mean = jnp.mean(y, axis=-1, keepdims=True)
    var = jnp.mean(jnp.square(y - mean), axis=-1, keepdims=True)
    y = ((y - mean) * lax.rsqrt(var + RW_GN_EPS) * ln_w.astype(f32).reshape(nh, dh)
         + ln_b.astype(f32).reshape(nh, dh))
    bonus = jnp.sum(rh * kh * r_k.astype(f32).reshape(nh, dh), axis=-1, keepdims=True) * vh
    return (y + bonus).reshape(bsz, seq, GW) * g

def moba_mixer(p, rel_bias):
    f32 = jnp.float32
    bsz, seq, _ = p.shape
    nh, dh, bs, qc = MB_HEADS, HEAD_DIM, MOBA_BLOCK, MOBA_QCHUNK
    nb = -(-seq // bs)
    k_sel_n = max(1, min(MOBA_TOPK, nb - 1))
    nqc = seq // qc
    q, k, v = split_cols(p, (GW, GW, GW))

    def heads(t):
        return t.astype(f32).reshape(bsz, seq, nh, dh).transpose(0, 2, 1, 3)

    qh = heads(q) * dh ** -0.5
    pad = ((0, 0), (0, 0), (0, nb * bs - seq), (0, 0))
    kb = jnp.pad(heads(k), pad).reshape(bsz, nh, nb, bs, dh)
    vb = jnp.pad(heads(v), pad).reshape(bsz, nh, nb, bs, dh)
    q_blk = jnp.arange(seq) // bs
    gate = jnp.einsum('bhld,bhnd->bhln', qh, jnp.mean(kb, axis=3))
    gate = jnp.where(jnp.arange(nb)[None, :] < q_blk[:, None], gate, -jnp.inf)
    _, sel = lax.top_k(gate, k_sel_n)
    q_ch = qh.reshape(bsz, nh, nqc, qc, dh).transpose(2, 0, 1, 3, 4)
    sel_ch = sel.reshape(bsz, nh, nqc, qc, k_sel_n).transpose(2, 0, 1, 3, 4)
    bias_t = rel_bias.astype(f32).T
    b_idx = jnp.arange(bsz)[:, None, None, None]
    h_idx = jnp.arange(nh)[None, :, None, None]
    offs = jnp.arange(bs)

    def query_chunk(args):
        c, q_c, sel_c = args
        qpos = c * qc + jnp.arange(qc)
        own = (c * qc) // bs
        k_g = kb[b_idx, h_idx, sel_c]
        v_g = vb[b_idx, h_idx, sel_c]
        kpos = sel_c[..., None] * bs + offs
        s_sel = (jnp.einsum('bhqd,bhqjtd->bhqjt', q_c, k_g)
                 + bias_t[h_idx[..., None], t5_bucket(qpos[:, None, None] - kpos)])
        ok = jnp.arange(k_sel_n) < own
        s_sel = jnp.where(ok[:, None], s_sel, -jnp.inf)
        k_o = lax.dynamic_index_in_dim(kb, own, axis=2, keepdims=False)
        v_o = lax.dynamic_index_in_dim(vb, own, axis=2, keepdims=False)
        rel = qpos[:, None] - (own * bs + offs)[None, :]
        s_own = jnp.einsum('bhqd,bhtd->bhqt', q_c, k_o) + bias_t[:, t5_bucket(rel)]
        s_own = jnp.where(rel >= 0, s_own, -jnp.inf)
        logits = jnp.concatenate([s_sel.reshape(bsz, nh, qc, k_sel_n * bs), s_own], axis=-1)
        probs = jax.nn.softmax(logits, axis=-1)
        p_sel = probs[..., :k_sel_n * bs].reshape(bsz, nh, qc, k_sel_n, bs)
        p_own = probs[..., k_sel_n * bs:]
        return (jnp.einsum('bhqjt,bhqjtd->bhqd', p_sel, v_g)
                + jnp.einsum('bhqt,bhtd->bhqd', p_own, v_o))

    out = lax.map(query_chunk, (jnp.arange(nqc), q_ch, sel_ch))
    return out.transpose(1, 0, 3, 2, 4).reshape(bsz, seq, GW)

def mixing_block(h, w_in, mix_out_gain, w_out, rel_bias,
                 s5_lam_re, s5_lam_im, s5_log_step, s5_b_re, s5_b_im, s5_c_re, s5_c_im,
                 s5_d, s5_w_glu, s5_b_glu, ml_conv, ml_i_bias, ml_f_bias,
                 rw_mu, rw_w0, rw_w2, rw_a0, rw_a2, rw_g2, rw_k_k, rw_k_a, rw_r_k, rw_ln_w, rw_ln_b):
    bsz, seq, _ = h.shape
    proj = h @ w_in
    u_s5, p_ml, p_rw, p_mb = split_cols(proj, (GW, ML_COLS, RW_COLS, MB_COLS))
    y_s5 = s5_mixer(u_s5, s5_lam_re, s5_lam_im, s5_log_step, s5_b_re, s5_b_im,
                    s5_c_re, s5_c_im, s5_d, s5_w_glu, s5_b_glu)
    y_ml = mlstm_mixer(p_ml, ml_conv, ml_i_bias, ml_f_bias)
    y_rw = rwkv7_mixer(p_rw, rw_mu, rw_w0, rw_w2, rw_a0, rw_a2, rw_g2,
                       rw_k_k, rw_k_a, rw_r_k, rw_ln_w, rw_ln_b)
    y_mb = moba_mixer(p_mb, rel_bias)
    y = jnp.concatenate([y_s5, y_ml, y_rw, y_mb], axis=-1).reshape(bsz, seq, N_GROUPS, GW)
    y = rms_norm(y, mix_out_gain.reshape(N_GROUPS, GW)).reshape(bsz, seq, D_MIX)
    return y @ w_out

def cross_attention(h, mem_n, wq, wkv, wo):
    f32 = jnp.float32
    bsz, seq, _ = h.shape
    m = mem_n.shape[1]
    q = (h @ wq).reshape(bsz, seq, XA_HEADS, XA_HEAD_DIM)
    kv = (mem_n @ wkv).reshape(bsz, m, 2, XA_HEADS, XA_HEAD_DIM)
    s = jnp.einsum('blhd,bmhd->bhlm', q, kv[:, :, 0]).astype(f32) * XA_HEAD_DIM ** -0.5
    probs = jax.nn.softmax(s, axis=-1)
    o = jnp.einsum('bhlm,bmhd->blhd', probs, kv[:, :, 1].astype(f32)).reshape(bsz, seq, D_MODEL)
    return o @ wo

def swiglu(h, w_in, w_out):
    gu = h @ w_in
    return (jax.nn.silu(gu[..., :D_FF]) * gu[..., D_FF:]) @ w_out

def setup_inputs(seed: int = 0) -> dict:
    key = jax.random.key(seed)
    ks = iter(jax.random.split(key, 64))
    f32 = jnp.float32
    D, G, P = D_MODEL, S5_GROUPS, S5_STATE

    def normal(shape, scale):
        return jax.random.normal(next(ks), shape, f32) * scale

    def gain(shape):
        return 1.0 + 0.02 * jax.random.normal(next(ks), shape, f32)

    n_idx = jnp.arange(P, dtype=f32)
    return {
        'x': normal((BATCH, SEQ, D), 1.0),
        'mem': normal((BATCH, N_MEM, D), 1.0),
        'rel_bias': normal((REL_BUCKETS, MB_HEADS), 0.5),
        'norm_pre_mix': gain((DEPTH, D)),
        'norm_post_mix': gain((DEPTH, D)),
        'norm_pre_xa': gain((DEPTH, D)),
        'norm_post_xa': gain((DEPTH, D)),
        'norm_pre_ffn': gain((DEPTH, D)),
        'norm_post_ffn': gain((DEPTH, D)),
        'norm_mem': gain((DEPTH, D)),
        'w_in': normal((DEPTH, D, D_IN), D ** -0.5),
        'mix_out_gain': gain((DEPTH, D_MIX)),
        'w_out': normal((DEPTH, D_MIX, D), D_MIX ** -0.5),
        's5_lam_re': -0.5 + normal((DEPTH, G, P), 0.01),
        's5_lam_im': math.pi * n_idx + normal((DEPTH, G, P), 0.01),
        's5_log_step': jax.random.uniform(next(ks), (DEPTH, G), f32, math.log(1e-3), math.log(1e-1)),
        's5_b_re': normal((DEPTH, G, P, S5_GROUP), (2 * S5_GROUP) ** -0.5),
        's5_b_im': normal((DEPTH, G, P, S5_GROUP), (2 * S5_GROUP) ** -0.5),
        's5_c_re': normal((DEPTH, G, S5_GROUP, P), (2 * P) ** -0.5),
        's5_c_im': normal((DEPTH, G, S5_GROUP, P), (2 * P) ** -0.5),
        's5_d': normal((DEPTH, GW), 0.5),
        's5_w_glu': normal((DEPTH, GW, GW), GW ** -0.5),
        's5_b_glu': normal((DEPTH, GW), 0.01),
        'ml_conv': normal((DEPTH, CONV_K, 2 * GW), CONV_K ** -0.5),
        'ml_i_bias': normal((DEPTH, ML_HEADS), 0.1),
        'ml_f_bias': jnp.linspace(3.0, 6.0, ML_HEADS, dtype=f32) + normal((DEPTH, ML_HEADS), 0.1),
        'rw_mu': jax.random.uniform(next(ks), (DEPTH, RW_COLS), f32),
        'rw_w0': jnp.linspace(-6.0, -1.0, GW, dtype=f32) + normal((DEPTH, GW), 0.1),
        'rw_w2': normal((DEPTH, RW_DECAY_RANK, GW), 0.5 * RW_DECAY_RANK ** -0.5),
        'rw_a0': normal((DEPTH, GW), 0.1),
        'rw_a2': normal((DEPTH, RW_A_RANK, GW), RW_A_RANK ** -0.5),
        'rw_g2': normal((DEPTH, RW_GATE_RANK, GW), RW_GATE_RANK ** -0.5),
        'rw_k_k': 0.85 + normal((DEPTH, GW), 0.02),
        'rw_k_a': 1.0 + normal((DEPTH, GW), 0.02),
        'rw_r_k': normal((DEPTH, GW), 0.1),
        'rw_ln_w': gain((DEPTH, GW)),
        'rw_ln_b': normal((DEPTH, GW), 0.01),
        'xa_wq': normal((DEPTH, D, D), D ** -0.5),
        'xa_wkv': normal((DEPTH, D, 2 * D), D ** -0.5),
        'xa_wo': normal((DEPTH, D, D), D ** -0.5),
        'ffn_w_in': normal((DEPTH, D, 2 * D_FF), D ** -0.5),
        'ffn_w_out': normal((DEPTH, D_FF, D), D_FF ** -0.5),
    }

def reference(x, mem, rel_bias, norm_pre_mix, norm_post_mix, norm_pre_xa, norm_post_xa,
              norm_pre_ffn, norm_post_ffn, norm_mem, w_in, mix_out_gain, w_out,
              s5_lam_re, s5_lam_im, s5_log_step, s5_b_re, s5_b_im, s5_c_re, s5_c_im,
              s5_d, s5_w_glu, s5_b_glu, ml_conv, ml_i_bias, ml_f_bias,
              rw_mu, rw_w0, rw_w2, rw_a0, rw_a2, rw_g2, rw_k_k, rw_k_a, rw_r_k, rw_ln_w, rw_ln_b,
              xa_wq, xa_wkv, xa_wo, ffn_w_in, ffn_w_out):
    for l in range(DEPTH):
        h = rms_norm(x, norm_pre_mix[l])
        y = mixing_block(h, w_in[l], mix_out_gain[l], w_out[l], rel_bias,
                         s5_lam_re[l], s5_lam_im[l], s5_log_step[l], s5_b_re[l], s5_b_im[l],
                         s5_c_re[l], s5_c_im[l], s5_d[l], s5_w_glu[l], s5_b_glu[l],
                         ml_conv[l], ml_i_bias[l], ml_f_bias[l],
                         rw_mu[l], rw_w0[l], rw_w2[l], rw_a0[l], rw_a2[l], rw_g2[l],
                         rw_k_k[l], rw_k_a[l], rw_r_k[l], rw_ln_w[l], rw_ln_b[l])
        x = x + rms_norm(y, norm_post_mix[l]).astype(x.dtype)
        h = rms_norm(x, norm_pre_xa[l])
        y = cross_attention(h, rms_norm(mem, norm_mem[l]), xa_wq[l], xa_wkv[l], xa_wo[l])
        x = x + rms_norm(y, norm_post_xa[l]).astype(x.dtype)
        h = rms_norm(x, norm_pre_ffn[l])
        y = swiglu(h, ffn_w_in[l], ffn_w_out[l])
        x = x + rms_norm(y, norm_post_ffn[l]).astype(x.dtype)
    return x


_drawn_inputs = setup_inputs


def setup_inputs(seed=0):
    import zlib

    import numpy as np

    out = dict(_drawn_inputs(seed))
    spreads = {}
    factors = {'norm_post_mix': 3.602,
     'norm_pre_xa': 4.218,
     'norm_post_xa': 12.291,
     'norm_pre_ffn': 10.843,
     'norm_post_ffn': 24.445,
     'norm_mem': 3.02,
     'mix_out_gain': 3.74,
     's5_lam_re': 64.0,
     's5_b_glu': 8.0,
     'ml_i_bias': 8.0,
     'rw_w2': 4.485,
     'rw_a0': 4.125,
     'rw_k_k': 25.979,
     'rw_k_a': 7.046,
     'rw_ln_w': 8.0,
     'rw_ln_b': 25.944}
    for name, (base, spread) in spreads.items():
        noise = np.random.default_rng([zlib.crc32(name.encode()), seed]).standard_normal(out[name].shape)
        drawn = base * np.exp(spread * noise) if base else spread * noise
        out[name] = jnp.asarray(drawn.astype(out[name].dtype))
    for name, factor in factors.items():
        out[name] = (out[name] * factor).astype(out[name].dtype)
    return out
```

```python
import concourse.bass as bass
from concourse import mybir
from contextlib import ExitStack
import math

F32 = mybir.dt.float32
ALU = mybir.AluOpType
ACT = mybir.ActivationFunctionType
AX = mybir.AxisListType

P = 128
D = 1024
T = 256
NMEM = 256
KD = D // P
GW = 256
HD = 64
NH = GW // HD
C = 128
NC = T // C
DFF = 2816
NFF = DFF // P
XH, XD = 4, 256
EPS = 1e-6
NEG = -1e30
DECAY = math.exp(-0.5)
TAU = 6.2831850
ROUND = 12582912.0
GELU = 2.0 * math.sqrt(2.0 / math.pi)
LEVELS = 7


def columns(sizes):
    at, out = 0, {}
    for name, n in sizes:
        out[name] = (at, at + n)
        at += n
    return out, at


CONST, NCONST = columns([
    ("ident", P), ("ones", P), ("pair_ones", P), ("strict", P), ("incl", P), ("causal_add", 384),
    ("levels", LEVELS * P), ("level0_t", P), ("time", T), ("head_sel", NH * P), ("pair_sel", 2 * P),
    ("onehot", 384), ("eps6", 1), ("eps12", 1), ("eps_gn", 1), ("half_pi", 1),
])
PARAM, NPARAM = columns([
    ("mu", 8), ("w0", 2), ("a0", 2), ("k_k", 2), ("k_a", 2), ("r_k", 2), ("ln_w", 2), ("ln_b", 2),
    ("s5_d", 2), ("b_glu", 2), ("mix_gain", 8), ("conv", 16), ("pre_mix", 8), ("pre_xa", 8),
    ("pre_ffn", 8), ("norm_mem", 8), ("lam_re", 8), ("lam_im", 8), ("log_step", 8), ("i_bias", 1),
    ("f_bias", 1), ("rel", 4), ("w_gate", KD * 8), ("w2a2", GW), ("g2", GW), ("w_glu", 2 * GW),
    ("b_re", GW), ("b_im", GW), ("c_re", GW), ("c_im", GW),
])

W_IN_ORDER = ["rw_wag", "rw_k", "rw_r", "rw_v", "s5_u", "ml_q", "ml_k", "ml_v", "ml_o", "mb_q", "mb_k", "mb_v"]
SLOT = 2048
N_WIN, N_WKV, N_WOUT, N_WQ, N_WO = 12, 8, 4, 4, 4
N_FIN, N_FOUT = 2 * NFF // 2, NFF // 2
S_WKV = N_WIN
S_WOUT = S_WKV + N_WKV
S_WQ = S_WOUT + N_WOUT
S_WO = S_WQ + N_WQ
S_FIN = S_WO + N_WO
S_FOUT = S_FIN + N_FIN
NSLOTS = S_FOUT + N_FOUT


def trunk_kernel(nc, x_t, x_rows, mem_t, consts_d, params_d, weights_d, gains_d, rel_scratch, out):
    ctx = ExitStack()
    with ctx:
        def sb(name, n):
            return ctx.enter_context(nc.sbuf_tensor(name, [P, n], F32))

        def v3(ap, n):
            return ap.rearrange("p (a b) -> p a b", b=n)

        def v4(ap, m, n):
            return ap.rearrange("p (a b c) -> p a b c", b=m, c=n)

        def copies(ap, n):
            return ap.unsqueeze(1).to_broadcast([ap.shape[0], n, ap.shape[1]])

        def spread(ap, n):
            return ap.unsqueeze(2).to_broadcast([ap.shape[0], ap.shape[1], n])

        cst = sb("cst", NCONST)
        par = sb("par", NPARAM)
        hT = v3(sb("hT", KD * T)[:, :], T)
        memT = v3(sb("memT", KD * NMEM)[:, :], NMEM)
        kx = v3(sb("kx", KD * NMEM)[:, :], NMEM)
        vx = v3(sb("vx", 2 * D)[:, :], D)
        ring = sb("ring", 3 * SLOT)
        ARENA = 33000
        arena = sb("arena", ARENA)
        small = sb("small", 160)
        bank = [ctx.enter_context(nc.psum_tensor(f"bank{i}", [P, 512], F32)) for i in range(8)]

        def const(name, rows=P):
            a, b = CONST[name]
            return cst[0:rows, a:b]

        def prm(name, rows=P):
            a, b = PARAM[name]
            return par[0:rows, a:b]

        def flat(ap):
            return ap.rearrange("p a b -> p (a b)")

        def gain_rows(n):
            return bass.AP(gains_d.tensor, n * D, [[0, P], [1, D]])

        def carve(at, sizes):
            views = []
            for n in sizes:
                views.append(arena[:, at:at + n])
                at += n
            assert at <= ARENA, at
            return views, at

        (yT_, rwP_, rwM_, rwE_, KR_, Bh_, Kh_), at = carve(0, [8 * T, 8 * 257, 8 * T, 3 * 512, 1024, 512, 512])
        yT = v3(yT_, T)
        rwP = v3(rwP_, 257)
        rwM = v3(rwM_, T)
        kk, ab, G, Gp = (v3(rwP_[:, 512 * i:512 * i + 512], T) for i in range(4))
        rwE = rwE_.rearrange("p (e j t) -> p e j t", e=3, t=T)
        KR = KR_.rearrange("p (e j t) -> p e j t", e=2, t=T)
        Bh, Kh = v3(Bh_, T), v3(Kh_, T)
        rwg, bon = rwM[:, 0:2, :], rwM[:, 4:6, :]
        (A_, X_, XT_, Pm_, Mj_), at = carve(at, [4096, 1024, 1024, 1024, 1024])
        A = v3(A_, 512)
        X, XT, Pm, Mj = (a.rearrange("p (c h t) -> p c h t", c=NC, t=P) for a in (X_, XT_, Pm_, Mj_))
        sq_x, sq_m = v3(A_[:, 0:2048], T), v3(A_[:, 2048:4096], T)
        (Vt_, BKt_, R_, U_, S0_), at = carve(at, [512, 512, 256, 512, 256])
        Vt, BKt, U, S0 = v3(Vt_, 256), v3(BKt_, 256), v3(U_, 256), v4(S0_, 2, HD)
        (cos_, sin_, bu_, t1_, t2_, pr_, s5u_), at = carve(at, [2048, 2048, 1024, 512, 512, 2048, 512])
        cos, sin, t1, t2, s5u = (v3(a, T) for a in (cos_, sin_, t1_, t2_, s5u_))
        bu, pr = v4(bu_, 2, T), v4(pr_, 2, T)
        (raw_cv, E_, c2n_), at = carve(at, [4 * 259 + 1024, 4 * 384, 256])
        raw, cv = v3(raw_cv[:, 0:1036], 259), v3(raw_cv[:, 1036:2060], T)
        mlo, mlv = v3(G.rearrange("p a b -> p (a b)"), T), v3(Gp.rearrange("p a b -> p (a b)"), 256)
        E = v3(E_, 384)
        rows = [yT[:, i, :] for i in (4, 5, 6, 7, 1)]
        c_re, c_im, c_nre = v3(prm("c_re"), 32), v3(prm("c_im"), 32), v3(c2n_, 32)
        mqk, mbv = v3(rwE_[:, 0:1024], T), v3(rwE_[:, 1024:1536], 256)
        Bz = v3(rwP_[:, 0:1024], T)
        Sm, PTm = E, v3(raw_cv[:, 0:1536], 384)

        Yrw, Ysq = v3(Mj_[:, 0:512], T), v3(Mj_[:, 512:1024], T)
        z5y, z5a, z5, z5b = v3(bu_[:, 0:512], T), v3(bu_[:, 512:1024], T), t1, t2
        gn_sq = [v3(pr_[:, 0:512], T), Bh, rwM[:, 2:4, :], Kh]
        rstd_x, rstd_m = t1_[:, 0:T], yT_[:, 0:T]

        (xres_, tmp_, gain_, px_, ptx_, qx_, ox_, act_, fft_, late), _ = carve(
            8 * T, [2048, 2048, 1024, 2048, 2048, 2048, 2048, NFF * T, 1024, 5 * SLOT])
        xres, xtmp = v3(xres_, D), v3(tmp_, D)
        px = px_.rearrange("p (h t m) -> p h t m", t=2, m=NMEM)
        ptx = ptx_.rearrange("p (h m t) -> p h m t", m=2, t=T)
        qx, ox, act = v3(qx_, T), v3(ox_, T), v3(act_, T)
        fft = v3(fft_, 512)

        taken = [0]

        def cols(n):
            taken[0] += n
            assert taken[0] <= 160
            return small[:, taken[0] - n:taken[0]]

        neg_w0a0, neg_bglu, one_ka = cols(4), cols(2), cols(2)
        mid, carry = cols(4), cols(2)
        step, mag, frac, frn, co_re, co_im, den8, s8a, s8b, s8c = (cols(8) for _ in range(10))
        gcol = cols(8)
        nmax, mb_sum = cols(8), cols(8)
        ssq, rst = cols(8), cols(2)
        xmax, xsum = cols(8), cols(8)

        S = {name: ctx.enter_context(nc.semaphore(name)) for name in """
            rotated_back s5_out_used rw_level_mask rw_x0 rw_xt0 ml_qk mb_prob consts_in params_in
            sq_ready h_ready sq_m_ready rw_lowrank rw_kx_sq rw_mix rw_tilde ml_rows mem_ready ml_em
            rw_bonus rw_ysq s5_z gn_done xn_ready x_prob slot_used xres_in gain_in  rel_stored
            rel_in x_new out_stored zeros_ready s5_co s5_c rotating scanned sincos x_in mem_in
            rstd_x s5_step s5_decay theta rstd_m rw_exp neg_ready rw_inv rw_G rw_kk rw_E ml_gate
            ml_log ml_conv ml_silu ml_E mb_max mb_exp rw_rstd s5_arg s5_exp rw_out s5_out post_ssq
            post_sum pre_ssq x_max f_exp rw_diff rw_low rw_kx rw_G0 rw_a rw_k2 s5_co_step
            ml_row_step ml_sig ml_den mb_inv s5_step2 rw_tail s5_sig x_inv f_sig s5_sq s5_root ml_sq
            ml_root rw_sq rw_root mb_sq mb_root
            """.split()}
        loaded = [ctx.enter_context(nc.semaphore(f"slot_loaded{i}")) for i in range(8)]
        full = [ctx.enter_context(nc.semaphore(f"bank_full{i}")) for i in range(8)]
        free = [ctx.enter_context(nc.semaphore(f"bank_free{i}")) for i in range(8)]

        uses, count = {}, [0] * 8

        def pe_open(pe, name, b):
            uses[name] = (b, count[b])
            if count[b] > 0:
                pe.wait_ge(free[b], count[b])
            count[b] += 1
            return bank[b]

        def wait_full(eng, name):
            b, n = uses[name]
            eng.wait_ge(full[b], n + 1)
            return bank[b]

        def moved(eng, name):
            b, n = uses[name]
            eng.wait_ge(free[b], n + 1)

        def free_of(name):
            return free[uses[name][0]]

        def place(n):
            return n % 3 if n < S_WQ else (n - S_WQ) % 8

        users = [[n for n in range(NSLOTS) if place(n) == i] for i in range(8)]
        user_of = {}

        def slot(n):
            i = place(n)
            return ring[:, i * SLOT:(i + 1) * SLOT] if i < 3 else late[:, (i - 3) * SLOT:(i - 2) * SLOT]

        def pe_slot(pe, n):
            pe.wait_ge(loaded[place(n)], 16 * (users[place(n)].index(n) + 1))
            return slot(n)

        def at(h):
            return slice(HD * (h % 2), HD * (h % 2) + HD), h // 2

        block = ctx.enter_context(nc.Block())

        @block.tensor
        def _(pe):
            def mm(out_, lhsT, rhs, start=True, stop=True):
                return nc.tensor.matmul(out_, lhsT, rhs, start=start, stop=stop, skip_group_check=True)

            def channel_major(n, name, b, act):
                o, w = v3(pe_open(pe, name, b)[:, :], T), v3(pe_slot(pe, n), 256)
                for c in range(2):
                    for k in range(KD):
                        last = mm(o[:, c, :], w[:, k, c * P:(c + 1) * P], act[:, k, :], k == 0, k == KD - 1)
                last.then_inc(full[b], 1)
                user_of[n] = name

            def token_major(n, name, b, act):
                o, w = v3(pe_open(pe, name, b)[:, :], 256), v3(pe_slot(pe, n), 256)
                for m in range(2):
                    for k in range(KD):
                        last = mm(o[:, m, :], act[:, k, m * P:(m + 1) * P], w[:, k, :], k == 0, k == KD - 1)
                last.then_inc(full[b], 1)
                user_of[n] = name

            def sumsq(name, b, sq):
                o = pe_open(pe, name, b)
                for k in range(KD):
                    last = mm(o[:, 0:T], const("ones"), sq[:, k, :], k == 0, k == KD - 1)
                last.then_inc(full[b], 1)

            def wkv(i, b):
                if i < 4:
                    channel_major(S_WKV + i, f"wkv{i}", b, memT)
                else:
                    token_major(S_WKV + i, f"wkv{i}", b, memT)

            def s5_in(i, b):
                o = pe_open(pe, f"bu{i}", b)
                r, j = slice(32 * (i % 4), 32 * (i % 4) + 32), i // 4
                for e, w in enumerate(("b_re", "b_im")):
                    last = mm(o[:, e * T:(e + 1) * T], v3(prm(w), P)[r, j, :], s5u[r, j, :])
                last.then_inc(full[b], 1)

            def s5_out(q, b):
                o = pe_open(pe, "s5_y", b) if q == 0 else bank[b]
                pe.wait_ge(S["rotated_back"], q + 1)
                for i in (2 * q, 2 * q + 1):
                    y = o[32 * (i % 4):32 * (i % 4) + 32, (i // 4) * T:(i // 4 + 1) * T]
                    for n, (w, x) in enumerate(((c_re, 0), (c_nre, 1), (c_im, 2), (c_im, 3))):
                        last = mm(y, w[:, i, :], pr[:, x, i % 2, :], n == 0, n == 3)
                last.then_inc(full[b] if q == 3 else S["s5_out_used"], 1)

            def level_p(n, c, b):
                o = v3(pe_open(pe, f"P{n}{c}", b)[:, :], P)
                pe.wait_ge(S["rw_level_mask"], 2 * (n - 1) + c + 1)
                if n == 1:
                    pe.wait_ge(S["rw_x0"], c + 1)
                else:
                    moved(pe, f"X{n - 1}{c}")
                for h in range(NH):
                    last = mm(o[:, h, :], Mj[:, c, h, :], X[:, c, h, :])
                last.then_inc(full[b], 1)

            def level_x(n, c):
                moved(pe, f"P{n}{c}")
                if n == 1:
                    pe.wait_ge(S["rw_xt0"], 2 * c + 2)
                else:
                    moved(pe, f"T{n - 1}{c}")
                if n < LEVELS - 1:
                    b = 5 + 2 * c
                    o = v3(pe_open(pe, f"X{n}{c}", b)[:, :], P)
                    for h in range(NH):
                        last = mm(o[:, h, :], XT[:, c, h, :], Pm[:, c, h, :])
                    last.then_inc(full[b], 1)
                b = 4 + 2 * c
                o = v3(pe_open(pe, f"T{n}{c}", b)[:, :], P)
                for h in range(NH):
                    last = mm(o[:, h, :], Pm[:, c, h, :], XT[:, c, h, :])
                last.then_inc(full[b], 1)

            def ml_qk(h, b):
                o = pe_open(pe, f"qk{h}", b)
                pe.wait_ge(S["ml_qk"], 1)
                r, j = at(h)
                mm(o[:, 0:T], cv[r, 2 + j, 0:P], cv[r, j, :])
                mm(o[:, T:T + P], cv[r, 2 + j, P:T], cv[r, j, P:T]).then_inc(full[b], 1)

            def attend(name, b, values, probs):
                o = pe_open(pe, name, b)
                for h in range(NH):
                    r, j = at(h)
                    v0 = values[:, 0, h * HD:(h + 1) * HD] if values is not None else const("ones")[:, 0:HD]
                    v1 = values[:, 1, h * HD:(h + 1) * HD] if values is not None else const("ones")[:, 0:HD]
                    mm(o[r, j * T:(j + 1) * T], v0, probs[:, h, 0:T], True, False)
                    last = mm(o[r, j * T + P:(j + 1) * T], v1, probs[:, h, T:T + P], False, True)
                last.then_inc(full[b], 1)

            def mb_scores(h, b):
                o = pe_open(pe, f"sc{h}", b)
                moved(pe, "mb_k")
                r, j = at(h)
                mm(o[:, 0:P], mqk[r, j, 0:P], mqk[r, 2 + j, 0:P])
                mm(o[:, P:P + T], mqk[r, j, P:T], mqk[r, 2 + j, :]).then_inc(full[b], 1)

            def mb_turn(h, b):
                o = pe_open(pe, f"pt{h}", b)
                pe.wait_ge(S["mb_prob"], 1)
                for i in range(3):
                    last = nc.tensor.transpose(o[:, i * P:(i + 1) * P], Sm[:, h, i * P:(i + 1) * P], const("ident"))
                last.then_inc(full[b], 1)

            def group_sumsq(name, g, b):
                o = pe_open(pe, name, b)
                pe.wait_ge(S[("s5", "ml", "rw", "mb")[g] + "_sq"], 1)
                for j in range(2):
                    last = mm(o[:, 0:T], const("ones"), gn_sq[g][:, j, :], j == 0, j == 1)
                last.then_inc(full[b], 1)

            def solve_r(c, b):
                o = v3(pe_open(pe, f"R{c}", b)[:, 0:GW], HD)
                for h in range(NH):
                    r, j = at(h)
                    last = mm(o[:, h, :], A[:, c * NH + h, T:T + P], Vt[:, c, h * HD:(h + 1) * HD], True, c == 0)
                    if c == 1:
                        last = mm(o[:, h, :], KR[:, 0, j, P:T], S0[:, j, h % 2, :], False, True)
                last.then_inc(full[b], 1)

            def solve_u(c, b):
                o = v3(pe_open(pe, f"U{c}", b)[:, 0:GW], HD)
                moved(pe, f"T{LEVELS - 1}{c}")
                moved(pe, f"R{c}")
                for h in range(NH):
                    last = mm(o[:, h, :], XT[:, c, h, :], v3(R_, HD)[:, h, :])
                last.then_inc(full[b], 1)

            pe.wait_ge(S["consts_in"], 16)
            pe.wait_ge(S["params_in"], 16)
            for h in range(NH):
                o = pe_open(pe, f"rel{h}", 4 + h)
                mm(o[:, 0:384], prm("rel", 33)[:, h:h + 1].to_broadcast([33, P]), const("onehot", 33)).then_inc(full[4 + h], 1)
            pe.wait_ge(S["sq_ready"], 1)
            sumsq("x_sumsq", 0, sq_x)
            pe.wait_ge(S["h_ready"], 1)
            channel_major(0, "rw_wag", 1, hT)
            channel_major(1, "rw_k", 0, hT)
            pe.wait_ge(S["sq_m_ready"], 1)
            sumsq("mem_sumsq", 3, sq_m)
            channel_major(2, "rw_r", 1, hT)
            channel_major(3, "rw_v", 0, hT)
            o = v3(pe_open(pe, "rw_w", 2)[:, :], T)
            pe.wait_ge(S["rw_lowrank"], 1)
            for j in range(2):
                last = mm(o[:, j, :], prm("w2a2")[0:HD, j * P:(j + 1) * P], rwE[0:HD, 0, 0, :])
            last.then_inc(full[2], 1)
            o = v3(pe_open(pe, "rw_a", 3)[:, :], T)
            for j in range(2):
                last = mm(o[:, j, :], prm("w2a2")[HD:P, j * P:(j + 1) * P], rwM[HD:P, 0, :])
            last.then_inc(full[3], 1)
            channel_major(4, "s5_u", 1, hT)
            o = v3(pe_open(pe, "rw_g", 2)[:, :], T)
            for j in range(2):
                last = mm(o[:, j, :], prm("g2")[:, j * P:(j + 1) * P], rwE[:, 0, 1, :])
            last.then_inc(full[2], 1)
            channel_major(5, "ml_q", 0, hT)
            o = pe_open(pe, "rw_kk", 3)
            pe.wait_ge(S["rw_kx_sq"], 1)
            mm(o[:, :], const("pair_ones"), flat(rwE[:, 1])).then_inc(full[3], 1)
            channel_major(6, "ml_k", 1, hT)
            o = pe_open(pe, "gates", 2)
            for e in range(2):
                for k in range(KD):
                    last = mm(o[0:NH, e * T:(e + 1) * T], v3(prm("w_gate"), 8)[:, k, 4 * e:4 * e + 4],
                              hT[:, k, :], k == 0, k == KD - 1)
            last.then_inc(full[2], 1)
            moved(pe, "s5_u")
            s5_in(0, 0)
            s5_in(1, 1)
            o = v4(pe_open(pe, "rw_vt", 3)[:, :], 2, P)
            pe.wait_ge(S["rw_mix"], 4)
            for c in range(NC):
                for j in range(2):
                    last = nc.tensor.transpose(o[:, c, j, :], rwM[:, 6 + j, c * P:(c + 1) * P], const("ident"))
            last.then_inc(full[3], 1)
            token_major(7, "ml_v", 0, hT)
            channel_major(8, "ml_o", 1, hT)
            pe.wait_ge(S["rw_tilde"], 4)
            for c in range(NC):
                for h in range(NH):
                    i = c * NH + h
                    r, j = at(h)
                    b = 4 + i % 4
                    o = v4(pe_open(pe, f"A{i}", b)[:, :], 2, P)
                    kr = KR[r, :, j, c * P:(c + 1) * P]
                    mm(o[:, 0], Bh[r, j, c * P:(c + 1) * P], kr)
                    mm(o[:, 1], Kh[r, j, c * P:(c + 1) * P], kr).then_inc(full[b], 1)
            for c in range(NC):
                for e in range(2):
                    b = 4 + 2 * c + e
                    o = v3(pe_open(pe, f"L{c}{e}", b)[:, 0:T], P)
                    r = slice(HD * e, HD * e + HD)
                    for j in range(2):
                        last = mm(o[:, j, :], KR[r, 0, j, c * P:(c + 1) * P], Bh[r, j, c * P:(c + 1) * P])
                    last.then_inc(full[b], 1)
            o = v4(pe_open(pe, "rw_bkt", 3)[:, :], 2, P)
            for e, src in enumerate((Bh, Kh)):
                for j in range(2):
                    last = nc.tensor.transpose(o[:, e, j, :], src[:, j, 0:P], const("ident"))
            last.then_inc(full[3], 1)

            level_p(1, 0, 4)
            level_p(1, 1, 6)
            s5_in(2, 0)
            s5_in(3, 2)
            channel_major(9, "mb_q", 1, hT)
            s5_out(0, 3)
            level_x(1, 0)
            level_x(1, 1)

            level_p(2, 0, 4)
            level_p(2, 1, 6)
            channel_major(10, "mb_k", 0, hT)
            o = v3(pe_open(pe, "g_col", 2)[:, 0:8], 4)
            pe.wait_ge(S["ml_rows"], 1)
            for c in range(NC):
                last = nc.tensor.transpose(o[:, c, :], rows[1][0:NH, c * P:(c + 1) * P], const("ident", NH)[:, 0:NH])
            last.then_inc(full[2], 1)
            pe.wait_ge(S["ml_rows"], 2)
            for m in range(2):
                b = 1 + m
                o = v3(pe_open(pe, f"m_row{m}", b)[:, :], T)
                for e in range(2):
                    h = 2 * m + e
                    last = mm(o[:, e, :], const("head_sel", NH)[:, h * P:(h + 1) * P], rows[2][0:NH, :])
                last.then_inc(full[b], 1)
            level_x(2, 0)
            level_x(2, 1)

            level_p(3, 0, 4)
            level_p(3, 1, 6)
            token_major(11, "mb_v", 0, hT)
            s5_in(4, 2)
            s5_in(5, 1)
            level_x(3, 0)
            level_x(3, 1)

            ml_qk(0, 2)
            ml_qk(1, 0)
            level_p(4, 0, 4)
            level_p(4, 1, 6)
            s5_out(1, 3)
            pe.wait_ge(S["mem_ready"], 1)
            wkv(0, 1)
            level_x(4, 0)
            level_x(4, 1)

            ml_qk(2, 2)
            ml_qk(3, 0)
            level_p(5, 0, 4)
            level_p(5, 1, 6)
            wkv(1, 1)
            level_x(5, 0)
            level_x(5, 1)

            moved(pe, "qk2")
            moved(pe, "qk3")
            moved(pe, "ml_v")
            attend("num", 2, mlv, E)
            attend("den", 0, None, E)
            o = v3(pe_open(pe, "em", 1)[:, :], T)
            pe.wait_ge(S["ml_em"], 1)
            for j in range(2):
                last = mm(o[:, j, :], const("pair_sel", NH)[:, j * P:(j + 1) * P], rows[4][0:NH, :])
            last.then_inc(full[1], 1)
            level_p(6, 0, 4)
            level_p(6, 1, 6)
            s5_in(6, 2)
            s5_in(7, 0)
            wkv(2, 1)
            level_x(6, 0)
            level_x(6, 1)

            moved(pe, "rw_vt")
            solve_r(0, 4)
            mb_scores(0, 2)
            mb_scores(1, 0)
            s5_out(2, 3)
            wkv(3, 1)
            solve_u(0, 5)
            mb_scores(2, 2)
            mb_scores(3, 0)
            wkv(4, 1)
            o = pe_open(pe, "S0", 4)
            moved(pe, "U0")
            moved(pe, "rw_bkt")
            for h in range(NH):
                r, j = at(h)
                hc = slice(h * HD, (h + 1) * HD)
                mm(o[r, j * HD:(j + 1) * HD], BKt[:, 0, hc], U[:, 0, hc], True, False)
                last = mm(o[r, j * HD:(j + 1) * HD], BKt[:, 1, hc], Vt[:, 0, hc], False, True)
            last.then_inc(full[4], 1)
            moved(pe, "S0")
            solve_r(1, 5)
            wkv(5, 1)
            solve_u(1, 4)
            o = pe_open(pe, "bonus", 7)
            pe.wait_ge(S["rw_bonus"], 1)
            mm(o[:, :], const("pair_ones"), flat(bon)).then_inc(full[7], 1)
            o = v3(pe_open(pe, "rw_y", 6)[:, :], T)
            moved(pe, "U1")
            for c in range(NC):
                for h in range(NH):
                    r, j = at(h)
                    hc = slice(h * HD, (h + 1) * HD)
                    y = o[r, j, c * P:(c + 1) * P]
                    mm(y, U[:, c, hc], A[:, c * NH + h, P:T], True, False)
                    last = mm(y, Vt[:, c, hc], A[:, c * NH + h, T + P:2 * T], False, c == 0)
                    if c == 1:
                        last = mm(y, S0[:, j, h % 2, :], KR[:, 1, j, P:T], False, True)
            last.then_inc(full[6], 1)
            wkv(6, 1)
            o = pe_open(pe, "mean", 4)
            moved(pe, "rw_y")
            mm(o[:, :], const("pair_ones"), flat(Yrw)).then_inc(full[4], 1)
            for h in range(NH):
                mb_turn(h, (2, 0)[h % 2])
            s5_out(3, 3)
            o = pe_open(pe, "var", 5)
            pe.wait_ge(S["rw_ysq"], 1)
            mm(o[:, :], const("pair_ones"), flat(Ysq)).then_inc(full[5], 1)
            group_sumsq("gn_ml", 1, 6)
            wkv(7, 1)
            moved(pe, "pt3")
            moved(pe, "mb_v")
            attend("mb_o", 2, mbv, PTm)
            o = v3(pe_open(pe, "glu", 3)[:, :], T)
            pe.wait_ge(S["s5_z"], 1)
            for j in range(2):
                for k in range(2):
                    last = mm(o[:, j, :], v3(prm("w_glu"), GW)[:, k, j * P:(j + 1) * P], z5[:, k, :], k == 0, k == 1)
            last.then_inc(full[3], 1)
            group_sumsq("gn_mb", 3, 0)
            group_sumsq("gn_rw", 2, 4)
            group_sumsq("gn_s5", 0, 1)

            pe.wait_ge(S["gn_done"], 4)
            for i in range(N_WOUT):
                token_major(S_WOUT + i, f"wout{i}", (5, 6, 7, 4)[i], yT)

            def turn_stream(tag, n):
                pe.wait_ge(S["xn_ready"], n)
                for i in range(4):
                    o = v4(pe_open(pe, f"{tag}{i}", i)[:, :], 2, P)
                    for k in range(2):
                        for m in range(2):
                            last = nc.tensor.transpose(o[:, k, m, :], xtmp[:, m, (2 * i + k) * P:(2 * i + k + 1) * P],
                                                       const("ident"))
                    last.then_inc(full[i], 1)

            turn_stream("xat", 1)
            for i in range(4):
                moved(pe, f"xat{i}")
            for i in range(N_WQ):
                channel_major(S_WQ + i, f"q{i}", 4 + i, hT)
            for h in range(XH):
                o = v3(pe_open(pe, f"xs{h}", h)[:, :], NMEM)
                moved(pe, f"q{h}")
                for m in range(2):
                    for k in range(2):
                        last = mm(o[:, m, :], qx[:, 2 * h + k, m * P:(m + 1) * P], kx[:, 2 * h + k, :], k == 0, k == 1)
                last.then_inc(full[h], 1)
            for h in range(XH):
                o = v3(pe_open(pe, f"xp{h}", 4 + h)[:, :], T)
                pe.wait_ge(S["x_prob"], h + 1)
                for m in range(2):
                    for t in range(2):
                        last = nc.tensor.transpose(o[:, m, t * P:(t + 1) * P], px[:, h, t, m * P:(m + 1) * P],
                                                   const("ident"))
                last.then_inc(full[4 + h], 1)
            for h in range(XH):
                o = v3(pe_open(pe, f"xo{h}", h)[:, :], T)
                moved(pe, f"xp{h}")
                for d in range(2):
                    for m in range(2):
                        c0 = h * XD + d * P
                        last = mm(o[:, d, :], vx[:, m, c0:c0 + P], ptx[:, h, m, :], m == 0, m == 1)
                last.then_inc(full[h], 1)
            for h in range(XH):
                moved(pe, f"xo{h}")
            for i in range(N_WO):
                token_major(S_WO + i, f"wo{i}", 4 + i, ox)

            turn_stream("fft", 2)
            for i in range(4):
                moved(pe, f"fft{i}")
            for p in range(NFF // 2):
                channel_major(S_FIN + 2 * p, f"g{p}", 2 * (p % 2), hT)
                channel_major(S_FIN + 2 * p + 1, f"u{p}", 2 * (p % 2) + 1, hT)
            ys = [pe_open(pe, f"y{i}", 4 + i) for i in range(4)]
            for s in range(N_FOUT):
                w = v3(pe_slot(pe, S_FOUT + s), D)
                moved(pe, f"u{s}")
                for k in range(2):
                    for m in range(2):
                        for half in range(2):
                            kt = 2 * s + k
                            last = mm(ys[2 * m + half][:, :], act[:, kt, m * P:(m + 1) * P],
                                      w[:, k, half * 512:(half + 1) * 512], kt == 0, kt == NFF - 1)
                            if kt == NFF - 1:
                                last.then_inc(full[4 + 2 * m + half], 1)
                if s < N_FOUT - 1:
                    last.then_inc(S["slot_used"], 1)

        @block.sync
        def _(sp):
            for n in range(NSLOTS):
                i = place(n)
                turn = users[i].index(n)
                if n == S_WQ:
                    sp.wait_ge(S["gn_done"], 4)
                    sp.dma_start(xres, x_rows.rearrange("(m p) c -> p m c", p=P)).then_inc(S["xres_in"], 16)
                    sp.dma_start(gain_, gain_rows(0)).then_inc(S["gain_in"], 16)
                if n in (S_FIN, S_FIN + 8):
                    g = 1 if n == S_FIN else 2
                    sp.wait_ge(S["x_new"], 2 * g - 1)
                    sp.dma_start(gain_, gain_rows(g)).then_inc(S["gain_in"], 16)
                if turn > 0:
                    before = users[i][turn - 1]
                    if before in user_of:
                        wait_full(sp, user_of[before])
                    else:
                        sp.wait_ge(S["slot_used"], before - S_FOUT + 1)
                sp.dma_start(slot(n), weights_d[n]).then_inc(loaded[i], 16)
                if n == 5:
                    for h in range(NH):
                        moved(sp, f"rel{h}")
                    sp.dma_start(rel_scratch.ap(), E_).then_inc(S["rel_stored"], 16)
                if n == 9:
                    sp.wait_ge(S["rel_stored"], 16)
                    sp.wait_ge(S["rw_tilde"], 4)
                    skew = bass.AP(rel_scratch, P - 1, [[NH * 384 - 1, P], [384, NH], [1, T]])
                    sp.dma_start(Bz, skew).then_inc(S["rel_in"], 16)
            for m in range(2):
                sp.wait_ge(S["x_new"], 5 + m)
                sp.dma_start(out[0, m * P:(m + 1) * P, :], xres[:, m, :]).then_inc(S["out_stored"], 16)
            sp.wait_ge(S["out_stored"], 32)

        @block.gpsimd
        def _(pool):
            g = nc.gpsimd
            g.memset(rwP[:, :, 0:1], 0.0).then_inc(S["zeros_ready"], 1)
            g.memset(raw[:, :, 0:3], 0.0).then_inc(S["zeros_ready"], 1)
            g.memset(S0_, 0.0).then_inc(S["zeros_ready"], 1)
            pool.wait_ge(S["s5_co"], 1)
            wr, wi, xr, xi = (v3(pr_[:, 256 * i:256 * i + 256], 32) for i in range(4))
            g.tensor_tensor(wr, c_re, spread(co_re, 32), ALU.mult)
            g.tensor_tensor(wi, c_im, spread(co_im, 32), ALU.mult)
            g.tensor_tensor(xr, c_re, spread(co_im, 32), ALU.mult)
            g.tensor_tensor(xi, c_im, spread(co_re, 32), ALU.mult).then_inc(S["s5_c"], 1)
            pool.wait_ge(S["s5_c"], 1)
            g.tensor_tensor(c_nre, wi, wr, ALU.subtract)
            g.tensor_tensor(c_re, wr, wi, ALU.subtract)
            g.tensor_tensor(xr, xr, xi, ALU.add).then_inc(S["s5_c"], 1)
            pool.wait_ge(S["s5_c"], 2)
            g.tensor_scalar(c_im, xr, -1.0, None, ALU.mult).then_inc(S["s5_c"], 1)

            def rotate(q):
                cq, sq = cos[:, 2 * q:2 * q + 2, :], sin[:, 2 * q:2 * q + 2, :]
                moved(pool, f"bu{2 * q}")
                moved(pool, f"bu{2 * q + 1}")
                if q > 0:
                    pool.wait_ge(S["rotated_back"], q)
                g.tensor_tensor(t1, cq, bu[:, 0], ALU.mult)
                g.tensor_tensor(t2, cq, bu[:, 1], ALU.mult).then_inc(S["rotating"], 1)
                pool.wait_ge(S["rotating"], 3 * q + 1)
                g.tensor_tensor(bu[:, 1], sq, bu[:, 1], ALU.mult)
                g.tensor_tensor(bu[:, 0], sq, bu[:, 0], ALU.mult).then_inc(S["rotating"], 1)
                pool.wait_ge(S["rotating"], 3 * q + 2)
                g.tensor_tensor(t1, t1, bu[:, 1], ALU.add)
                g.tensor_tensor(t2, t2, bu[:, 0], ALU.subtract).then_inc(S["rotating"], 1)

            def rotate_back(q):
                cq, sq = cos[:, 2 * q:2 * q + 2, :], sin[:, 2 * q:2 * q + 2, :]
                pool.wait_ge(S["scanned"], q + 1)
                if q > 0:
                    pool.wait_ge(S["s5_out_used"], q)
                for x, (a_, b_) in enumerate(((cq, t1), (sq, t2), (cq, t2), (sq, t1))):
                    last = g.tensor_tensor(pr[:, x], a_, b_, ALU.mult)
                last.then_inc(S["rotated_back"], 1)

            def level_mask(n):
                for c in range(NC):
                    if n > 1:
                        wait_full(pool, f"P{n - 1}{c}")
                    g.tensor_tensor(Mj[:, c], A[:, NH * c:NH * (c + 1), 0:P],
                                    copies(const("levels")[:, n * P:(n + 1) * P], NH),
                                    ALU.mult).then_inc(S["rw_level_mask"], 1)

            pool.wait_ge(S["sincos"], 3)
            rotate(0)
            rotate_back(0)
            for c in range(NC):
                moved(pool, f"A{NH * c + 3}")
                for i in range(NH * c, NH * c + 3):
                    moved(pool, f"A{i}")
                g.tensor_tensor(XT[:, c], A[:, NH * c:NH * (c + 1), 0:P], copies(const("levels")[:, 0:P], NH),
                                ALU.mult).then_inc(S["rw_xt0"], 1)
                pool.wait_ge(S["rw_xt0"], 2 * c + 1)
                g.tensor_tensor(XT[:, c], copies(const("ident"), NH), XT[:, c], ALU.subtract).then_inc(S["rw_xt0"], 1)
            level_mask(1)
            rotate(1)
            level_mask(2)
            rotate_back(1)
            level_mask(3)
            rotate(2)
            level_mask(4)
            rotate_back(2)
            level_mask(5)
            level_mask(6)
            rotate(3)
            rotate_back(3)

        @block.scalar
        def _(act):
            a = nc.scalar
            LN_EXP = "natural_log_exp_and_others"
            act.dma_start(hT, v3(x_t, T)).then_inc(S["x_in"], 16)
            act.dma_start(cst[:, :], consts_d).then_inc(S["consts_in"], 16)
            act.dma_start(par[:, :], params_d).then_inc(S["params_in"], 16)
            act.dma_start(memT, v3(mem_t, NMEM)).then_inc(S["mem_in"], 16)
            a.preload_act_table_set(LN_EXP)

            def project(name, out_):
                o = wait_full(act, name)
                a.activation(out_, v3(o[:, :], 256), ACT.Copy).then_inc(free_of(name), 1)

            def inv_root(name, out_, width, scale, eps):
                o = wait_full(act, name)
                a.activation(out_, o[:, 0:width], ACT.Ln, bias=const(eps), scale=scale).then_inc(free_of(name), 1)
                moved(act, name)
                return a.activation(out_, out_, ACT.Exp, scale=-0.5)

            def s5_driving(i):
                if i in (2, 4, 6):
                    act.wait_ge(S["rotating"], 3 * (i // 2))
                project(f"bu{i}", bu[:, :, i % 2, :])

            def level_evac(n):
                for c in range(NC):
                    o = wait_full(act, f"P{n}{c}")
                    a.activation(Pm[:, c], v3(o[:, :], P), ACT.Copy).then_inc(free_of(f"P{n}{c}"), 1)

            def wkv_evac(i):
                project(f"wkv{i}", kx[:, 2 * i:2 * i + 2, :] if i < 4 else vx[:, :, (i - 4) * 256:(i - 3) * 256])

            act.wait_ge(S["x_in"], 16)
            a.activation(sq_x, hT, ACT.Square).then_inc(S["sq_ready"], 1)
            act.wait_ge(S["consts_in"], 16)
            inv_root("x_sumsq", rstd_x, T, 1.0 / D, "eps6").then_inc(S["rstd_x"], 1)
            act.wait_ge(S["params_in"], 16)
            a.activation(step, prm("log_step"), ACT.Exp).then_inc(S["s5_step"], 1)
            act.wait_ge(S["s5_decay"], 1)
            a.activation(mag, s8a, ACT.Exp).then_inc(S["s5_step"], 1)
            act.wait_ge(S["mem_in"], 16)
            a.activation(sq_m, memT, ACT.Square).then_inc(S["sq_m_ready"], 1)
            act.wait_ge(S["theta"], 6)
            a.activation(cos, sin, ACT.Abs).then_inc(S["sincos"], 1)
            act.wait_ge(S["sincos"], 1)
            a.activation(cos, cos, ACT.Sin, bias=const("half_pi"), scale=-TAU).then_inc(S["sincos"], 1)
            a.activation(sin, sin, ACT.Sin, scale=TAU).then_inc(S["sincos"], 1)
            a.preload_act_table_set(LN_EXP)
            act.wait_ge(S["zeros_ready"], 1)
            project("rw_wag", rwP[:, 0:2, 1:257])
            project("rw_k", rwP[:, 2:4, 1:257])
            inv_root("mem_sumsq", rstd_m, T, 1.0 / D, "eps6").then_inc(S["rstd_m"], 1)
            act.wait_ge(S["rw_mix"], 1)
            a.activation(rwE[0:HD, 0, 0, :], rwM[0:HD, 0, :], ACT.Exp, scale=-2.0)
            a.activation(rwE[:, 0, 1, :], rwM[:, 1, :], ACT.Exp, scale=-1.0).then_inc(S["rw_exp"], 1)
            project("rw_r", rwP[:, 4:6, 1:257])
            project("rw_v", rwP[:, 6:8, 1:257])
            act.wait_ge(S["rw_mix"], 4)
            act.wait_ge(S["neg_ready"], 1)
            for name, out_, b in (("rw_w", G, 0), ("rw_a", ab, 2)):
                o = v3(wait_full(act, name)[:, :], T)
                for j in range(2):
                    e = a.activation(out_[:, j, :], o[:, j, :], ACT.Exp, bias=neg_w0a0[:, b + j:b + j + 1], scale=-1.0)
                e.then_inc(free_of(name), 1)
            project("s5_u", s5u)
            project("rw_g", rwg)
            act.wait_ge(S["zeros_ready"], 2)
            project("ml_q", raw[:, 0:2, 3:259])
            inv_root("rw_kk", flat(rwE[:, 2]), 512, 1.0, "eps12").then_inc(S["rw_inv"], 1)
            project("ml_k", raw[:, 2:4, 3:259])
            act.wait_ge(S["rw_G"], 4)
            a.activation(rwE[:, 0], Gp, ACT.Exp)
            a.activation(rwE[:, 1], G, ACT.Exp)
            a.activation(carry, carry, ACT.Exp)
            act.wait_ge(S["rw_kk"], 1)
            a.activation(rwE[:, 2], Gp, ACT.Exp, scale=-1.0).then_inc(S["rw_E"], 1)
            s5_driving(0)
            s5_driving(1)
            project("rw_vt", Vt)
            act.wait_ge(S["rw_E"], 1)
            project("ml_v", mlv)
            o = wait_full(act, "ml_o")
            a.activation(mlo, v3(o[:, :], T), ACT.Exp, scale=-1.0).then_inc(free_of("ml_o"), 1)
            project("rw_bkt", BKt)

            level_evac(1)
            s5_driving(2)
            s5_driving(3)
            act.wait_ge(S["rw_tilde"], 4)
            project("mb_q", mqk[:, 0:2, :])
            act.wait_ge(S["ml_gate"], 1)
            a.activation(rows[3][0:NH, :], rows[0][0:NH, :], ACT.Abs).then_inc(S["ml_log"], 1)
            act.wait_ge(S["ml_log"], 1)
            a.activation(rows[3][0:NH, :], rows[3][0:NH, :], ACT.Exp, scale=-1.0).then_inc(S["ml_log"], 1)
            act.wait_ge(S["ml_log"], 2)
            a.activation(rows[3][0:NH, :], rows[3][0:NH, :], ACT.Ln, bias=const("ones", NH)[:, 0:1]).then_inc(S["ml_log"], 1)
            act.wait_ge(S["ml_conv"], 4)
            act.wait_ge(S["rel_stored"], 16)
            a.activation(E_[:, 0:1024], flat(cv), ACT.Exp, scale=-1.0).then_inc(S["ml_silu"], 1)
            level_evac(2)
            project("mb_k", mqk[:, 2:4, :])
            act.wait_ge(S["ml_rows"], 3)
            a.activation(rows[4][0:NH, :], rows[4][0:NH, :], ACT.Exp).then_inc(S["ml_em"], 1)
            level_evac(3)
            project("mb_v", mbv)
            moved(act, "m_row0")
            moved(act, "m_row1")
            a.activation(E_, E_, ACT.Exp).then_inc(S["ml_E"], 1)
            s5_driving(4)
            s5_driving(5)
            level_evac(4)
            wkv_evac(0)
            level_evac(5)
            wkv_evac(1)
            level_evac(6)
            s5_driving(6)
            s5_driving(7)
            wkv_evac(2)
            wkv_evac(3)
            wkv_evac(4)
            act.wait_ge(S["mb_max"], 1)
            for h in range(NH):
                for m, (lo, hi) in enumerate(((0, P), (P, P + T))):
                    e = a.activation(Sm[:, h, lo:hi], Sm[:, h, lo:hi], ACT.Exp, bias=nmax[:, 4 * m + h:4 * m + h + 1],
                                     accum_out=mb_sum[:, 4 * m + h:4 * m + h + 1])
            e.then_inc(S["mb_exp"], 1)
            wkv_evac(5)
            wkv_evac(6)
            moved(act, "mean")
            a.activation(Ysq, Yrw, ACT.Square).then_inc(S["rw_ysq"], 1)
            for h in range(NH):
                o = wait_full(act, f"pt{h}")
                a.activation(PTm[:, h, :], o[:, 0:384], ACT.Copy).then_inc(free_of(f"pt{h}"), 1)
            inv_root("var", Pm_[:, 0:512], 512, 1.0 / HD, "eps_gn").then_inc(S["rw_rstd"], 1)

            def group_square(g_, name):
                a.activation(gn_sq[g_], yT[:, 2 * g_:2 * g_ + 2, :], ACT.Square).then_inc(S[name + "_sq"], 1)

            def group_root(g_, name):
                inv_root("gn_" + name, gn_sq[g_][:, 0, :], T, 1.0 / GW, "eps6").then_inc(S[name + "_root"], 1)

            moved(act, "num")
            group_square(1, "ml")
            group_root(1, "ml")
            wkv_evac(7)
            act.wait_ge(S["s5_arg"], 1)
            a.activation(z5b, z5a, ACT.Exp, scale=-GELU).then_inc(S["s5_exp"], 1)
            moved(act, "mb_o")
            group_square(3, "mb")
            o = v3(wait_full(act, "glu")[:, :], T)
            for j in range(2):
                e = a.activation(z5b[:, j, :], o[:, j, :], ACT.Exp, bias=neg_bglu[:, j:j + 1], scale=-1.0)
            e.then_inc(free_of("glu"), 1)
            group_root(3, "mb")
            act.wait_ge(S["rw_out"], 1)
            group_square(2, "rw")
            group_root(2, "rw")
            act.wait_ge(S["s5_out"], 1)
            group_square(0, "s5")
            group_root(0, "s5")

            def post_root(n, pieces):
                for name, src, m, part in pieces:
                    o = wait_full(act, name)
                    w = src[1] - src[0]
                    e = a.activation(xtmp[:, m, part * w:(part + 1) * w], o[:, src[0]:src[1]], ACT.Square,
                                     accum_out=ssq[:, 4 * m + part:4 * m + part + 1])
                e.then_inc(S["post_ssq"], 1)
                act.wait_ge(S["post_sum"], n + 1)
                a.activation(rst, rst, ACT.Ln, bias=const("eps6"), scale=1.0 / D).then_inc(S["post_ssq"], 1)
                act.wait_ge(S["post_ssq"], 3 * n + 2)
                a.activation(rst, rst, ACT.Exp, scale=-0.5).then_inc(S["post_ssq"], 1)

            def pre_root(n):
                act.wait_ge(S["x_new"], 2 * (n + 1))
                for m in range(2):
                    e = a.activation(xtmp[:, m, :], xres[:, m, :], ACT.Square, accum_out=rst[:, m:m + 1])
                e.then_inc(S["pre_ssq"], 1)
                act.wait_ge(S["pre_ssq"], 3 * n + 1)
                a.activation(rst, rst, ACT.Ln, bias=const("eps6"), scale=1.0 / D).then_inc(S["pre_ssq"], 1)
                act.wait_ge(S["pre_ssq"], 3 * n + 2)
                a.activation(rst, rst, ACT.Exp, scale=-0.5).then_inc(S["pre_ssq"], 1)

            def turned(tag, gain):
                for i in (1, 3):
                    o = v3(wait_full(act, f"{tag}{i}")[:, :], T)
                    for k in range(2):
                        e = a.activation(hT[:, 2 * i + k, :], o[:, k, :], ACT.Copy, scale=prm(gain)[:, 2 * i + k:2 * i + k + 1])
                    e.then_inc(free_of(f"{tag}{i}"), 1)

            act.wait_ge(S["gn_done"], 4)
            post_root(0, [(f"wout{i}", (256 * m, 256 * m + 256), m, i) for i in range(4) for m in range(2)])
            pre_root(0)
            turned("xat", "pre_xa")
            for i in range(N_WQ):
                project(f"q{i}", qx[:, 2 * i:2 * i + 2, :])
            for h in range(XH):
                o = v3(wait_full(act, f"xs{h}")[:, :], NMEM)
                act.wait_ge(S["x_max"], 2 * (h + 1))
                for m in range(2):
                    e = a.activation(px[:, h, m, :], o[:, m, :], ACT.Exp, bias=xmax[:, 2 * h + m:2 * h + m + 1],
                                     scale=XD ** -0.5, accum_out=xsum[:, 2 * h + m:2 * h + m + 1])
                e.then_inc(free_of(f"xs{h}"), 1)
            for h in range(XH):
                project(f"xp{h}", ptx[:, h])
            for h in range(XH):
                project(f"xo{h}", ox[:, 2 * h:2 * h + 2, :])
            post_root(1, [(f"wo{i}", (256 * m, 256 * m + 256), m, i) for i in range(4) for m in range(2)])
            pre_root(1)
            turned("fft", "pre_ffn")
            for p in range(NFF // 2):
                o = wait_full(act, f"g{p}")
                if p > 1:
                    moved(act, f"u{p - 2}")
                a.activation(fft[:, p % 2, :], o[:, :], ACT.Exp, scale=-1.0).then_inc(S["f_exp"], 1)
            post_root(2, [(f"y{2 * m + i}", (0, 512), m, i) for m in range(2) for i in range(2)])

        @block.vector
        def _(dve):
            v = nc.vector

            def sigmoid_of_exp(x, name, n):
                v.tensor_scalar(x, x, 1.0, None, ALU.add).then_inc(S[name], 1)
                dve.wait_ge(S[name], n + 1)
                return v.reciprocal(x, x)

            dve.wait_ge(S["params_in"], 16)
            dve.wait_ge(S["consts_in"], 16)
            a, b = PARAM["w0"][0], PARAM["a0"][1]
            v.tensor_scalar(neg_w0a0, par[:, a:b], -1.0, None, ALU.mult)
            v.tensor_scalar(neg_bglu, prm("b_glu"), -1.0, None, ALU.mult)
            v.tensor_scalar(one_ka, prm("k_a"), -1.0, 1.0, ALU.mult, ALU.add).then_inc(S["neg_ready"], 1)
            for h in range(NH):
                o = wait_full(dve, f"rel{h}")
                v.tensor_copy(E[:, h, :], o[:, 0:384]).then_inc(free_of(f"rel{h}"), 1)
            dve.wait_ge(S["rstd_x"], 1)
            for k in range(KD):
                last = v.scalar_tensor_tensor(hT[:, k, :], hT[:, k, :], prm("pre_mix")[:, k:k + 1], rstd_x,
                                              ALU.mult, ALU.mult)
            last.then_inc(S["h_ready"], 1)
            dve.wait_ge(S["s5_step"], 1)
            v.tensor_tensor(s8a, prm("lam_re"), step, ALU.mult).then_inc(S["s5_decay"], 1)
            v.scalar_tensor_tensor(frac, prm("lam_im"), 1.0 / (2.0 * math.pi), step, ALU.mult, ALU.mult).then_inc(S["theta"], 1)
            dve.wait_ge(S["theta"], 1)
            v.tensor_scalar(frn, frac, ROUND, None, ALU.add).then_inc(S["theta"], 1)
            dve.wait_ge(S["theta"], 2)
            v.scalar_tensor_tensor(frac, frn, ROUND, frac, ALU.subtract, ALU.subtract).then_inc(S["theta"], 1)
            dve.wait_ge(S["theta"], 3)
            for i in range(8):
                last = v.tensor_scalar(sin[:, i, :], const("time"), frac[:, i:i + 1], None, ALU.mult)
            last.then_inc(S["theta"], 1)
            dve.wait_ge(S["theta"], 4)
            v.tensor_scalar(cos, sin, ROUND, None, ALU.add).then_inc(S["theta"], 1)
            dve.wait_ge(S["theta"], 5)
            v.scalar_tensor_tensor(sin, cos, ROUND, sin, ALU.subtract, ALU.subtract).then_inc(S["theta"], 1)

            def mix(n, name):
                moved(dve, name)
                v.tensor_tensor(rwM[:, 2 * n:2 * n + 2, :], rwP[:, 2 * n:2 * n + 2, 0:T], rwP[:, 2 * n:2 * n + 2, 1:T + 1],
                                ALU.subtract).then_inc(S["rw_diff"], 1)
                dve.wait_ge(S["rw_diff"], n + 1)
                for i in (2 * n, 2 * n + 1):
                    last = v.scalar_tensor_tensor(rwM[:, i, :], rwM[:, i, :], prm("mu")[:, i:i + 1], rwP[:, i, 1:T + 1],
                                                  ALU.mult, ALU.add)
                last.then_inc(S["rw_mix"], 1)

            dve.wait_ge(S["zeros_ready"], 1)
            mix(0, "rw_wag")
            mix(1, "rw_k")
            dve.wait_ge(S["rw_exp"], 1)
            v.tensor_scalar(rwE[0:HD, 0, 0, :], rwE[0:HD, 0, 0, :], 1.0, None, ALU.add)
            v.tensor_scalar(rwE[:, 0, 1, :], rwE[:, 0, 1, :], 1.0, None, ALU.add).then_inc(S["rw_low"], 1)
            dve.wait_ge(S["rw_low"], 1)
            v.reciprocal(rwE[0:HD, 0, 0, :], rwE[0:HD, 0, 0, :])
            v.reciprocal(rwE[:, 0, 1, :], rwE[:, 0, 1, :]).then_inc(S["rw_low"], 1)
            dve.wait_ge(S["rw_low"], 2)
            v.tensor_scalar(rwE[0:HD, 0, 0, :], rwE[0:HD, 0, 0, :], 2.0, -1.0, ALU.mult, ALU.add).then_inc(S["rw_lowrank"], 1)
            mix(2, "rw_r")
            mix(3, "rw_v")
            dve.wait_ge(S["rw_mix"], 4)
            for j in range(2):
                last = v.tensor_scalar(kk[:, j, :], rwM[:, 2 + j, :], prm("k_k")[:, j:j + 1], None, ALU.mult)
            last.then_inc(S["rw_kx"], 1)
            dve.wait_ge(S["rw_kx"], 1)
            v.tensor_tensor(rwE[:, 1], kk, kk, ALU.mult).then_inc(S["rw_kx_sq"], 1)
            moved(dve, "rw_w")
            sigmoid_of_exp(G, "rw_G0", 0).then_inc(S["rw_G0"], 1)
            dve.wait_ge(S["rw_G0"], 2)
            v.tensor_scalar(G, G, -DECAY, None, ALU.mult).then_inc(S["rw_G0"], 1)
            dve.wait_ge(S["rw_G0"], 3)
            for j in range(2):
                for c in range(NC):
                    cs = slice(c * C, (c + 1) * C)
                    last = v.tensor_tensor_scan(Gp[:, j, cs], const("ones"), G[:, j, cs], 0.0, ALU.mult, ALU.add)
            last.then_inc(S["rw_G"], 1)
            dve.wait_ge(S["rw_G"], 1)
            Gpc, Gc = v3(flat(Gp), C), v3(flat(G), C)
            v.tensor_copy(mid, Gpc[:, :, C // 2 - 1]).then_inc(S["rw_G"], 1)
            dve.wait_ge(S["rw_G"], 2)
            v.tensor_tensor(Gpc, Gpc, spread(mid, C), ALU.subtract).then_inc(S["rw_G"], 1)
            dve.wait_ge(S["rw_G"], 3)
            v.tensor_tensor(carry, Gp[:, :, C - 1], mid[:, 1:4:2], ALU.add)
            v.tensor_tensor(G, Gp, G, ALU.subtract).then_inc(S["rw_G"], 1)
            moved(dve, "rw_a")
            sigmoid_of_exp(ab, "rw_a", 0).then_inc(S["rw_a"], 1)
            dve.wait_ge(S["rw_inv"], 1)
            v.tensor_tensor(kk, kk, rwE[:, 2], ALU.mult).then_inc(S["rw_kk"], 1)
            dve.wait_ge(S["rw_a"], 2)
            k2 = rwM[:, 2:4, :]
            for j in range(2):
                last = v.tensor_scalar(Kh[:, j, :], ab[:, j, :], prm("k_a")[:, j:j + 1], one_ka[:, j:j + 1], ALU.mult, ALU.add)
            last.then_inc(S["rw_k2"], 1)
            dve.wait_ge(S["rw_kk"], 1)
            dve.wait_ge(S["rw_k2"], 1)
            v.tensor_tensor(ab, kk, ab, ALU.mult).then_inc(S["rw_k2"], 1)
            v.tensor_tensor(k2, k2, Kh, ALU.mult).then_inc(S["rw_k2"], 1)
            dve.wait_ge(S["rw_k2"], 3)
            dve.wait_ge(S["rw_E"], 1)
            v.tensor_tensor(KR[:, 0], kk, rwE[:, 1], ALU.mult).then_inc(S["rw_tilde"], 1)
            v.tensor_tensor(KR[:, 1], rwM[:, 4:6, :], rwE[:, 0], ALU.mult).then_inc(S["rw_tilde"], 1)
            v.tensor_tensor(Bh, ab, rwE[:, 2], ALU.mult).then_inc(S["rw_tilde"], 1)
            v.tensor_tensor(Kh, k2, rwE[:, 2], ALU.mult).then_inc(S["rw_tilde"], 1)
            dve.wait_ge(S["rw_tilde"], 2)
            for j in range(2):
                last = v.scalar_tensor_tensor(bon[:, j, :], bon[:, j, :], prm("r_k")[:, j:j + 1], k2[:, j, :],
                                              ALU.mult, ALU.mult)
            last.then_inc(S["rw_bonus"], 1)
            dve.wait_ge(S["sincos"], 3)
            cos1, sin1, lr, li = cos[:, :, 1], sin[:, :, 1], prm("lam_re"), prm("lam_im")
            v.tensor_tensor(s8b, mag, cos1, ALU.mult)
            v.tensor_tensor(s8c, mag, sin1, ALU.mult)
            v.tensor_tensor(den8, lr, lr, ALU.mult)
            v.tensor_tensor(s8a, li, li, ALU.mult).then_inc(S["s5_co_step"], 1)
            dve.wait_ge(S["s5_co_step"], 1)
            v.tensor_tensor(den8, den8, s8a, ALU.add)
            v.tensor_scalar(s8b, s8b, -1.0, None, ALU.add).then_inc(S["s5_co_step"], 1)
            dve.wait_ge(S["s5_co_step"], 2)
            v.reciprocal(den8, den8)
            v.tensor_tensor(co_re, s8b, lr, ALU.mult)
            v.tensor_tensor(s8a, s8c, li, ALU.mult)
            v.tensor_tensor(co_im, s8c, lr, ALU.mult)
            v.tensor_tensor(frn, s8b, li, ALU.mult).then_inc(S["s5_co_step"], 1)
            dve.wait_ge(S["s5_co_step"], 3)
            v.tensor_tensor(co_re, co_re, s8a, ALU.add)
            v.tensor_tensor(co_im, co_im, frn, ALU.subtract).then_inc(S["s5_co_step"], 1)
            dve.wait_ge(S["s5_co_step"], 4)
            v.tensor_tensor(co_re, co_re, den8, ALU.mult)
            v.tensor_tensor(co_im, co_im, den8, ALU.mult).then_inc(S["s5_co"], 1)

            def scan(q):
                dve.wait_ge(S["rotating"], 3 * (q + 1))
                for i in range(2):
                    decay = mag[:, 2 * q + i:2 * q + i + 1].to_broadcast([P, T])
                    v.tensor_tensor_scan(t1[:, i, :], decay, t1[:, i, :], 0.0, ALU.mult, ALU.add)
                    last = v.tensor_tensor_scan(t2[:, i, :], decay, t2[:, i, :], 0.0, ALU.mult, ALU.add)
                last.then_inc(S["scanned"], 1)

            mask2 = cst[:, CONST["strict"][0]:CONST["incl"][1]]
            for i in range(8):
                o = wait_full(dve, f"A{i}")
                v.tensor_tensor(v3(A[:, i, :], 256), v3(o[:, :], 256), copies(mask2, 2), ALU.mult).then_inc(free_of(f"A{i}"), 1)
            for c in range(NC):
                for e in range(2):
                    o = wait_full(dve, f"L{c}{e}")
                    v.tensor_tensor(X[:, c, e:NH:2], v3(o[:, 0:T], P), copies(const("level0_t"), 2),
                                    ALU.mult).then_inc(free_of(f"L{c}{e}"), 1)
                moved(dve, f"L{c}0")
                moved(dve, f"L{c}1")
                v.tensor_tensor(X[:, c], copies(const("ident"), NH), X[:, c], ALU.subtract).then_inc(S["rw_x0"], 1)
            scan(0)
            o = wait_full(dve, "gates")
            v.tensor_scalar(rows[0][0:NH, :], o[0:NH, T:2 * T], prm("f_bias", NH), None, ALU.add).then_inc(S["ml_gate"], 1)
            v.tensor_scalar(rows[1][0:NH, :], o[0:NH, 0:T], prm("i_bias", NH), None, ALU.add).then_inc(free_of("gates"), 1)
            moved(dve, "ml_q")
            moved(dve, "ml_k")
            dve.wait_ge(S["zeros_ready"], 2)
            cw = v3(prm("conv"), 4)
            for tap in range(4):
                if tap > 0:
                    dve.wait_ge(S["ml_conv"], tap)
                for i in range(4):
                    w, x = cw[:, i, tap:tap + 1], raw[:, i, tap:tap + T]
                    if tap == 0:
                        last = v.tensor_scalar(cv[:, i, :], x, w, None, ALU.mult)
                    else:
                        last = v.scalar_tensor_tensor(cv[:, i, :], x, w, cv[:, i, :], ALU.mult, ALU.add)
                last.then_inc(S["ml_conv"], 1)

            def level_update(n):
                for c in range(NC):
                    if n < LEVELS - 1:
                        o = wait_full(dve, f"X{n}{c}")
                        v.tensor_tensor(X[:, c], X[:, c], v3(o[:, :], P), ALU.subtract).then_inc(free_of(f"X{n}{c}"), 1)
                    o = wait_full(dve, f"T{n}{c}")
                    v.tensor_tensor(XT[:, c], XT[:, c], v3(o[:, :], P), ALU.subtract).then_inc(free_of(f"T{n}{c}"), 1)

            level_update(1)
            scan(1)
            dve.wait_ge(S["ml_log"], 3)
            lf, g_, nM, F, em = (rows[i][0:NH, :] for i in (0, 1, 2, 3, 4))
            v.scalar_tensor_tensor(lf, lf, 0.0, F, ALU.min, ALU.subtract).then_inc(S["ml_row_step"], 1)
            dve.wait_ge(S["ml_row_step"], 1)
            one = const("ones", NH)[:, 0:1].to_broadcast([NH, T])
            v.tensor_tensor_scan(F, one, lf, 0.0, ALU.mult, ALU.add).then_inc(S["ml_row_step"], 1)
            dve.wait_ge(S["ml_row_step"], 2)
            v.tensor_tensor(g_, g_, F, ALU.subtract).then_inc(S["ml_rows"], 1)
            dve.wait_ge(S["ml_rows"], 1)
            v.tensor_tensor_scan(lf, g_, g_, 0.0, ALU.max, ALU.max).then_inc(S["ml_row_step"], 1)
            dve.wait_ge(S["ml_row_step"], 3)
            v.tensor_scalar(nM, lf, -1.0, None, ALU.mult).then_inc(S["ml_rows"], 1)
            v.scalar_tensor_tensor(em, F, -1.0, lf, ALU.mult, ALU.subtract).then_inc(S["ml_rows"], 1)
            dve.wait_ge(S["ml_silu"], 1)
            ex = v3(E_[:, 0:1024], T)
            sigmoid_of_exp(ex, "ml_sig", 0).then_inc(S["ml_sig"], 1)
            dve.wait_ge(S["ml_sig"], 2)
            v.tensor_tensor(cv, cv, ex, ALU.mult).then_inc(S["ml_qk"], 1)
            o = wait_full(dve, "g_col")
            v.tensor_copy(gcol, o[:, 0:8]).then_inc(free_of("g_col"), 1)
            level_update(2)
            moved(dve, "g_col")
            dve.wait_ge(S["ml_qk"], 1)
            ca = const("causal_add")
            for m in range(2):
                o = v3(wait_full(dve, f"m_row{m}")[:, :], T)
                for e in range(2):
                    h = 2 * m + e
                    v.scalar_tensor_tensor(E[:, h, 0:T], o[:, e, :], gcol[:, h:h + 1], ca[:, 0:T], ALU.add, ALU.add)
                    last = v.scalar_tensor_tensor(E[:, h, T:T + P], o[:, e, P:T], gcol[:, 4 + h:5 + h], ca[:, T:T + P],
                                                  ALU.add, ALU.add)
                last.then_inc(free_of(f"m_row{m}"), 1)
            level_update(3)

            def ml_weight(h):
                o = wait_full(dve, f"qk{h}")
                dve.wait_ge(S["ml_E"], 1)
                v.scalar_tensor_tensor(E[:, h, :], o[:, 0:384], HD ** -0.5, E[:, h, :], ALU.mult,
                                       ALU.mult).then_inc(free_of(f"qk{h}"), 1)

            ml_weight(0)
            ml_weight(1)
            dve.wait_ge(S["rstd_m"], 1)
            for k in range(KD):
                last = v.scalar_tensor_tensor(memT[:, k, :], memT[:, k, :], prm("norm_mem")[:, k:k + 1], rstd_m,
                                              ALU.mult, ALU.mult)
            last.then_inc(S["mem_ready"], 1)
            level_update(4)
            scan(2)
            ml_weight(2)
            ml_weight(3)
            level_update(5)
            o = wait_full(dve, "den")
            den = v3(raw_cv[:, 0:512], T)
            v.tensor_scalar(den, v3(o[:, :], T), -1.0, None, ALU.mult).then_inc(S["ml_den"], 1)
            dve.wait_ge(S["ml_den"], 1)
            e = wait_full(dve, "em")
            v.tensor_tensor(den, den, v3(e[:, :], T), ALU.max).then_inc(free_of("em"), 1)
            moved(dve, "em")
            v.tensor_tensor(den, den, v3(o[:, :], T), ALU.max).then_inc(free_of("den"), 1)
            moved(dve, "den")
            moved(dve, "ml_o")
            v.scalar_tensor_tensor(den, mlo, 1.0, den, ALU.add, ALU.mult).then_inc(S["ml_den"], 1)
            dve.wait_ge(S["ml_den"], 2)
            v.reciprocal(den, den).then_inc(S["ml_den"], 1)
            dve.wait_ge(S["ml_den"], 3)
            o = wait_full(dve, "num")
            v.tensor_tensor(yT[:, 2:4, :], v3(o[:, :], T), den, ALU.mult).then_inc(free_of("num"), 1)
            level_update(6)

            def solve_rhs(c):
                o = wait_full(dve, f"R{c}")
                v.tensor_scalar(R_, o[:, 0:GW], -1.0, None, ALU.mult).then_inc(free_of(f"R{c}"), 1)

            def solution(c):
                o = wait_full(dve, f"U{c}")
                v.tensor_copy(U[:, c, :], o[:, 0:GW]).then_inc(free_of(f"U{c}"), 1)

            def mb_biased(h):
                o = wait_full(dve, f"sc{h}")
                dve.wait_ge(S["rel_in"], 16)
                v.scalar_tensor_tensor(Sm[:, h, 0:P], o[:, 0:P], HD ** -0.5, Bz[:, h, P:T], ALU.mult, ALU.add)
                v.scalar_tensor_tensor(Sm[:, h, P:P + T], o[:, P:P + T], HD ** -0.5, Bz[:, h, :], ALU.mult,
                                       ALU.add).then_inc(free_of(f"sc{h}"), 1)

            solve_rhs(0)
            mb_biased(0)
            mb_biased(1)
            solution(0)
            mb_biased(2)
            mb_biased(3)
            for h in range(NH):
                moved(dve, f"sc{h}")
            v.tensor_reduce(nmax[:, 0:4], Sm[:, :, 0:P], AX.X, ALU.max, negate=True)
            v.tensor_reduce(nmax[:, 4:8], Sm[:, :, P:P + T], AX.X, ALU.max, negate=True).then_inc(S["mb_max"], 1)
            o = wait_full(dve, "S0")
            dve.wait_ge(S["zeros_ready"], 3)
            for h in range(NH):
                r, j = at(h)
                last = v.tensor_scalar(S0[r, j, h % 2, :], o[r, j * HD:(j + 1) * HD], carry[r, j:j + 1], None, ALU.mult)
            last.then_inc(free_of("S0"), 1)
            solve_rhs(1)
            solution(1)
            scan(3)
            dve.wait_ge(S["mb_exp"], 1)
            v.reciprocal(mb_sum, mb_sum).then_inc(S["mb_inv"], 1)
            o = wait_full(dve, "rw_y")
            v.tensor_copy(Yrw, v3(o[:, :], T)).then_inc(free_of("rw_y"), 1)
            dve.wait_ge(S["mb_inv"], 1)
            v.tensor_tensor(Sm[:, :, 0:P], Sm[:, :, 0:P], spread(mb_sum[:, 0:4], P), ALU.mult)
            v.tensor_tensor(Sm[:, :, P:P + T], Sm[:, :, P:P + T], spread(mb_sum[:, 4:8], T), ALU.mult).then_inc(S["mb_prob"], 1)
            o = wait_full(dve, "mean")
            moved(dve, "rw_y")
            v.scalar_tensor_tensor(flat(Yrw), o[:, :], -1.0 / HD, flat(Yrw), ALU.mult, ALU.add).then_inc(free_of("mean"), 1)
            moved(dve, "mean")
            o = v3(wait_full(dve, "s5_y")[:, :], T)
            for j in range(2):
                last = v.scalar_tensor_tensor(z5y[:, j, :], s5u[:, j, :], prm("s5_d")[:, j:j + 1], o[:, j, :],
                                              ALU.mult, ALU.add)
            last.then_inc(free_of("s5_y"), 1)
            moved(dve, "s5_y")
            v.tensor_tensor(z5a, z5y, z5y, ALU.mult).then_inc(S["s5_step2"], 1)
            dve.wait_ge(S["s5_step2"], 1)
            v.tensor_scalar(z5a, z5a, 0.044715, 1.0, ALU.mult, ALU.add).then_inc(S["s5_step2"], 1)
            dve.wait_ge(S["s5_step2"], 2)
            v.tensor_tensor(z5a, z5a, z5y, ALU.mult).then_inc(S["s5_arg"], 1)
            dve.wait_ge(S["rw_rstd"], 1)
            v.tensor_tensor(flat(Yrw), flat(Yrw), Pm_[:, 0:512], ALU.mult).then_inc(S["rw_tail"], 1)
            o = v3(wait_full(dve, "bonus")[:, :], T)
            v.tensor_tensor(Ysq, o, rwM[:, 6:8, :], ALU.mult).then_inc(free_of("bonus"), 1)
            dve.wait_ge(S["rw_tail"], 1)
            for j in range(2):
                last = v.tensor_scalar(Yrw[:, j, :], Yrw[:, j, :], prm("ln_w")[:, j:j + 1], prm("ln_b")[:, j:j + 1],
                                       ALU.mult, ALU.add)
            last.then_inc(S["rw_tail"], 1)
            moved(dve, "bonus")
            dve.wait_ge(S["rw_tail"], 2)
            v.tensor_tensor(Yrw, Yrw, Ysq, ALU.add).then_inc(S["rw_tail"], 1)
            dve.wait_ge(S["rw_tail"], 3)
            moved(dve, "rw_g")
            v.tensor_tensor(yT[:, 4:6, :], Yrw, rwg, ALU.mult).then_inc(S["rw_out"], 1)
            dve.wait_ge(S["s5_exp"], 1)
            sigmoid_of_exp(z5b, "s5_sig", 0).then_inc(S["s5_sig"], 1)
            dve.wait_ge(S["s5_sig"], 2)
            v.tensor_tensor(z5, z5y, z5b, ALU.mult).then_inc(S["s5_z"], 1)
            o = wait_full(dve, "mb_o")
            v.tensor_copy(yT[:, 6:8, :], v3(o[:, :], T)).then_inc(free_of("mb_o"), 1)

            def group_gain(g_, name):
                dve.wait_ge(S[name + "_root"], 1)
                for j in range(2):
                    k = 2 * g_ + j
                    last = v.scalar_tensor_tensor(yT[:, k, :], yT[:, k, :], prm("mix_gain")[:, k:k + 1],
                                                  gn_sq[g_][:, 0, :], ALU.mult, ALU.mult)
                last.then_inc(S["gn_done"], 1)

            group_gain(1, "ml")
            moved(dve, "glu")
            sigmoid_of_exp(z5b, "s5_sig", 2).then_inc(S["s5_sig"], 1)
            dve.wait_ge(S["s5_sig"], 4)
            v.tensor_tensor(yT[:, 0:2, :], z5, z5b, ALU.mult).then_inc(S["s5_out"], 1)
            group_gain(3, "mb")
            group_gain(2, "rw")
            group_gain(0, "s5")

            def post_norm(n, pieces, parts):
                dve.wait_ge(S["post_ssq"], 3 * n + 1)
                v.tensor_reduce(rst, v3(ssq, 4)[:, :, 0:parts], AX.X, ALU.add).then_inc(S["post_sum"], 1)
                dve.wait_ge(S["post_ssq"], 3 * n + 3)
                dve.wait_ge(S["gain_in"], 16 * (n + 1))
                for name, src, m, part in pieces:
                    w = src[1] - src[0]
                    o = wait_full(dve, name)
                    e = v.scalar_tensor_tensor(xtmp[:, m, part * w:(part + 1) * w], o[:, src[0]:src[1]], rst[:, m:m + 1],
                                               gain_[:, part * w:(part + 1) * w], ALU.mult, ALU.mult)
                    if parts == 2 or m == 1:
                        e.then_inc(free_of(name), 1)
                moved(dve, pieces[-1][0])
                if n == 0:
                    dve.wait_ge(S["xres_in"], 16)
                for m in range(2):
                    v.tensor_tensor(xres[:, m, :], xres[:, m, :], xtmp[:, m, :], ALU.add).then_inc(S["x_new"], 1)

            def pre_norm(n):
                dve.wait_ge(S["pre_ssq"], 3 * n + 3)
                for m in range(2):
                    last = v.tensor_scalar(xtmp[:, m, :], xres[:, m, :], rst[:, m:m + 1], None, ALU.mult)
                last.then_inc(S["xn_ready"], 1)

            def turned(tag, gain):
                for i in (0, 2):
                    o = v3(wait_full(dve, f"{tag}{i}")[:, :], T)
                    for k in range(2):
                        e = v.tensor_scalar(hT[:, 2 * i + k, :], o[:, k, :], prm(gain)[:, 2 * i + k:2 * i + k + 1],
                                            None, ALU.mult)
                    e.then_inc(free_of(f"{tag}{i}"), 1)

            post_norm(0, [(f"wout{i}", (256 * m, 256 * m + 256), m, i) for i in range(4) for m in range(2)], 4)
            pre_norm(0)
            turned("xat", "pre_xa")
            for h in range(XH):
                o = v3(wait_full(dve, f"xs{h}")[:, :], NMEM)
                mx = xmax[:, 2 * h:2 * h + 2]
                v.tensor_reduce(mx, o, AX.X, ALU.max, negate=True).then_inc(S["x_max"], 1)
                dve.wait_ge(S["x_max"], 2 * h + 1)
                v.tensor_scalar(mx, mx, XD ** -0.5, None, ALU.mult).then_inc(S["x_max"], 1)
            for h in range(XH):
                moved(dve, f"xs{h}")
                sm = xsum[:, 2 * h:2 * h + 2]
                v.reciprocal(sm, sm).then_inc(S["x_inv"], 1)
                dve.wait_ge(S["x_inv"], h + 1)
                v.tensor_tensor(px[:, h], px[:, h], spread(sm, NMEM), ALU.mult).then_inc(S["x_prob"], 1)
            post_norm(1, [(f"wo{i}", (256 * m, 256 * m + 256), m, i) for i in range(4) for m in range(2)], 4)
            pre_norm(1)
            turned("fft", "pre_ffn")
            for p in range(NFF // 2):
                f = fft[:, p % 2, :]
                dve.wait_ge(S["f_exp"], p + 1)
                sigmoid_of_exp(f, "f_sig", 2 * p).then_inc(S["f_sig"], 1)
                dve.wait_ge(S["f_sig"], 2 * p + 2)
                o = wait_full(dve, f"g{p}")
                v.tensor_tensor(f, f, o[:, :], ALU.mult).then_inc(free_of(f"g{p}"), 1)
                moved(dve, f"g{p}")
                o = wait_full(dve, f"u{p}")
                v.tensor_tensor(flat(act[:, 2 * p:2 * p + 2, :]), f, o[:, :], ALU.mult).then_inc(free_of(f"u{p}"), 1)
            post_norm(2, [(f"y{2 * m + i}", (0, 512), m, i) for m in range(2) for i in range(2)], 2)


def _constants():
    import numpy as np

    c = np.zeros((P, NCONST), np.float32)

    def put(name, a):
        c[:a.shape[0], CONST[name][0]:CONST[name][0] + a.shape[1]] = a

    i = np.arange(P)
    put("ident", np.eye(P))
    put("ones", np.ones((P, P)))
    put("pair_ones", (i[:, None] // HD == i[None, :] // HD) * 1.0)
    put("strict", (i[:, None] < i[None, :]) * 1.0)
    put("incl", (i[:, None] <= i[None, :]) * 1.0)
    diag = np.where(i[:, None] <= i[None, :], 0.0, NEG)
    put("causal_add", np.concatenate([diag, np.zeros((P, P)), diag], axis=1))
    levels = []
    for n in range(LEVELS):
        b = 1 << n
        levels.append(((i[:, None] // (2 * b) == i[None, :] // (2 * b)) & (i[:, None] // b % 2 == 0)
                       & (i[None, :] // b % 2 == 1)) * 1.0)
    put("levels", np.concatenate(levels, axis=1))
    put("level0_t", levels[0].T)
    put("time", np.tile(np.arange(T), (P, 1)))
    put("head_sel", np.repeat(np.eye(NH), P, axis=1))
    put("pair_sel", np.repeat(np.eye(NH), HD, axis=1))
    rel = T - 1 - np.arange(384)
    n = np.maximum(rel, 0)
    large = 16 + (np.log(np.maximum(n, 1).astype(np.float32) / 16) / math.log(128 / 16) * 16).astype(np.int32)
    bucket = np.where(n < 16, n, np.minimum(large, 31))
    hot = np.zeros((33, 384))
    hot[bucket, np.arange(384)] = rel >= 0
    hot[32] = np.where(rel < 0, NEG, 0.0)
    put("onehot", hot)
    for name, value in (("eps6", 1e-6), ("eps12", 1e-12), ("eps_gn", 64e-5), ("half_pi", math.pi / 2)):
        put(name, np.full((P, 1), value))
    return c


def _parameters(a):
    import numpy as np

    p = np.zeros((P, NPARAM), np.float32)

    def put(name, block, at=0):
        lo = PARAM[name][0] + at
        p[:block.shape[0], lo:lo + block.shape[1]] = block

    def channels(v):
        return v.reshape(-1, P).T

    mu = a["rw_mu"][0]
    put("mu", channels(np.concatenate([mu[768:1024], mu[256:512], mu[0:256], mu[512:768]])))
    for name, src in (("w0", "rw_w0"), ("a0", "rw_a0"), ("k_k", "rw_k_k"), ("k_a", "rw_k_a"), ("r_k", "rw_r_k"),
                      ("ln_w", "rw_ln_w"), ("ln_b", "rw_ln_b"), ("s5_d", "s5_d"), ("b_glu", "s5_b_glu"),
                      ("mix_gain", "mix_out_gain"), ("pre_mix", "norm_pre_mix"), ("pre_xa", "norm_pre_xa"),
                      ("pre_ffn", "norm_pre_ffn"), ("norm_mem", "norm_mem"), ("lam_re", "s5_lam_re"),
                      ("lam_im", "s5_lam_im")):
        put(name, channels(a[src][0]))
    put("conv", a["ml_conv"][0].reshape(4, 4, P).transpose(2, 1, 0).reshape(P, 16))
    put("log_step", channels(np.repeat(a["s5_log_step"][0], 64)))
    put("i_bias", a["ml_i_bias"][0].reshape(NH, 1))
    put("f_bias", a["ml_f_bias"][0].reshape(NH, 1))
    put("rel", a["rel_bias"])
    p[32, PARAM["rel"][0]:PARAM["rel"][1]] = 1.0
    gate = a["w_in"][0][:, 1280:1288]
    put("w_gate", gate.reshape(KD, P, 8).transpose(1, 0, 2).reshape(P, KD * 8))
    put("w2a2", np.concatenate([a["rw_w2"][0], a["rw_a2"][0]], axis=0))
    put("g2", a["rw_g2"][0])
    put("w_glu", a["s5_w_glu"][0].reshape(2, P, GW).transpose(1, 0, 2).reshape(P, 2 * GW))
    for name, src in (("b_re", "s5_b_re"), ("b_im", "s5_b_im")):
        b = np.zeros((4, 2, 16, 2, 2, 64), np.float32)
        w = a[src][0].reshape(2, 4, 2, 64, 16)
        for g in range(2):
            b[:, g, :, :, g, :] = w[:, :, g].transpose(1, 3, 0, 2)
        put(name, b.reshape(P, 256))
    for name, src in (("c_re", "s5_c_re"), ("c_im", "s5_c_im")):
        c = np.zeros((2, 64, 8, 2, 16), np.float32)
        w = a[src][0].reshape(8, 2, 16, 64)
        for g in range(2):
            c[g, :, :, g, :] = w[:, g].transpose(2, 0, 1)
        put(name, c.reshape(P, 256))
    return p


def _weight_slots(a):
    import numpy as np

    def columns_of(w):
        n = w.shape[1] // 256
        return w.reshape(KD, P, n, 256).transpose(2, 1, 0, 3).reshape(n, P, SLOT)

    w = a["w_in"][0]
    ml, rw, mb = GW, GW + 4 * GW + 8, GW + 4 * GW + 8 + 1024
    first = {"rw_wag": rw + 768, "rw_k": rw + 256, "rw_r": rw, "rw_v": rw + 512, "s5_u": 0, "ml_q": ml,
             "ml_k": ml + 256, "ml_v": ml + 512, "ml_o": ml + 768, "mb_q": mb, "mb_k": mb + 256, "mb_v": mb + 512}
    parts = [columns_of(w[:, first[n]:first[n] + 256]) for n in W_IN_ORDER]
    parts += [columns_of(a[n][0]) for n in ("xa_wkv", "w_out", "xa_wq", "xa_wo")]
    gu = columns_of(a["ffn_w_in"][0])
    half = NFF // 2
    parts.append(np.stack([gu[:half], gu[half:]], axis=1).reshape(2 * half, P, SLOT))
    parts.append(a["ffn_w_out"][0].reshape(half, 2, P, D).transpose(0, 2, 1, 3).reshape(half, P, SLOT))
    return np.concatenate(parts, axis=0)


def kernel(**inputs):
    import numpy as np
    import concourse.bacc as bacc
    from concourse.bass_utils import run_bass_kernel_spmd

    a = {name: np.asarray(value) for name, value in inputs.items()}
    arrays = {
        "x_t": a["x"][0].T.reshape(KD, P, T).transpose(1, 0, 2).reshape(P, KD * T),
        "x_rows": a["x"][0],
        "mem_t": a["mem"][0].T.reshape(KD, P, NMEM).transpose(1, 0, 2).reshape(P, KD * NMEM),
        "consts": _constants(),
        "params": _parameters(a),
        "weights": _weight_slots(a),
        "gains": np.concatenate([a["norm_post_mix"], a["norm_post_xa"], a["norm_post_ffn"]], axis=0),
    }
    arrays = {name: np.ascontiguousarray(v) for name, v in arrays.items()}
    nc = bacc.Bacc("TRN2", target_bir_lowering=False, num_devices=1)
    aps = {name: nc.dram_tensor(name, v.shape, F32, kind="ExternalInput").ap() for name, v in arrays.items()}
    rel_scratch = nc.dram_tensor("rel_scratch", (P, NH * 384), F32)
    out = nc.dram_tensor("out", (1, T, D), F32, kind="ExternalOutput").ap()
    trunk_kernel(nc, aps["x_t"], aps["x_rows"], aps["mem_t"], aps["consts"], aps["params"], aps["weights"],
                 aps["gains"], rel_scratch, out)
    r = run_bass_kernel_spmd(nc, [arrays], core_ids=[0])
    return r.results[0]["out"]
```

```python
import concourse.bass as bass
from concourse import mybir
from contextlib import ExitStack
import math

F32 = mybir.dt.float32
F32R = mybir.dt.float32r
ALU = mybir.AluOpType
ACT = mybir.ActivationFunctionType
AX = mybir.AxisListType

P = 128
D = 1024
T = 256
NMEM = 256
KD = D // P
GW = 256
HD = 64
NH = GW // HD
C = 128
NC = T // C
DFF = 2816
NFF = DFF // P
XH, XD = 4, 256
EPS = 1e-6
NEG = -1e30
DECAY = math.exp(-0.5)
TAU = 6.2831850
ROUND = 12582912.0
GELU = 2.0 * math.sqrt(2.0 / math.pi)
LEVELS = 7


def columns(sizes):
    at, out = 0, {}
    for name, n in sizes:
        out[name] = (at, at + n)
        at += n
    return out, at


CONST, NCONST = columns([
    ("ident", P), ("ones", P), ("pair_ones", P), ("strict", P), ("incl", P), ("causal_add", 384),
    ("levels", LEVELS * P), ("level0_t", P), ("time", T), ("head_sel", NH * P), ("pair_sel", 2 * P),
    ("onehot", 384), ("eps6", 1), ("eps12", 1), ("eps_gn", 1), ("half_pi", 1),
])
PARAM, NPARAM = columns([
    ("mu", 8), ("w0", 2), ("a0", 2), ("k_k", 2), ("k_a", 2), ("r_k", 2), ("ln_w", 2), ("ln_b", 2),
    ("s5_d", 2), ("b_glu", 2), ("mix_gain", 8), ("conv", 16), ("pre_mix", 8), ("pre_xa", 8),
    ("pre_ffn", 8), ("norm_mem", 8), ("lam_re", 8), ("lam_im", 8), ("log_step", 8), ("i_bias", 1),
    ("f_bias", 1), ("rel", 4), ("w_gate", KD * 8), ("w2a2", GW), ("g2", GW), ("w_glu", 2 * GW),
    ("b_re", GW), ("b_im", GW), ("c_re", GW), ("c_im", GW),
])

W_IN_ORDER = ["rw_wag", "rw_k", "rw_r", "rw_v", "s5_u", "ml_q", "ml_k", "ml_v", "ml_o", "mb_q", "mb_k", "mb_v"]
SLOT = 2048
N_WIN, N_WKV, N_WOUT, N_WQ, N_WO = 12, 8, 4, 4, 4
N_FIN, N_FOUT = 2 * NFF // 2, NFF // 2
S_WKV = N_WIN
S_WOUT = S_WKV + N_WKV
S_WQ = S_WOUT + N_WOUT
S_WO = S_WQ + N_WQ
S_FIN = S_WO + N_WO
S_FOUT = S_FIN + N_FIN
NSLOTS = S_FOUT + N_FOUT
RING = 3
S_SPLIT = S_WOUT
HALF = SLOT // 2
NHALF = 2 * (NSLOTS - S_SPLIT)
HALF_BUFS = 4
Y_ORDER = [2, 3, 6, 7, 4, 5, 0, 1]


def trunk_kernel(nc, x_t, x_rows, mem_t, consts_d, params_d, weights_d, gains_d, rel_scratch, out):
    ctx = ExitStack()
    with ctx:
        def sb(name, n):
            return ctx.enter_context(nc.sbuf_tensor(name, [P, n], F32))

        def v3(ap, n):
            return ap.rearrange("p (a b) -> p a b", b=n)

        def v4(ap, m, n):
            return ap.rearrange("p (a b c) -> p a b c", b=m, c=n)

        def copies(ap, n):
            return ap.unsqueeze(1).to_broadcast([ap.shape[0], n, ap.shape[1]])

        def spread(ap, n):
            return ap.unsqueeze(2).to_broadcast([ap.shape[0], ap.shape[1], n])

        cst = sb("cst", NCONST)
        par = sb("par", NPARAM)
        kx = v3(sb("kx", KD * NMEM)[:, :], NMEM)
        vx = v3(sb("vx", 2 * D)[:, :], D)
        ring = sb("ring", RING * SLOT)
        small = sb("small", 160)
        ARENA = 33000
        with ExitStack() as early:
            hT, memT, arena = (early.enter_context(nc.sbuf_tensor(name, [P, n], F32))
                               for name, n in (("hT", KD * T), ("memT", KD * NMEM), ("arena", ARENA)))
            hT = v3(hT[:, :], T)
            memT = v3(memT[:, :], NMEM)
        bank = [ctx.enter_context(nc.psum_tensor(f"bank{i}", [P, 512], F32)) for i in range(8)]

        def const(name, rows=P):
            a, b = CONST[name]
            return cst[0:rows, a:b]

        def prm(name, rows=P):
            a, b = PARAM[name]
            return par[0:rows, a:b]

        def flat(ap):
            return ap.rearrange("p a b -> p (a b)")

        def gain_rows(n):
            return bass.AP(gains_d.tensor, n * D, [[0, P], [1, D]])

        def carve(at, sizes):
            views = []
            for n in sizes:
                views.append(arena[:, at:at + n])
                at += n
            assert at <= ARENA, at
            return views, at

        (yT_, rwP_, rwM_, rwE_, KR_, Bh_, Kh_), at = carve(0, [8 * T, 8 * 257, 8 * T, 3 * 512, 1024, 512, 512])
        yT = v3(yT_, T)
        rwP = v3(rwP_, 257)
        rwM = v3(rwM_, T)
        kk, ab, G, Gp = (v3(rwP_[:, 512 * i:512 * i + 512], T) for i in range(4))
        rwE = rwE_.rearrange("p (e j t) -> p e j t", e=3, t=T)
        KR = KR_.rearrange("p (e j t) -> p e j t", e=2, t=T)
        Bh, Kh = v3(Bh_, T), v3(Kh_, T)
        rwg, bon = rwM[:, 0:2, :], rwM[:, 4:6, :]
        A_AT = at
        (A_, X_, XT_, Pm_, Mj_), at = carve(at, [4096, 1024, 1024, 1024, 1024])
        A = v3(A_, 512)
        X, XT, Pm, Mj = (a.rearrange("p (c h t) -> p c h t", c=NC, t=P) for a in (X_, XT_, Pm_, Mj_))
        sq_x, sq_m = v3(A_[:, 0:2048], T), v3(A_[:, 2048:4096], T)
        (Vt_, BKt_, R_, U_, S0_), at = carve(at, [512, 512, 256, 512, 256])
        Vt, BKt, U, S0 = v3(Vt_, 256), v3(BKt_, 256), v3(U_, 256), v4(S0_, 2, HD)
        (cos_, sin_, bu_, t1_, t2_, pr_, s5u_), at = carve(at, [2048, 2048, 1024, 512, 512, 2048, 512])
        cos, sin, t1, t2, s5u = (v3(a, T) for a in (cos_, sin_, t1_, t2_, s5u_))
        bu, pr = v4(bu_, 2, T), v4(pr_, 2, T)
        (raw_cv, E_, c2n_), at = carve(at, [4 * 259 + 1024, 4 * 384, 256])
        raw, cv = v3(raw_cv[:, 0:1036], 259), v3(raw_cv[:, 1036:2060], T)
        mlo, mlv = v3(G.rearrange("p a b -> p (a b)"), T), v3(Gp.rearrange("p a b -> p (a b)"), 256)
        E = v3(E_, 384)
        rows = [yT[:, i, :] for i in (4, 5, 6, 7, 1)]
        c_re, c_im, c_nre = v3(prm("c_re"), 32), v3(prm("c_im"), 32), v3(c2n_, 32)
        mqk, mbv = v3(rwE_[:, 0:1024], T), v3(rwE_[:, 1024:1536], 256)
        Bz = v3(rwP_[:, 0:1024], T)
        Sm, PTm = E, v3(raw_cv[:, 0:1536], 384)

        Yrw, Ysq = v3(Mj_[:, 0:512], T), v3(Mj_[:, 512:1024], T)
        z5y, z5a, z5, z5b = v3(bu_[:, 0:512], T), v3(bu_[:, 512:1024], T), t1, t2
        gn_sq = [v3(pr_[:, 0:512], T), Bh, rwM[:, 2:4, :], Kh]
        rstd_x, rstd_m = t1_[:, 0:T], yT_[:, 0:T]

        def pair(stack, name, n, width):
            return [v3(stack.enter_context(nc.sbuf_tensor(name + part, [P, n], F32R))[:, :], width)
                    for part in ("_high", "_rest")]

        def own(stack, name, n):
            return stack.enter_context(nc.sbuf_tensor(name, [P, n], F32))[:, :]

        h_split = pair(ctx, "h", KD * T, T)
        xtmp = v3(own(ctx, "xtmp", 2 * D), D)
        xres = v3(own(ctx, "xres", 2 * D), D)
        gain_ = own(ctx, "gain", D)
        px = own(ctx, "px", XH * 2 * NMEM).rearrange("p (h t m) -> p h t m", t=2, m=NMEM)
        qx = v3(own(ctx, "qx", KD * T), T)
        own(ctx, "gap0", A_AT - 7 * D - 2 * D)
        w_split = [pair(ctx, f"w{i}", HALF, 256) for i in range(2)]
        with ExitStack() as stage:
            y_high = v3(stage.enter_context(nc.sbuf_tensor("y_high", [P, 8 * T], F32R))[:, :], T)
            ptx = own(stage, "ptx", XH * 2 * T).rearrange("p (h m t) -> p h m t", m=2, t=T)
            y_rest = v3(stage.enter_context(nc.sbuf_tensor("y_rest", [P, 8 * T], F32R))[:, :], T)
            y_split = [y_high, y_rest]
        act_high = v3(ctx.enter_context(nc.sbuf_tensor("act_high", [P, NFF * T], F32R))[:, :], T)
        own(ctx, "gap1", 3 * 8 * T - NFF * T)
        w_split += [pair(ctx, f"w{i}", HALF, 256) for i in range(2, HALF_BUFS)]
        with ExitStack() as stage:
            ox_split = pair(stage, "ox", KD * T, T)
        act_rest = v3(ctx.enter_context(nc.sbuf_tensor("act_rest", [P, NFF * T], F32R))[:, :], T)
        act_split = [act_high, act_rest]
        fft = v3(own(ctx, "fft", 1024), 512)

        taken = [0]

        def cols(n):
            taken[0] += n
            assert taken[0] <= 160
            return small[:, taken[0] - n:taken[0]]

        neg_w0a0, neg_bglu, one_ka = cols(4), cols(2), cols(2)
        mid, carry = cols(4), cols(2)
        step, mag, frac, frn, co_re, co_im, den8, s8a, s8b, s8c = (cols(8) for _ in range(10))
        gcol = cols(8)
        nmax, mb_sum = cols(8), cols(8)
        ssq, rst = cols(8), cols(2)
        xmax, xsum = cols(8), cols(8)

        S = {name: ctx.enter_context(nc.semaphore(name)) for name in """
            rotated_back s5_out_used rw_level_mask rw_x0 rw_xt0 ml_qk mb_prob consts_in params_in
            sq_ready h_ready sq_m_ready rw_lowrank rw_kx_sq rw_mix rw_tilde ml_rows mem_ready ml_em
            rw_bonus rw_ysq s5_z gn_done xn_ready x_prob slot_used xres_in gain_in  rel_stored
            rel_in x_new out_stored zeros_ready s5_co s5_c rotating scanned sincos x_in mem_in
            rstd_x s5_step s5_decay theta rstd_m rw_exp neg_ready rw_inv rw_G rw_kk rw_E ml_gate
            ml_log ml_conv ml_silu ml_E mb_max mb_exp rw_rstd s5_arg s5_exp rw_out s5_out post_ssq
            post_sum pre_ssq x_max f_exp rw_diff rw_low rw_kx rw_G0 rw_a rw_k2 s5_co_step
            ml_row_step ml_sig ml_den mb_inv s5_step2 rw_tail s5_sig x_inv f_sig s5_sq s5_root ml_sq
            ml_root rw_sq rw_root mb_sq mb_root
            w_high w_rest_even w_rest_odd w_used high_ready act_rest y_rest
            """.split()}
        loaded = [ctx.enter_context(nc.semaphore(f"slot_loaded{i}")) for i in range(RING)]
        full = [ctx.enter_context(nc.semaphore(f"bank_full{i}")) for i in range(8)]
        free = [ctx.enter_context(nc.semaphore(f"bank_free{i}")) for i in range(8)]

        uses, count = {}, [0] * 8

        def pe_open(pe, name, b):
            uses[name] = (b, count[b])
            if count[b] > 0:
                pe.wait_ge(free[b], count[b])
            count[b] += 1
            return bank[b]

        def wait_full(eng, name):
            b, n = uses[name]
            eng.wait_ge(full[b], n + 1)
            return bank[b]

        def moved(eng, name):
            b, n = uses[name]
            eng.wait_ge(free[b], n + 1)

        def free_of(name):
            return free[uses[name][0]]

        def slot(n):
            return ring[:, n % RING * SLOT:(n % RING + 1) * SLOT]

        user_of = {}

        def wait_slot(eng, n):
            eng.wait_ge(loaded[n % RING], 16 * (n // RING + 1))
            return slot(n)

        half_user = {}

        def raw_half(i):
            at = i % 2 * HALF
            return v3(slot(S_SPLIT + i // 2)[:, at:at + HALF], 256)

        def wait_rest(eng, i):
            eng.wait_ge(S[("w_rest_even", "w_rest_odd")[i % 2]], i // 2 + 1)

        HIGHS = {"y": 0, "xat": 4, "ox": 8, "fft": 12, "act": 16}

        def high_part(act, i):
            if i % 2 == 0:
                wait_slot(act, S_SPLIT + i // 2)
            if i >= HALF_BUFS:
                user = half_user[i - HALF_BUFS]
                if isinstance(user, str):
                    wait_full(act, user)
                else:
                    act.wait_ge(S["w_used"], user)
            nc.scalar.activation(w_split[i % HALF_BUFS][0], raw_half(i), ACT.Copy).then_inc(S["w_high"], 1)

        def rest(eng, e, i):
            eng.wait_ge(S["w_high"], i + 1)
            high, rest_ = w_split[i % HALF_BUFS]
            e.tensor_tensor(rest_, raw_half(i), high.bitcast(F32),
                            ALU.subtract).then_inc(S[("w_rest_even", "w_rest_odd")[i % 2]], 1)

        def at(h):
            return slice(HD * (h % 2), HD * (h % 2) + HD), h // 2

        block = ctx.enter_context(nc.Block())

        @block.tensor
        def _(pe):
            def mm(out_, lhsT, rhs, start=True, stop=True):
                return nc.tensor.matmul(out_, lhsT, rhs, start=start, stop=stop, skip_group_check=True)

            def channel_major(n, name, b, act):
                o, w = v3(pe_open(pe, name, b)[:, :], T), v3(wait_slot(pe, n), 256)
                for c in range(2):
                    for k in range(KD):
                        last = mm(o[:, c, :], w[:, k, c * P:(c + 1) * P], act[:, k, :], k == 0, k == KD - 1)
                last.then_inc(full[b], 1)
                user_of[n] = name

            def token_major(n, name, b, act):
                o, w = v3(pe_open(pe, name, b)[:, :], 256), v3(wait_slot(pe, n), 256)
                for m in range(2):
                    for k in range(KD):
                        last = mm(o[:, m, :], act[:, k, m * P:(m + 1) * P], w[:, k, :], k == 0, k == KD - 1)
                last.then_inc(full[b], 1)
                user_of[n] = name

            def mm3(out_, lhs, rhs, start, stop):
                mm(out_, lhs[0], rhs[0], start, False)
                mm(out_, lhs[0], rhs[1], False, False)
                return mm(out_, lhs[1], rhs[0], False, stop)

            def used(last, i, name=None):
                if name:
                    last.then_inc(full[uses[name][0]], 1)
                    half_user[i] = name
                else:
                    last.then_inc(S["w_used"], 1)
                    half_user[i] = sum(not isinstance(u, str) for u in half_user.values()) + 1

            def split_channel_major(n, name, b, act, arrive=None):
                o = v3(pe_open(pe, name, b)[:, :], T)
                for j in range(2):
                    i = 2 * (n - S_SPLIT) + j
                    wait_rest(pe, i)
                    if arrive:
                        arrive(j)
                    w = w_split[i % HALF_BUFS]
                    for c in range(2):
                        for k in range(4):
                            last = mm3(o[:, c, :], [x[:, k, c * P:(c + 1) * P] for x in w],
                                       [x[:, 4 * j + k, :] for x in act], c + j + k == 0, 4 * j + k == KD - 1)
                    used(last, i, name if j else None)

            def split_token_major(n, q, name, b, act, order):
                o = v3((pe_open(pe, name, b) if q < 4 else bank[b])[:, :], 256)
                i = 2 * (n - S_SPLIT) + q
                wait_rest(pe, i)
                for m in range(2):
                    for k in range(4):
                        kt = 4 * (q // 4) + k
                        last = mm3(o[:, m, :], [x[:, order[kt], m * P:(m + 1) * P] for x in act],
                                   [x[:, k, :] for x in w_split[i % HALF_BUFS]], m + kt == 0, kt == KD - 1)
                used(last, i, name if q >= 4 else None)

            def sumsq(name, b, sq):
                o = pe_open(pe, name, b)
                for k in range(KD):
                    last = mm(o[:, 0:T], const("ones"), sq[:, k, :], k == 0, k == KD - 1)
                last.then_inc(full[b], 1)

            def wkv(i, b):
                if i < 4:
                    channel_major(S_WKV + i, f"wkv{i}", b, memT)
                else:
                    token_major(S_WKV + i, f"wkv{i}", b, memT)

            def s5_in(i, b):
                o = pe_open(pe, f"bu{i}", b)
                r, j = slice(32 * (i % 4), 32 * (i % 4) + 32), i // 4
                for e, w in enumerate(("b_re", "b_im")):
                    last = mm(o[:, e * T:(e + 1) * T], v3(prm(w), P)[r, j, :], s5u[r, j, :])
                last.then_inc(full[b], 1)

            def s5_out(q, b):
                o = pe_open(pe, "s5_y", b) if q == 0 else bank[b]
                pe.wait_ge(S["rotated_back"], q + 1)
                for i in (2 * q, 2 * q + 1):
                    y = o[32 * (i % 4):32 * (i % 4) + 32, (i // 4) * T:(i // 4 + 1) * T]
                    for n, (w, x) in enumerate(((c_re, 0), (c_nre, 1), (c_im, 2), (c_im, 3))):
                        last = mm(y, w[:, i, :], pr[:, x, i % 2, :], n == 0, n == 3)
                last.then_inc(full[b] if q == 3 else S["s5_out_used"], 1)

            def level_p(n, c, b):
                o = v3(pe_open(pe, f"P{n}{c}", b)[:, :], P)
                pe.wait_ge(S["rw_level_mask"], 2 * (n - 1) + c + 1)
                if n == 1:
                    pe.wait_ge(S["rw_x0"], c + 1)
                else:
                    moved(pe, f"X{n - 1}{c}")
                for h in range(NH):
                    last = mm(o[:, h, :], Mj[:, c, h, :], X[:, c, h, :])
                last.then_inc(full[b], 1)

            def level_x(n, c):
                moved(pe, f"P{n}{c}")
                if n == 1:
                    pe.wait_ge(S["rw_xt0"], 2 * c + 2)
                else:
                    moved(pe, f"T{n - 1}{c}")
                if n < LEVELS - 1:
                    b = 5 + 2 * c
                    o = v3(pe_open(pe, f"X{n}{c}", b)[:, :], P)
                    for h in range(NH):
                        last = mm(o[:, h, :], XT[:, c, h, :], Pm[:, c, h, :])
                    last.then_inc(full[b], 1)
                b = 4 + 2 * c
                o = v3(pe_open(pe, f"T{n}{c}", b)[:, :], P)
                for h in range(NH):
                    last = mm(o[:, h, :], Pm[:, c, h, :], XT[:, c, h, :])
                last.then_inc(full[b], 1)

            def ml_qk(h, b):
                o = pe_open(pe, f"qk{h}", b)
                pe.wait_ge(S["ml_qk"], 1)
                r, j = at(h)
                mm(o[:, 0:T], cv[r, 2 + j, 0:P], cv[r, j, :])
                mm(o[:, T:T + P], cv[r, 2 + j, P:T], cv[r, j, P:T]).then_inc(full[b], 1)

            def attend(name, b, values, probs):
                o = pe_open(pe, name, b)
                for h in range(NH):
                    r, j = at(h)
                    v0 = values[:, 0, h * HD:(h + 1) * HD] if values is not None else const("ones")[:, 0:HD]
                    v1 = values[:, 1, h * HD:(h + 1) * HD] if values is not None else const("ones")[:, 0:HD]
                    mm(o[r, j * T:(j + 1) * T], v0, probs[:, h, 0:T], True, False)
                    last = mm(o[r, j * T + P:(j + 1) * T], v1, probs[:, h, T:T + P], False, True)
                last.then_inc(full[b], 1)

            def mb_scores(h, b):
                o = pe_open(pe, f"sc{h}", b)
                moved(pe, "mb_k")
                r, j = at(h)
                mm(o[:, 0:P], mqk[r, j, 0:P], mqk[r, 2 + j, 0:P])
                mm(o[:, P:P + T], mqk[r, j, P:T], mqk[r, 2 + j, :]).then_inc(full[b], 1)

            def mb_turn(h, b):
                o = pe_open(pe, f"pt{h}", b)
                pe.wait_ge(S["mb_prob"], 1)
                for i in range(3):
                    last = nc.tensor.transpose(o[:, i * P:(i + 1) * P], Sm[:, h, i * P:(i + 1) * P], const("ident"))
                last.then_inc(full[b], 1)

            def group_sumsq(name, g, b):
                o = pe_open(pe, name, b)
                pe.wait_ge(S[("s5", "ml", "rw", "mb")[g] + "_sq"], 1)
                for j in range(2):
                    last = mm(o[:, 0:T], const("ones"), gn_sq[g][:, j, :], j == 0, j == 1)
                last.then_inc(full[b], 1)

            def solve_r(c, b):
                o = v3(pe_open(pe, f"R{c}", b)[:, 0:GW], HD)
                for h in range(NH):
                    r, j = at(h)
                    last = mm(o[:, h, :], A[:, c * NH + h, T:T + P], Vt[:, c, h * HD:(h + 1) * HD], True, c == 0)
                    if c == 1:
                        last = mm(o[:, h, :], KR[:, 0, j, P:T], S0[:, j, h % 2, :], False, True)
                last.then_inc(full[b], 1)

            def solve_u(c, b):
                o = v3(pe_open(pe, f"U{c}", b)[:, 0:GW], HD)
                moved(pe, f"T{LEVELS - 1}{c}")
                moved(pe, f"R{c}")
                for h in range(NH):
                    last = mm(o[:, h, :], XT[:, c, h, :], v3(R_, HD)[:, h, :])
                last.then_inc(full[b], 1)

            pe.wait_ge(S["consts_in"], 16)
            pe.wait_ge(S["params_in"], 16)
            for h in range(NH):
                o = pe_open(pe, f"rel{h}", 4 + h)
                mm(o[:, 0:384], prm("rel", 33)[:, h:h + 1].to_broadcast([33, P]), const("onehot", 33)).then_inc(full[4 + h], 1)
            pe.wait_ge(S["sq_ready"], 1)
            sumsq("x_sumsq", 0, sq_x)
            pe.wait_ge(S["h_ready"], 1)
            channel_major(0, "rw_wag", 1, hT)
            channel_major(1, "rw_k", 0, hT)
            pe.wait_ge(S["sq_m_ready"], 1)
            sumsq("mem_sumsq", 3, sq_m)
            channel_major(2, "rw_r", 1, hT)
            channel_major(3, "rw_v", 0, hT)
            o = v3(pe_open(pe, "rw_w", 2)[:, :], T)
            pe.wait_ge(S["rw_lowrank"], 1)
            for j in range(2):
                last = mm(o[:, j, :], prm("w2a2")[0:HD, j * P:(j + 1) * P], rwE[0:HD, 0, 0, :])
            last.then_inc(full[2], 1)
            o = v3(pe_open(pe, "rw_a", 3)[:, :], T)
            for j in range(2):
                last = mm(o[:, j, :], prm("w2a2")[HD:P, j * P:(j + 1) * P], rwM[HD:P, 0, :])
            last.then_inc(full[3], 1)
            channel_major(4, "s5_u", 1, hT)
            o = v3(pe_open(pe, "rw_g", 2)[:, :], T)
            for j in range(2):
                last = mm(o[:, j, :], prm("g2")[:, j * P:(j + 1) * P], rwE[:, 0, 1, :])
            last.then_inc(full[2], 1)
            channel_major(5, "ml_q", 0, hT)
            o = pe_open(pe, "rw_kk", 3)
            pe.wait_ge(S["rw_kx_sq"], 1)
            mm(o[:, :], const("pair_ones"), flat(rwE[:, 1])).then_inc(full[3], 1)
            channel_major(6, "ml_k", 1, hT)
            o = pe_open(pe, "gates", 2)
            for e in range(2):
                for k in range(KD):
                    last = mm(o[0:NH, e * T:(e + 1) * T], v3(prm("w_gate"), 8)[:, k, 4 * e:4 * e + 4],
                              hT[:, k, :], k == 0, k == KD - 1)
            last.then_inc(full[2], 1)
            moved(pe, "s5_u")
            s5_in(0, 0)
            s5_in(1, 1)
            o = v4(pe_open(pe, "rw_vt", 3)[:, :], 2, P)
            pe.wait_ge(S["rw_mix"], 4)
            for c in range(NC):
                for j in range(2):
                    last = nc.tensor.transpose(o[:, c, j, :], rwM[:, 6 + j, c * P:(c + 1) * P], const("ident"))
            last.then_inc(full[3], 1)
            token_major(7, "ml_v", 0, hT)
            channel_major(8, "ml_o", 1, hT)
            pe.wait_ge(S["rw_tilde"], 4)
            for c in range(NC):
                for h in range(NH):
                    i = c * NH + h
                    r, j = at(h)
                    b = 4 + i % 4
                    o = v4(pe_open(pe, f"A{i}", b)[:, :], 2, P)
                    kr = KR[r, :, j, c * P:(c + 1) * P]
                    mm(o[:, 0], Bh[r, j, c * P:(c + 1) * P], kr)
                    mm(o[:, 1], Kh[r, j, c * P:(c + 1) * P], kr).then_inc(full[b], 1)
            for c in range(NC):
                for e in range(2):
                    b = 4 + 2 * c + e
                    o = v3(pe_open(pe, f"L{c}{e}", b)[:, 0:T], P)
                    r = slice(HD * e, HD * e + HD)
                    for j in range(2):
                        last = mm(o[:, j, :], KR[r, 0, j, c * P:(c + 1) * P], Bh[r, j, c * P:(c + 1) * P])
                    last.then_inc(full[b], 1)
            o = v4(pe_open(pe, "rw_bkt", 3)[:, :], 2, P)
            for e, src in enumerate((Bh, Kh)):
                for j in range(2):
                    last = nc.tensor.transpose(o[:, e, j, :], src[:, j, 0:P], const("ident"))
            last.then_inc(full[3], 1)

            level_p(1, 0, 4)
            level_p(1, 1, 6)
            s5_in(2, 0)
            s5_in(3, 2)
            channel_major(9, "mb_q", 1, hT)
            s5_out(0, 3)
            level_x(1, 0)
            level_x(1, 1)

            level_p(2, 0, 4)
            level_p(2, 1, 6)
            channel_major(10, "mb_k", 0, hT)
            o = v3(pe_open(pe, "g_col", 2)[:, 0:8], 4)
            pe.wait_ge(S["ml_rows"], 1)
            for c in range(NC):
                last = nc.tensor.transpose(o[:, c, :], rows[1][0:NH, c * P:(c + 1) * P], const("ident", NH)[:, 0:NH])
            last.then_inc(full[2], 1)
            pe.wait_ge(S["ml_rows"], 2)
            for m in range(2):
                b = 1 + m
                o = v3(pe_open(pe, f"m_row{m}", b)[:, :], T)
                for e in range(2):
                    h = 2 * m + e
                    last = mm(o[:, e, :], const("head_sel", NH)[:, h * P:(h + 1) * P], rows[2][0:NH, :])
                last.then_inc(full[b], 1)
            level_x(2, 0)
            level_x(2, 1)

            level_p(3, 0, 4)
            level_p(3, 1, 6)
            token_major(11, "mb_v", 0, hT)
            s5_in(4, 2)
            s5_in(5, 1)
            level_x(3, 0)
            level_x(3, 1)

            ml_qk(0, 2)
            ml_qk(1, 0)
            level_p(4, 0, 4)
            level_p(4, 1, 6)
            s5_out(1, 3)
            pe.wait_ge(S["mem_ready"], 1)
            wkv(0, 1)
            level_x(4, 0)
            level_x(4, 1)

            ml_qk(2, 2)
            ml_qk(3, 0)
            level_p(5, 0, 4)
            level_p(5, 1, 6)
            wkv(1, 1)
            level_x(5, 0)
            level_x(5, 1)

            moved(pe, "qk2")
            moved(pe, "qk3")
            moved(pe, "ml_v")
            attend("num", 2, mlv, E)
            attend("den", 0, None, E)
            o = v3(pe_open(pe, "em", 1)[:, :], T)
            pe.wait_ge(S["ml_em"], 1)
            for j in range(2):
                last = mm(o[:, j, :], const("pair_sel", NH)[:, j * P:(j + 1) * P], rows[4][0:NH, :])
            last.then_inc(full[1], 1)
            level_p(6, 0, 4)
            level_p(6, 1, 6)
            s5_in(6, 2)
            s5_in(7, 0)
            wkv(2, 1)
            level_x(6, 0)
            level_x(6, 1)

            moved(pe, "rw_vt")
            solve_r(0, 4)
            mb_scores(0, 2)
            mb_scores(1, 0)
            s5_out(2, 3)
            wkv(3, 1)
            solve_u(0, 5)
            mb_scores(2, 2)
            mb_scores(3, 0)
            wkv(4, 1)
            o = pe_open(pe, "S0", 4)
            moved(pe, "U0")
            moved(pe, "rw_bkt")
            for h in range(NH):
                r, j = at(h)
                hc = slice(h * HD, (h + 1) * HD)
                mm(o[r, j * HD:(j + 1) * HD], BKt[:, 0, hc], U[:, 0, hc], True, False)
                last = mm(o[r, j * HD:(j + 1) * HD], BKt[:, 1, hc], Vt[:, 0, hc], False, True)
            last.then_inc(full[4], 1)
            moved(pe, "S0")
            solve_r(1, 5)
            wkv(5, 1)
            solve_u(1, 4)
            o = pe_open(pe, "bonus", 7)
            pe.wait_ge(S["rw_bonus"], 1)
            mm(o[:, :], const("pair_ones"), flat(bon)).then_inc(full[7], 1)
            o = v3(pe_open(pe, "rw_y", 6)[:, :], T)
            moved(pe, "U1")
            for c in range(NC):
                for h in range(NH):
                    r, j = at(h)
                    hc = slice(h * HD, (h + 1) * HD)
                    y = o[r, j, c * P:(c + 1) * P]
                    mm(y, U[:, c, hc], A[:, c * NH + h, P:T], True, False)
                    last = mm(y, Vt[:, c, hc], A[:, c * NH + h, T + P:2 * T], False, c == 0)
                    if c == 1:
                        last = mm(y, S0[:, j, h % 2, :], KR[:, 1, j, P:T], False, True)
            last.then_inc(full[6], 1)
            wkv(6, 1)
            o = pe_open(pe, "mean", 4)
            moved(pe, "rw_y")
            mm(o[:, :], const("pair_ones"), flat(Yrw)).then_inc(full[4], 1)
            for h in range(NH):
                mb_turn(h, (2, 0)[h % 2])
            s5_out(3, 3)
            o = pe_open(pe, "var", 5)
            pe.wait_ge(S["rw_ysq"], 1)
            mm(o[:, :], const("pair_ones"), flat(Ysq)).then_inc(full[5], 1)
            group_sumsq("gn_ml", 1, 6)
            wkv(7, 1)
            moved(pe, "pt3")
            moved(pe, "mb_v")
            attend("mb_o", 2, mbv, PTm)
            o = v3(pe_open(pe, "glu", 3)[:, :], T)
            pe.wait_ge(S["s5_z"], 1)
            for j in range(2):
                for k in range(2):
                    last = mm(o[:, j, :], v3(prm("w_glu"), GW)[:, k, j * P:(j + 1) * P], z5[:, k, :], k == 0, k == 1)
            last.then_inc(full[3], 1)
            group_sumsq("gn_mb", 3, 0)
            group_sumsq("gn_rw", 2, 3)

            for q in range(8):
                if q == 2:
                    group_sumsq("gn_s5", 0, 1)
                if q in (0, 4):
                    pe.wait_ge(S["y_rest"], 2 * (q // 4) + 2)
                split_token_major(S_WOUT, q, f"wout{q % 4}", 4 + q % 4, y_split, Y_ORDER)

            def turn_stream(tag, n):
                pe.wait_ge(S["xn_ready"], n)
                for i in range(4):
                    o = v4(pe_open(pe, f"{tag}{i}", i)[:, :], 2, P)
                    for k in range(2):
                        for m in range(2):
                            last = nc.tensor.transpose(o[:, k, m, :], xtmp[:, m, (2 * i + k) * P:(2 * i + k + 1) * P],
                                                       const("ident"))
                    last.then_inc(full[i], 1)

            def turned(tag):
                def arrive(j):
                    for i in (2 * j, 2 * j + 1):
                        moved(pe, f"{tag}{i}")
                return arrive

            turn_stream("xat", 1)
            for i in range(N_WQ):
                split_channel_major(S_WQ + i, f"q{i}", 4 + i, h_split, None if i else turned("xat"))
            for h in range(XH):
                o = v3(pe_open(pe, f"xs{h}", h)[:, :], NMEM)
                moved(pe, f"q{h}")
                for m in range(2):
                    for k in range(2):
                        last = mm(o[:, m, :], qx[:, 2 * h + k, m * P:(m + 1) * P], kx[:, 2 * h + k, :], k == 0, k == 1)
                last.then_inc(full[h], 1)
            for h in range(XH):
                o = v3(pe_open(pe, f"xp{h}", 4 + h)[:, :], T)
                pe.wait_ge(S["x_prob"], h + 1)
                for m in range(2):
                    for t in range(2):
                        last = nc.tensor.transpose(o[:, m, t * P:(t + 1) * P], px[:, h, t, m * P:(m + 1) * P],
                                                   const("ident"))
                last.then_inc(full[4 + h], 1)
            for h in range(XH):
                o = v3(pe_open(pe, f"xo{h}", h)[:, :], T)
                moved(pe, f"xp{h}")
                for d in range(2):
                    for m in range(2):
                        c0 = h * XD + d * P
                        last = mm(o[:, d, :], vx[:, m, c0:c0 + P], ptx[:, h, m, :], m == 0, m == 1)
                last.then_inc(full[h], 1)
            for q in range(8):
                if q in (0, 4):
                    for h in (q // 2, q // 2 + 1):
                        moved(pe, f"xo{h}")
                split_token_major(S_WO, q, f"wo{q % 4}", 4 + q % 4, ox_split, range(KD))

            turn_stream("fft", 2)
            for p in range(NFF // 2):
                split_channel_major(S_FIN + 2 * p, f"g{p}", 2 * (p % 2), h_split, None if p else turned("fft"))
                split_channel_major(S_FIN + 2 * p + 1, f"u{p}", 2 * (p % 2) + 1, h_split)
            ys = [pe_open(pe, f"y{i}", 4 + i) for i in range(4)]
            for kt in range(NFF):
                i = 2 * (S_FOUT - S_SPLIT) + kt
                wait_rest(pe, i)
                if kt % 2 == 0:
                    pe.wait_ge(S["act_rest"], kt // 2 + 1)
                w = [flat(x) for x in w_split[i % HALF_BUFS]]
                for m in range(2):
                    for half in range(2):
                        last = mm3(ys[2 * m + half][:, :], [x[:, kt, m * P:(m + 1) * P] for x in act_split],
                                   [x[:, half * 512:(half + 1) * 512] for x in w], kt == 0, kt == NFF - 1)
                        if kt == NFF - 1:
                            last.then_inc(full[4 + 2 * m + half], 1)
                if kt < NFF - 1:
                    used(last, i)

        @block.sync
        def _(sp):
            for n in range(NSLOTS):
                if n == S_WQ:
                    sp.wait_ge(S["gn_done"], 4)
                    sp.dma_start(xres, x_rows.rearrange("(m p) c -> p m c", p=P)).then_inc(S["xres_in"], 16)
                    sp.dma_start(gain_, gain_rows(0)).then_inc(S["gain_in"], 16)
                if n in (S_WO, S_FIN + 8):
                    g = 1 if n == S_WO else 2
                    sp.wait_ge(S["x_new"], 2 * g - 1)
                    sp.dma_start(gain_, gain_rows(g)).then_inc(S["gain_in"], 16)
                before = n - RING
                if before >= S_SPLIT:
                    for i in range(2):
                        wait_rest(sp, 2 * (before - S_SPLIT) + i)
                elif before >= 0:
                    wait_full(sp, user_of[before])
                sp.dma_start(slot(n), weights_d[n]).then_inc(loaded[n % RING], 16)
                if n == 5:
                    for h in range(NH):
                        moved(sp, f"rel{h}")
                    sp.dma_start(rel_scratch.ap(), E_).then_inc(S["rel_stored"], 16)
                if n == 9:
                    sp.wait_ge(S["rel_stored"], 16)
                    sp.wait_ge(S["rw_tilde"], 4)
                    skew = bass.AP(rel_scratch, P - 1, [[NH * 384 - 1, P], [384, NH], [1, T]])
                    sp.dma_start(Bz, skew).then_inc(S["rel_in"], 16)
            for m in range(2):
                sp.wait_ge(S["x_new"], 5 + m)
                sp.dma_start(out[0, m * P:(m + 1) * P, :], xres[:, m, :]).then_inc(S["out_stored"], 16)
            sp.wait_ge(S["out_stored"], 32)

        @block.gpsimd
        def _(pool):
            g = nc.gpsimd
            g.memset(rwP[:, :, 0:1], 0.0).then_inc(S["zeros_ready"], 1)
            g.memset(raw[:, :, 0:3], 0.0).then_inc(S["zeros_ready"], 1)
            g.memset(S0_, 0.0).then_inc(S["zeros_ready"], 1)
            pool.wait_ge(S["s5_co"], 1)
            wr, wi, xr, xi = (v3(pr_[:, 256 * i:256 * i + 256], 32) for i in range(4))
            g.tensor_tensor(wr, c_re, spread(co_re, 32), ALU.mult)
            g.tensor_tensor(wi, c_im, spread(co_im, 32), ALU.mult)
            g.tensor_tensor(xr, c_re, spread(co_im, 32), ALU.mult)
            g.tensor_tensor(xi, c_im, spread(co_re, 32), ALU.mult).then_inc(S["s5_c"], 1)
            pool.wait_ge(S["s5_c"], 1)
            g.tensor_tensor(c_nre, wi, wr, ALU.subtract)
            g.tensor_tensor(c_re, wr, wi, ALU.subtract)
            g.tensor_tensor(xr, xr, xi, ALU.add).then_inc(S["s5_c"], 1)
            pool.wait_ge(S["s5_c"], 2)
            g.tensor_scalar(c_im, xr, -1.0, None, ALU.mult).then_inc(S["s5_c"], 1)

            def rotate(q):
                cq, sq = cos[:, 2 * q:2 * q + 2, :], sin[:, 2 * q:2 * q + 2, :]
                moved(pool, f"bu{2 * q}")
                moved(pool, f"bu{2 * q + 1}")
                if q > 0:
                    pool.wait_ge(S["rotated_back"], q)
                g.tensor_tensor(t1, cq, bu[:, 0], ALU.mult)
                g.tensor_tensor(t2, cq, bu[:, 1], ALU.mult).then_inc(S["rotating"], 1)
                pool.wait_ge(S["rotating"], 3 * q + 1)
                g.tensor_tensor(bu[:, 1], sq, bu[:, 1], ALU.mult)
                g.tensor_tensor(bu[:, 0], sq, bu[:, 0], ALU.mult).then_inc(S["rotating"], 1)
                pool.wait_ge(S["rotating"], 3 * q + 2)
                g.tensor_tensor(t1, t1, bu[:, 1], ALU.add)
                g.tensor_tensor(t2, t2, bu[:, 0], ALU.subtract).then_inc(S["rotating"], 1)

            def rotate_back(q):
                cq, sq = cos[:, 2 * q:2 * q + 2, :], sin[:, 2 * q:2 * q + 2, :]
                pool.wait_ge(S["scanned"], q + 1)
                if q > 0:
                    pool.wait_ge(S["s5_out_used"], q)
                for x, (a_, b_) in enumerate(((cq, t1), (sq, t2), (cq, t2), (sq, t1))):
                    last = g.tensor_tensor(pr[:, x], a_, b_, ALU.mult)
                last.then_inc(S["rotated_back"], 1)

            def level_mask(n):
                for c in range(NC):
                    if n > 1:
                        wait_full(pool, f"P{n - 1}{c}")
                    g.tensor_tensor(Mj[:, c], A[:, NH * c:NH * (c + 1), 0:P],
                                    copies(const("levels")[:, n * P:(n + 1) * P], NH),
                                    ALU.mult).then_inc(S["rw_level_mask"], 1)

            pool.wait_ge(S["sincos"], 3)
            rotate(0)
            rotate_back(0)
            for c in range(NC):
                moved(pool, f"A{NH * c + 3}")
                for i in range(NH * c, NH * c + 3):
                    moved(pool, f"A{i}")
                g.tensor_tensor(XT[:, c], A[:, NH * c:NH * (c + 1), 0:P], copies(const("levels")[:, 0:P], NH),
                                ALU.mult).then_inc(S["rw_xt0"], 1)
                pool.wait_ge(S["rw_xt0"], 2 * c + 1)
                g.tensor_tensor(XT[:, c], copies(const("ident"), NH), XT[:, c], ALU.subtract).then_inc(S["rw_xt0"], 1)
            level_mask(1)
            rotate(1)
            level_mask(2)
            rotate_back(1)
            level_mask(3)
            rotate(2)
            level_mask(4)
            rotate_back(2)
            level_mask(5)
            level_mask(6)
            rotate(3)
            rotate_back(3)
            for i in range(1, NHALF, 2):
                rest(pool, g, i)

        @block.scalar
        def _(act):
            a = nc.scalar
            LN_EXP = "natural_log_exp_and_others"
            act.dma_start(hT, v3(x_t, T)).then_inc(S["x_in"], 16)
            act.dma_start(cst[:, :], consts_d).then_inc(S["consts_in"], 16)
            act.dma_start(par[:, :], params_d).then_inc(S["params_in"], 16)
            act.dma_start(memT, v3(mem_t, NMEM)).then_inc(S["mem_in"], 16)
            a.preload_act_table_set(LN_EXP)

            def project(name, out_):
                o = wait_full(act, name)
                a.activation(out_, v3(o[:, :], 256), ACT.Copy).then_inc(free_of(name), 1)

            def inv_root(name, out_, width, scale, eps):
                o = wait_full(act, name)
                a.activation(out_, o[:, 0:width], ACT.Ln, bias=const(eps), scale=scale).then_inc(free_of(name), 1)
                moved(act, name)
                return a.activation(out_, out_, ACT.Exp, scale=-0.5)

            def s5_driving(i):
                if i in (2, 4, 6):
                    act.wait_ge(S["rotating"], 3 * (i // 2))
                project(f"bu{i}", bu[:, :, i % 2, :])

            def level_evac(n):
                for c in range(NC):
                    o = wait_full(act, f"P{n}{c}")
                    a.activation(Pm[:, c], v3(o[:, :], P), ACT.Copy).then_inc(free_of(f"P{n}{c}"), 1)

            def wkv_evac(i):
                project(f"wkv{i}", kx[:, 2 * i:2 * i + 2, :] if i < 4 else vx[:, :, (i - 4) * 256:(i - 3) * 256])

            act.wait_ge(S["x_in"], 16)
            a.activation(sq_x, hT, ACT.Square).then_inc(S["sq_ready"], 1)
            act.wait_ge(S["consts_in"], 16)
            inv_root("x_sumsq", rstd_x, T, 1.0 / D, "eps6").then_inc(S["rstd_x"], 1)
            act.wait_ge(S["params_in"], 16)
            a.activation(step, prm("log_step"), ACT.Exp).then_inc(S["s5_step"], 1)
            act.wait_ge(S["s5_decay"], 1)
            a.activation(mag, s8a, ACT.Exp).then_inc(S["s5_step"], 1)
            act.wait_ge(S["mem_in"], 16)
            a.activation(sq_m, memT, ACT.Square).then_inc(S["sq_m_ready"], 1)
            act.wait_ge(S["theta"], 6)
            a.activation(cos, sin, ACT.Abs).then_inc(S["sincos"], 1)
            act.wait_ge(S["sincos"], 1)
            a.activation(cos, cos, ACT.Sin, bias=const("half_pi"), scale=-TAU).then_inc(S["sincos"], 1)
            a.activation(sin, sin, ACT.Sin, scale=TAU).then_inc(S["sincos"], 1)
            a.preload_act_table_set(LN_EXP)
            act.wait_ge(S["zeros_ready"], 1)
            project("rw_wag", rwP[:, 0:2, 1:257])
            project("rw_k", rwP[:, 2:4, 1:257])
            inv_root("mem_sumsq", rstd_m, T, 1.0 / D, "eps6").then_inc(S["rstd_m"], 1)
            act.wait_ge(S["rw_mix"], 1)
            a.activation(rwE[0:HD, 0, 0, :], rwM[0:HD, 0, :], ACT.Exp, scale=-2.0)
            a.activation(rwE[:, 0, 1, :], rwM[:, 1, :], ACT.Exp, scale=-1.0).then_inc(S["rw_exp"], 1)
            project("rw_r", rwP[:, 4:6, 1:257])
            project("rw_v", rwP[:, 6:8, 1:257])
            act.wait_ge(S["rw_mix"], 4)
            act.wait_ge(S["neg_ready"], 1)
            for name, out_, b in (("rw_w", G, 0), ("rw_a", ab, 2)):
                o = v3(wait_full(act, name)[:, :], T)
                for j in range(2):
                    e = a.activation(out_[:, j, :], o[:, j, :], ACT.Exp, bias=neg_w0a0[:, b + j:b + j + 1], scale=-1.0)
                e.then_inc(free_of(name), 1)
            project("s5_u", s5u)
            project("rw_g", rwg)
            act.wait_ge(S["zeros_ready"], 2)
            project("ml_q", raw[:, 0:2, 3:259])
            inv_root("rw_kk", flat(rwE[:, 2]), 512, 1.0, "eps12").then_inc(S["rw_inv"], 1)
            project("ml_k", raw[:, 2:4, 3:259])
            act.wait_ge(S["rw_G"], 4)
            a.activation(rwE[:, 0], Gp, ACT.Exp)
            a.activation(rwE[:, 1], G, ACT.Exp)
            a.activation(carry, carry, ACT.Exp)
            act.wait_ge(S["rw_kk"], 1)
            a.activation(rwE[:, 2], Gp, ACT.Exp, scale=-1.0).then_inc(S["rw_E"], 1)
            s5_driving(0)
            s5_driving(1)
            project("rw_vt", Vt)
            act.wait_ge(S["rw_E"], 1)
            project("ml_v", mlv)
            o = wait_full(act, "ml_o")
            a.activation(mlo, v3(o[:, :], T), ACT.Exp, scale=-1.0).then_inc(free_of("ml_o"), 1)
            project("rw_bkt", BKt)

            level_evac(1)
            s5_driving(2)
            s5_driving(3)
            act.wait_ge(S["rw_tilde"], 4)
            project("mb_q", mqk[:, 0:2, :])
            act.wait_ge(S["ml_gate"], 1)
            a.activation(rows[3][0:NH, :], rows[0][0:NH, :], ACT.Abs).then_inc(S["ml_log"], 1)
            act.wait_ge(S["ml_log"], 1)
            a.activation(rows[3][0:NH, :], rows[3][0:NH, :], ACT.Exp, scale=-1.0).then_inc(S["ml_log"], 1)
            act.wait_ge(S["ml_log"], 2)
            a.activation(rows[3][0:NH, :], rows[3][0:NH, :], ACT.Ln, bias=const("ones", NH)[:, 0:1]).then_inc(S["ml_log"], 1)
            act.wait_ge(S["ml_conv"], 4)
            act.wait_ge(S["rel_stored"], 16)
            a.activation(E_[:, 0:1024], flat(cv), ACT.Exp, scale=-1.0).then_inc(S["ml_silu"], 1)
            level_evac(2)
            project("mb_k", mqk[:, 2:4, :])
            act.wait_ge(S["ml_rows"], 3)
            a.activation(rows[4][0:NH, :], rows[4][0:NH, :], ACT.Exp).then_inc(S["ml_em"], 1)
            level_evac(3)
            project("mb_v", mbv)
            moved(act, "m_row0")
            moved(act, "m_row1")
            a.activation(E_, E_, ACT.Exp).then_inc(S["ml_E"], 1)
            s5_driving(4)
            s5_driving(5)
            level_evac(4)
            wkv_evac(0)
            level_evac(5)
            wkv_evac(1)
            level_evac(6)
            s5_driving(6)
            s5_driving(7)
            wkv_evac(2)
            wkv_evac(3)
            wkv_evac(4)
            act.wait_ge(S["mb_max"], 1)
            for h in range(NH):
                for m, (lo, hi) in enumerate(((0, P), (P, P + T))):
                    e = a.activation(Sm[:, h, lo:hi], Sm[:, h, lo:hi], ACT.Exp, bias=nmax[:, 4 * m + h:4 * m + h + 1],
                                     accum_out=mb_sum[:, 4 * m + h:4 * m + h + 1])
            e.then_inc(S["mb_exp"], 1)
            wkv_evac(5)
            wkv_evac(6)
            moved(act, "mean")
            a.activation(Ysq, Yrw, ACT.Square).then_inc(S["rw_ysq"], 1)
            for h in range(NH):
                o = wait_full(act, f"pt{h}")
                a.activation(PTm[:, h, :], o[:, 0:384], ACT.Copy).then_inc(free_of(f"pt{h}"), 1)
            inv_root("var", Pm_[:, 0:512], 512, 1.0 / HD, "eps_gn").then_inc(S["rw_rstd"], 1)
            split = [0]

            def highs(upto):
                while split[0] < min(upto, NHALF):
                    high_part(act, split[0])
                    split[0] += 1

            wait_full(act, "rw_y")
            act.wait_ge(S["rotated_back"], 4)
            highs(4)

            def group_square(g_, name):
                a.activation(gn_sq[g_], yT[:, 2 * g_:2 * g_ + 2, :], ACT.Square).then_inc(S[name + "_sq"], 1)

            def group_root(g_, name):
                inv_root("gn_" + name, gn_sq[g_][:, 0, :], T, 1.0 / GW, "eps6").then_inc(S[name + "_root"], 1)

            moved(act, "num")
            group_square(1, "ml")
            group_root(1, "ml")
            wkv_evac(7)
            act.wait_ge(S["s5_arg"], 1)
            a.activation(z5b, z5a, ACT.Exp, scale=-GELU).then_inc(S["s5_exp"], 1)
            moved(act, "mb_o")
            group_square(3, "mb")
            o = v3(wait_full(act, "glu")[:, :], T)
            for j in range(2):
                e = a.activation(z5b[:, j, :], o[:, j, :], ACT.Exp, bias=neg_bglu[:, j:j + 1], scale=-1.0)
            e.then_inc(free_of("glu"), 1)
            group_root(3, "mb")
            act.wait_ge(S["rw_out"], 1)
            group_square(2, "rw")
            group_root(2, "rw")

            def y_high(turn, g_):
                act.wait_ge(S["gn_done"], turn + 1)
                a.activation(y_split[0][:, 2 * g_:2 * g_ + 2, :], yT[:, 2 * g_:2 * g_ + 2, :],
                             ACT.Copy).then_inc(S["high_ready"], 1)

            y_high(0, 1)
            y_high(1, 3)
            act.wait_ge(S["s5_out"], 1)
            group_square(0, "s5")
            group_root(0, "s5")
            y_high(2, 2)
            y_high(3, 0)
            highs(11)

            def post_root(n, pieces):
                for name, src, m, part in pieces:
                    o = wait_full(act, name)
                    w = src[1] - src[0]
                    e = a.activation(xtmp[:, m, part * w:(part + 1) * w], o[:, src[0]:src[1]], ACT.Square,
                                     accum_out=ssq[:, 4 * m + part:4 * m + part + 1])
                e.then_inc(S["post_ssq"], 1)
                act.wait_ge(S["post_sum"], n + 1)
                a.activation(rst, rst, ACT.Ln, bias=const("eps6"), scale=1.0 / D).then_inc(S["post_ssq"], 1)
                act.wait_ge(S["post_ssq"], 3 * n + 2)
                a.activation(rst, rst, ACT.Exp, scale=-0.5).then_inc(S["post_ssq"], 1)

            def pre_root(n):
                act.wait_ge(S["x_new"], 2 * (n + 1))
                for m in range(2):
                    e = a.activation(xtmp[:, m, :], xres[:, m, :], ACT.Square, accum_out=rst[:, m:m + 1])
                e.then_inc(S["pre_ssq"], 1)
                act.wait_ge(S["pre_ssq"], 3 * n + 1)
                a.activation(rst, rst, ACT.Ln, bias=const("eps6"), scale=1.0 / D).then_inc(S["pre_ssq"], 1)
                act.wait_ge(S["pre_ssq"], 3 * n + 2)
                a.activation(rst, rst, ACT.Exp, scale=-0.5).then_inc(S["pre_ssq"], 1)

            def high_of_bank(name, out_, scale=1.0):
                o = v3(wait_full(act, name)[:, :], T)
                if isinstance(scale, float):
                    return a.activation(out_, o, ACT.Copy, scale=scale)
                for k in range(2):
                    e = a.activation(out_[:, k, :], o[:, k, :], ACT.Copy, scale=scale[:, k:k + 1])
                return e

            def turned(tag, gain):
                for i in range(4):
                    high_of_bank(f"{tag}{i}", h_split[0][:, 2 * i:2 * i + 2, :],
                                 prm(gain)[:, 2 * i:2 * i + 2]).then_inc(S["high_ready"], 1)

            post_root(0, [(f"wout{i}", (256 * m, 256 * m + 256), m, i) for i in range(4) for m in range(2)])
            pre_root(0)
            turned("xat", "pre_xa")
            highs(12)
            for i in range(N_WQ):
                highs(14 + 2 * i)
                project(f"q{i}", qx[:, 2 * i:2 * i + 2, :])
            for h in range(XH):
                o = v3(wait_full(act, f"xs{h}")[:, :], NMEM)
                act.wait_ge(S["x_max"], 2 * (h + 1))
                for m in range(2):
                    e = a.activation(px[:, h, m, :], o[:, m, :], ACT.Exp, bias=xmax[:, 2 * h + m:2 * h + m + 1],
                                     scale=XD ** -0.5, accum_out=xsum[:, 2 * h + m:2 * h + m + 1])
                e.then_inc(free_of(f"xs{h}"), 1)
            for h in range(XH):
                project(f"xp{h}", ptx[:, h])
            for h in range(XH):
                high_of_bank(f"xo{h}", ox_split[0][:, 2 * h:2 * h + 2, :]).then_inc(S["high_ready"], 1)
            first = 2 * (S_FIN - S_SPLIT)
            highs(first + 3)
            post_root(1, [(f"wo{i}", (256 * m, 256 * m + 256), m, i) for i in range(4) for m in range(2)])
            pre_root(1)
            turned("fft", "pre_ffn")
            highs(first + 4)

            def act_high(p):
                moved(act, f"u{p}")
                a.activation(flat(act_split[0][:, 2 * p:2 * p + 2, :]), fft[:, p % 2, :],
                             ACT.Copy).then_inc(S["high_ready"], 1)

            for p in range(NFF // 2):
                highs(first + 4 * p + 6)
                o = wait_full(act, f"g{p}")
                if p > 1:
                    act.wait_ge(S["act_rest"], p - 1)
                a.activation(fft[:, p % 2, :], o[:, :], ACT.Exp, scale=-1.0).then_inc(S["f_exp"], 1)
                if p > 0:
                    act_high(p - 1)
                highs(first + 4 * p + 8)
            act_high(NFF // 2 - 1)
            highs(NHALF)
            post_root(2, [(f"y{2 * m + i}", (0, 512), m, i) for m in range(2) for i in range(2)])

        @block.vector
        def _(dve):
            v = nc.vector

            def sigmoid_of_exp(x, name, n):
                v.tensor_scalar(x, x, 1.0, None, ALU.add).then_inc(S[name], 1)
                dve.wait_ge(S[name], n + 1)
                return v.reciprocal(x, x)

            dve.wait_ge(S["params_in"], 16)
            dve.wait_ge(S["consts_in"], 16)
            a, b = PARAM["w0"][0], PARAM["a0"][1]
            v.tensor_scalar(neg_w0a0, par[:, a:b], -1.0, None, ALU.mult)
            v.tensor_scalar(neg_bglu, prm("b_glu"), -1.0, None, ALU.mult)
            v.tensor_scalar(one_ka, prm("k_a"), -1.0, 1.0, ALU.mult, ALU.add).then_inc(S["neg_ready"], 1)
            for h in range(NH):
                o = wait_full(dve, f"rel{h}")
                v.tensor_copy(E[:, h, :], o[:, 0:384]).then_inc(free_of(f"rel{h}"), 1)
            dve.wait_ge(S["rstd_x"], 1)
            for k in range(KD):
                last = v.scalar_tensor_tensor(hT[:, k, :], hT[:, k, :], prm("pre_mix")[:, k:k + 1], rstd_x,
                                              ALU.mult, ALU.mult)
            last.then_inc(S["h_ready"], 1)
            dve.wait_ge(S["s5_step"], 1)
            v.tensor_tensor(s8a, prm("lam_re"), step, ALU.mult).then_inc(S["s5_decay"], 1)
            v.scalar_tensor_tensor(frac, prm("lam_im"), 1.0 / (2.0 * math.pi), step, ALU.mult, ALU.mult).then_inc(S["theta"], 1)
            dve.wait_ge(S["theta"], 1)
            v.tensor_scalar(frn, frac, ROUND, None, ALU.add).then_inc(S["theta"], 1)
            dve.wait_ge(S["theta"], 2)
            v.scalar_tensor_tensor(frac, frn, ROUND, frac, ALU.subtract, ALU.subtract).then_inc(S["theta"], 1)
            dve.wait_ge(S["theta"], 3)
            for i in range(8):
                last = v.tensor_scalar(sin[:, i, :], const("time"), frac[:, i:i + 1], None, ALU.mult)
            last.then_inc(S["theta"], 1)
            dve.wait_ge(S["theta"], 4)
            v.tensor_scalar(cos, sin, ROUND, None, ALU.add).then_inc(S["theta"], 1)
            dve.wait_ge(S["theta"], 5)
            v.scalar_tensor_tensor(sin, cos, ROUND, sin, ALU.subtract, ALU.subtract).then_inc(S["theta"], 1)

            def mix(n, name):
                moved(dve, name)
                v.tensor_tensor(rwM[:, 2 * n:2 * n + 2, :], rwP[:, 2 * n:2 * n + 2, 0:T], rwP[:, 2 * n:2 * n + 2, 1:T + 1],
                                ALU.subtract).then_inc(S["rw_diff"], 1)
                dve.wait_ge(S["rw_diff"], n + 1)
                for i in (2 * n, 2 * n + 1):
                    last = v.scalar_tensor_tensor(rwM[:, i, :], rwM[:, i, :], prm("mu")[:, i:i + 1], rwP[:, i, 1:T + 1],
                                                  ALU.mult, ALU.add)
                last.then_inc(S["rw_mix"], 1)

            dve.wait_ge(S["zeros_ready"], 1)
            mix(0, "rw_wag")
            mix(1, "rw_k")
            dve.wait_ge(S["rw_exp"], 1)
            v.tensor_scalar(rwE[0:HD, 0, 0, :], rwE[0:HD, 0, 0, :], 1.0, None, ALU.add)
            v.tensor_scalar(rwE[:, 0, 1, :], rwE[:, 0, 1, :], 1.0, None, ALU.add).then_inc(S["rw_low"], 1)
            dve.wait_ge(S["rw_low"], 1)
            v.reciprocal(rwE[0:HD, 0, 0, :], rwE[0:HD, 0, 0, :])
            v.reciprocal(rwE[:, 0, 1, :], rwE[:, 0, 1, :]).then_inc(S["rw_low"], 1)
            dve.wait_ge(S["rw_low"], 2)
            v.tensor_scalar(rwE[0:HD, 0, 0, :], rwE[0:HD, 0, 0, :], 2.0, -1.0, ALU.mult, ALU.add).then_inc(S["rw_lowrank"], 1)
            mix(2, "rw_r")
            mix(3, "rw_v")
            dve.wait_ge(S["rw_mix"], 4)
            for j in range(2):
                last = v.tensor_scalar(kk[:, j, :], rwM[:, 2 + j, :], prm("k_k")[:, j:j + 1], None, ALU.mult)
            last.then_inc(S["rw_kx"], 1)
            dve.wait_ge(S["rw_kx"], 1)
            v.tensor_tensor(rwE[:, 1], kk, kk, ALU.mult).then_inc(S["rw_kx_sq"], 1)
            moved(dve, "rw_w")
            sigmoid_of_exp(G, "rw_G0", 0).then_inc(S["rw_G0"], 1)
            dve.wait_ge(S["rw_G0"], 2)
            v.tensor_scalar(G, G, -DECAY, None, ALU.mult).then_inc(S["rw_G0"], 1)
            dve.wait_ge(S["rw_G0"], 3)
            for j in range(2):
                for c in range(NC):
                    cs = slice(c * C, (c + 1) * C)
                    last = v.tensor_tensor_scan(Gp[:, j, cs], const("ones"), G[:, j, cs], 0.0, ALU.mult, ALU.add)
            last.then_inc(S["rw_G"], 1)
            dve.wait_ge(S["rw_G"], 1)
            Gpc, Gc = v3(flat(Gp), C), v3(flat(G), C)
            v.tensor_copy(mid, Gpc[:, :, C // 2 - 1]).then_inc(S["rw_G"], 1)
            dve.wait_ge(S["rw_G"], 2)
            v.tensor_tensor(Gpc, Gpc, spread(mid, C), ALU.subtract).then_inc(S["rw_G"], 1)
            dve.wait_ge(S["rw_G"], 3)
            v.tensor_tensor(carry, Gp[:, :, C - 1], mid[:, 1:4:2], ALU.add)
            v.tensor_tensor(G, Gp, G, ALU.subtract).then_inc(S["rw_G"], 1)
            moved(dve, "rw_a")
            sigmoid_of_exp(ab, "rw_a", 0).then_inc(S["rw_a"], 1)
            dve.wait_ge(S["rw_inv"], 1)
            v.tensor_tensor(kk, kk, rwE[:, 2], ALU.mult).then_inc(S["rw_kk"], 1)
            dve.wait_ge(S["rw_a"], 2)
            k2 = rwM[:, 2:4, :]
            for j in range(2):
                last = v.tensor_scalar(Kh[:, j, :], ab[:, j, :], prm("k_a")[:, j:j + 1], one_ka[:, j:j + 1], ALU.mult, ALU.add)
            last.then_inc(S["rw_k2"], 1)
            dve.wait_ge(S["rw_kk"], 1)
            dve.wait_ge(S["rw_k2"], 1)
            v.tensor_tensor(ab, kk, ab, ALU.mult).then_inc(S["rw_k2"], 1)
            v.tensor_tensor(k2, k2, Kh, ALU.mult).then_inc(S["rw_k2"], 1)
            dve.wait_ge(S["rw_k2"], 3)
            dve.wait_ge(S["rw_E"], 1)
            v.tensor_tensor(KR[:, 0], kk, rwE[:, 1], ALU.mult).then_inc(S["rw_tilde"], 1)
            v.tensor_tensor(KR[:, 1], rwM[:, 4:6, :], rwE[:, 0], ALU.mult).then_inc(S["rw_tilde"], 1)
            v.tensor_tensor(Bh, ab, rwE[:, 2], ALU.mult).then_inc(S["rw_tilde"], 1)
            v.tensor_tensor(Kh, k2, rwE[:, 2], ALU.mult).then_inc(S["rw_tilde"], 1)
            dve.wait_ge(S["rw_tilde"], 2)
            for j in range(2):
                last = v.scalar_tensor_tensor(bon[:, j, :], bon[:, j, :], prm("r_k")[:, j:j + 1], k2[:, j, :],
                                              ALU.mult, ALU.mult)
            last.then_inc(S["rw_bonus"], 1)
            dve.wait_ge(S["sincos"], 3)
            cos1, sin1, lr, li = cos[:, :, 1], sin[:, :, 1], prm("lam_re"), prm("lam_im")
            v.tensor_tensor(s8b, mag, cos1, ALU.mult)
            v.tensor_tensor(s8c, mag, sin1, ALU.mult)
            v.tensor_tensor(den8, lr, lr, ALU.mult)
            v.tensor_tensor(s8a, li, li, ALU.mult).then_inc(S["s5_co_step"], 1)
            dve.wait_ge(S["s5_co_step"], 1)
            v.tensor_tensor(den8, den8, s8a, ALU.add)
            v.tensor_scalar(s8b, s8b, -1.0, None, ALU.add).then_inc(S["s5_co_step"], 1)
            dve.wait_ge(S["s5_co_step"], 2)
            v.reciprocal(den8, den8)
            v.tensor_tensor(co_re, s8b, lr, ALU.mult)
            v.tensor_tensor(s8a, s8c, li, ALU.mult)
            v.tensor_tensor(co_im, s8c, lr, ALU.mult)
            v.tensor_tensor(frn, s8b, li, ALU.mult).then_inc(S["s5_co_step"], 1)
            dve.wait_ge(S["s5_co_step"], 3)
            v.tensor_tensor(co_re, co_re, s8a, ALU.add)
            v.tensor_tensor(co_im, co_im, frn, ALU.subtract).then_inc(S["s5_co_step"], 1)
            dve.wait_ge(S["s5_co_step"], 4)
            v.tensor_tensor(co_re, co_re, den8, ALU.mult)
            v.tensor_tensor(co_im, co_im, den8, ALU.mult).then_inc(S["s5_co"], 1)

            def scan(q):
                dve.wait_ge(S["rotating"], 3 * (q + 1))
                for i in range(2):
                    decay = mag[:, 2 * q + i:2 * q + i + 1].to_broadcast([P, T])
                    v.tensor_tensor_scan(t1[:, i, :], decay, t1[:, i, :], 0.0, ALU.mult, ALU.add)
                    last = v.tensor_tensor_scan(t2[:, i, :], decay, t2[:, i, :], 0.0, ALU.mult, ALU.add)
                last.then_inc(S["scanned"], 1)

            mask2 = cst[:, CONST["strict"][0]:CONST["incl"][1]]
            for i in range(8):
                o = wait_full(dve, f"A{i}")
                v.tensor_tensor(v3(A[:, i, :], 256), v3(o[:, :], 256), copies(mask2, 2), ALU.mult).then_inc(free_of(f"A{i}"), 1)
            for c in range(NC):
                for e in range(2):
                    o = wait_full(dve, f"L{c}{e}")
                    v.tensor_tensor(X[:, c, e:NH:2], v3(o[:, 0:T], P), copies(const("level0_t"), 2),
                                    ALU.mult).then_inc(free_of(f"L{c}{e}"), 1)
                moved(dve, f"L{c}0")
                moved(dve, f"L{c}1")
                v.tensor_tensor(X[:, c], copies(const("ident"), NH), X[:, c], ALU.subtract).then_inc(S["rw_x0"], 1)
            scan(0)
            o = wait_full(dve, "gates")
            v.tensor_scalar(rows[0][0:NH, :], o[0:NH, T:2 * T], prm("f_bias", NH), None, ALU.add).then_inc(S["ml_gate"], 1)
            v.tensor_scalar(rows[1][0:NH, :], o[0:NH, 0:T], prm("i_bias", NH), None, ALU.add).then_inc(free_of("gates"), 1)
            moved(dve, "ml_q")
            moved(dve, "ml_k")
            dve.wait_ge(S["zeros_ready"], 2)
            cw = v3(prm("conv"), 4)
            for tap in range(4):
                if tap > 0:
                    dve.wait_ge(S["ml_conv"], tap)
                for i in range(4):
                    w, x = cw[:, i, tap:tap + 1], raw[:, i, tap:tap + T]
                    if tap == 0:
                        last = v.tensor_scalar(cv[:, i, :], x, w, None, ALU.mult)
                    else:
                        last = v.scalar_tensor_tensor(cv[:, i, :], x, w, cv[:, i, :], ALU.mult, ALU.add)
                last.then_inc(S["ml_conv"], 1)

            def level_update(n):
                for c in range(NC):
                    if n < LEVELS - 1:
                        o = wait_full(dve, f"X{n}{c}")
                        v.tensor_tensor(X[:, c], X[:, c], v3(o[:, :], P), ALU.subtract).then_inc(free_of(f"X{n}{c}"), 1)
                    o = wait_full(dve, f"T{n}{c}")
                    v.tensor_tensor(XT[:, c], XT[:, c], v3(o[:, :], P), ALU.subtract).then_inc(free_of(f"T{n}{c}"), 1)

            level_update(1)
            scan(1)
            dve.wait_ge(S["ml_log"], 3)
            lf, g_, nM, F, em = (rows[i][0:NH, :] for i in (0, 1, 2, 3, 4))
            v.scalar_tensor_tensor(lf, lf, 0.0, F, ALU.min, ALU.subtract).then_inc(S["ml_row_step"], 1)
            dve.wait_ge(S["ml_row_step"], 1)
            one = const("ones", NH)[:, 0:1].to_broadcast([NH, T])
            v.tensor_tensor_scan(F, one, lf, 0.0, ALU.mult, ALU.add).then_inc(S["ml_row_step"], 1)
            dve.wait_ge(S["ml_row_step"], 2)
            v.tensor_tensor(g_, g_, F, ALU.subtract).then_inc(S["ml_rows"], 1)
            dve.wait_ge(S["ml_rows"], 1)
            v.tensor_tensor_scan(lf, g_, g_, 0.0, ALU.max, ALU.max).then_inc(S["ml_row_step"], 1)
            dve.wait_ge(S["ml_row_step"], 3)
            v.tensor_scalar(nM, lf, -1.0, None, ALU.mult).then_inc(S["ml_rows"], 1)
            v.scalar_tensor_tensor(em, F, -1.0, lf, ALU.mult, ALU.subtract).then_inc(S["ml_rows"], 1)
            dve.wait_ge(S["ml_silu"], 1)
            ex = v3(E_[:, 0:1024], T)
            sigmoid_of_exp(ex, "ml_sig", 0).then_inc(S["ml_sig"], 1)
            dve.wait_ge(S["ml_sig"], 2)
            v.tensor_tensor(cv, cv, ex, ALU.mult).then_inc(S["ml_qk"], 1)
            o = wait_full(dve, "g_col")
            v.tensor_copy(gcol, o[:, 0:8]).then_inc(free_of("g_col"), 1)
            level_update(2)
            moved(dve, "g_col")
            dve.wait_ge(S["ml_qk"], 1)
            ca = const("causal_add")
            for m in range(2):
                o = v3(wait_full(dve, f"m_row{m}")[:, :], T)
                for e in range(2):
                    h = 2 * m + e
                    v.scalar_tensor_tensor(E[:, h, 0:T], o[:, e, :], gcol[:, h:h + 1], ca[:, 0:T], ALU.add, ALU.add)
                    last = v.scalar_tensor_tensor(E[:, h, T:T + P], o[:, e, P:T], gcol[:, 4 + h:5 + h], ca[:, T:T + P],
                                                  ALU.add, ALU.add)
                last.then_inc(free_of(f"m_row{m}"), 1)
            level_update(3)

            def ml_weight(h):
                o = wait_full(dve, f"qk{h}")
                dve.wait_ge(S["ml_E"], 1)
                v.scalar_tensor_tensor(E[:, h, :], o[:, 0:384], HD ** -0.5, E[:, h, :], ALU.mult,
                                       ALU.mult).then_inc(free_of(f"qk{h}"), 1)

            ml_weight(0)
            ml_weight(1)
            dve.wait_ge(S["rstd_m"], 1)
            for k in range(KD):
                last = v.scalar_tensor_tensor(memT[:, k, :], memT[:, k, :], prm("norm_mem")[:, k:k + 1], rstd_m,
                                              ALU.mult, ALU.mult)
            last.then_inc(S["mem_ready"], 1)
            level_update(4)
            scan(2)
            ml_weight(2)
            ml_weight(3)
            level_update(5)
            o = wait_full(dve, "den")
            den = v3(raw_cv[:, 0:512], T)
            v.tensor_scalar(den, v3(o[:, :], T), -1.0, None, ALU.mult).then_inc(S["ml_den"], 1)
            dve.wait_ge(S["ml_den"], 1)
            e = wait_full(dve, "em")
            v.tensor_tensor(den, den, v3(e[:, :], T), ALU.max).then_inc(free_of("em"), 1)
            moved(dve, "em")
            v.tensor_tensor(den, den, v3(o[:, :], T), ALU.max).then_inc(free_of("den"), 1)
            moved(dve, "den")
            moved(dve, "ml_o")
            v.scalar_tensor_tensor(den, mlo, 1.0, den, ALU.add, ALU.mult).then_inc(S["ml_den"], 1)
            dve.wait_ge(S["ml_den"], 2)
            v.reciprocal(den, den).then_inc(S["ml_den"], 1)
            dve.wait_ge(S["ml_den"], 3)
            o = wait_full(dve, "num")
            v.tensor_tensor(yT[:, 2:4, :], v3(o[:, :], T), den, ALU.mult).then_inc(free_of("num"), 1)
            level_update(6)

            def solve_rhs(c):
                o = wait_full(dve, f"R{c}")
                v.tensor_scalar(R_, o[:, 0:GW], -1.0, None, ALU.mult).then_inc(free_of(f"R{c}"), 1)

            def solution(c):
                o = wait_full(dve, f"U{c}")
                v.tensor_copy(U[:, c, :], o[:, 0:GW]).then_inc(free_of(f"U{c}"), 1)

            def mb_biased(h):
                o = wait_full(dve, f"sc{h}")
                dve.wait_ge(S["rel_in"], 16)
                v.scalar_tensor_tensor(Sm[:, h, 0:P], o[:, 0:P], HD ** -0.5, Bz[:, h, P:T], ALU.mult, ALU.add)
                v.scalar_tensor_tensor(Sm[:, h, P:P + T], o[:, P:P + T], HD ** -0.5, Bz[:, h, :], ALU.mult,
                                       ALU.add).then_inc(free_of(f"sc{h}"), 1)

            solve_rhs(0)
            mb_biased(0)
            mb_biased(1)
            solution(0)
            mb_biased(2)
            mb_biased(3)
            for h in range(NH):
                moved(dve, f"sc{h}")
            v.tensor_reduce(nmax[:, 0:4], Sm[:, :, 0:P], AX.X, ALU.max, negate=True)
            v.tensor_reduce(nmax[:, 4:8], Sm[:, :, P:P + T], AX.X, ALU.max, negate=True).then_inc(S["mb_max"], 1)
            o = wait_full(dve, "S0")
            dve.wait_ge(S["zeros_ready"], 3)
            for h in range(NH):
                r, j = at(h)
                last = v.tensor_scalar(S0[r, j, h % 2, :], o[r, j * HD:(j + 1) * HD], carry[r, j:j + 1], None, ALU.mult)
            last.then_inc(free_of("S0"), 1)
            solve_rhs(1)
            solution(1)
            scan(3)
            dve.wait_ge(S["mb_exp"], 1)
            v.reciprocal(mb_sum, mb_sum).then_inc(S["mb_inv"], 1)
            o = wait_full(dve, "rw_y")
            v.tensor_copy(Yrw, v3(o[:, :], T)).then_inc(free_of("rw_y"), 1)
            dve.wait_ge(S["mb_inv"], 1)
            v.tensor_tensor(Sm[:, :, 0:P], Sm[:, :, 0:P], spread(mb_sum[:, 0:4], P), ALU.mult)
            v.tensor_tensor(Sm[:, :, P:P + T], Sm[:, :, P:P + T], spread(mb_sum[:, 4:8], T), ALU.mult).then_inc(S["mb_prob"], 1)
            o = wait_full(dve, "mean")
            moved(dve, "rw_y")
            v.scalar_tensor_tensor(flat(Yrw), o[:, :], -1.0 / HD, flat(Yrw), ALU.mult, ALU.add).then_inc(free_of("mean"), 1)
            moved(dve, "mean")
            o = v3(wait_full(dve, "s5_y")[:, :], T)
            for j in range(2):
                last = v.scalar_tensor_tensor(z5y[:, j, :], s5u[:, j, :], prm("s5_d")[:, j:j + 1], o[:, j, :],
                                              ALU.mult, ALU.add)
            last.then_inc(free_of("s5_y"), 1)
            moved(dve, "s5_y")
            v.tensor_tensor(z5a, z5y, z5y, ALU.mult).then_inc(S["s5_step2"], 1)
            dve.wait_ge(S["s5_step2"], 1)
            v.tensor_scalar(z5a, z5a, 0.044715, 1.0, ALU.mult, ALU.add).then_inc(S["s5_step2"], 1)
            dve.wait_ge(S["s5_step2"], 2)
            v.tensor_tensor(z5a, z5a, z5y, ALU.mult).then_inc(S["s5_arg"], 1)
            dve.wait_ge(S["rw_rstd"], 1)
            v.tensor_tensor(flat(Yrw), flat(Yrw), Pm_[:, 0:512], ALU.mult).then_inc(S["rw_tail"], 1)
            o = v3(wait_full(dve, "bonus")[:, :], T)
            v.tensor_tensor(Ysq, o, rwM[:, 6:8, :], ALU.mult).then_inc(free_of("bonus"), 1)
            dve.wait_ge(S["rw_tail"], 1)
            for j in range(2):
                last = v.tensor_scalar(Yrw[:, j, :], Yrw[:, j, :], prm("ln_w")[:, j:j + 1], prm("ln_b")[:, j:j + 1],
                                       ALU.mult, ALU.add)
            last.then_inc(S["rw_tail"], 1)
            moved(dve, "bonus")
            dve.wait_ge(S["rw_tail"], 2)
            v.tensor_tensor(Yrw, Yrw, Ysq, ALU.add).then_inc(S["rw_tail"], 1)
            dve.wait_ge(S["rw_tail"], 3)
            moved(dve, "rw_g")
            v.tensor_tensor(yT[:, 4:6, :], Yrw, rwg, ALU.mult).then_inc(S["rw_out"], 1)
            dve.wait_ge(S["s5_exp"], 1)
            sigmoid_of_exp(z5b, "s5_sig", 0).then_inc(S["s5_sig"], 1)
            dve.wait_ge(S["s5_sig"], 2)
            v.tensor_tensor(z5, z5y, z5b, ALU.mult).then_inc(S["s5_z"], 1)
            o = wait_full(dve, "mb_o")
            v.tensor_copy(yT[:, 6:8, :], v3(o[:, :], T)).then_inc(free_of("mb_o"), 1)

            split = [0]

            def rests(upto):
                while split[0] < min(upto, NHALF):
                    rest(dve, v, split[0])
                    split[0] += 2

            def y_rest(turn, g_):
                dve.wait_ge(S["high_ready"], HIGHS["y"] + turn + 1)
                tiles = slice(2 * g_, 2 * g_ + 2)
                v.tensor_tensor(y_split[1][:, tiles, :], yT[:, tiles, :], y_split[0][:, tiles, :].bitcast(F32),
                                ALU.subtract).then_inc(S["y_rest"], 1)

            rests(4)

            def group_gain(g_, name):
                dve.wait_ge(S[name + "_root"], 1)
                for j in range(2):
                    k = 2 * g_ + j
                    last = v.scalar_tensor_tensor(yT[:, k, :], yT[:, k, :], prm("mix_gain")[:, k:k + 1],
                                                  gn_sq[g_][:, 0, :], ALU.mult, ALU.mult)
                last.then_inc(S["gn_done"], 1)

            group_gain(1, "ml")
            moved(dve, "glu")
            sigmoid_of_exp(z5b, "s5_sig", 2).then_inc(S["s5_sig"], 1)
            dve.wait_ge(S["s5_sig"], 4)
            v.tensor_tensor(yT[:, 0:2, :], z5, z5b, ALU.mult).then_inc(S["s5_out"], 1)
            group_gain(3, "mb")
            group_gain(2, "rw")
            y_rest(0, 1)
            y_rest(1, 3)
            group_gain(0, "s5")
            y_rest(2, 2)
            y_rest(3, 0)
            rests(11)

            def post_norm(n, pieces, parts):
                dve.wait_ge(S["post_ssq"], 3 * n + 1)
                v.tensor_reduce(rst, v3(ssq, 4)[:, :, 0:parts], AX.X, ALU.add).then_inc(S["post_sum"], 1)
                dve.wait_ge(S["post_ssq"], 3 * n + 3)
                dve.wait_ge(S["gain_in"], 16 * (n + 1))
                for name, src, m, part in pieces:
                    w = src[1] - src[0]
                    o = wait_full(dve, name)
                    e = v.scalar_tensor_tensor(xtmp[:, m, part * w:(part + 1) * w], o[:, src[0]:src[1]], rst[:, m:m + 1],
                                               gain_[:, part * w:(part + 1) * w], ALU.mult, ALU.mult)
                    if parts == 2 or m == 1:
                        e.then_inc(free_of(name), 1)
                moved(dve, pieces[-1][0])
                if n == 0:
                    dve.wait_ge(S["xres_in"], 16)
                for m in range(2):
                    v.tensor_tensor(xres[:, m, :], xres[:, m, :], xtmp[:, m, :], ALU.add).then_inc(S["x_new"], 1)

            def pre_norm(n):
                dve.wait_ge(S["pre_ssq"], 3 * n + 3)
                for m in range(2):
                    last = v.tensor_scalar(xtmp[:, m, :], xres[:, m, :], rst[:, m:m + 1], None, ALU.mult)
                last.then_inc(S["xn_ready"], 1)

            def rest_of_bank(tag, i, out, high, scale=None):
                o = v3(wait_full(dve, f"{tag}{i}")[:, :], T)
                dve.wait_ge(S["high_ready"], HIGHS[tag.replace("xo", "ox")] + i + 1)
                for k in range(2):
                    c = 2 * i + k
                    if scale is None:
                        e = v.tensor_tensor(out[:, c, :], o[:, k, :], high[:, c, :].bitcast(F32), ALU.subtract)
                    else:
                        e = v.scalar_tensor_tensor(out[:, c, :], o[:, k, :], scale[:, c:c + 1],
                                                   high[:, c, :].bitcast(F32), ALU.mult, ALU.subtract)
                e.then_inc(free_of(f"{tag}{i}"), 1)

            post_norm(0, [(f"wout{i}", (256 * m, 256 * m + 256), m, i) for i in range(4) for m in range(2)], 4)
            pre_norm(0)
            for i in range(4):
                rest_of_bank("xat", i, h_split[1], h_split[0], prm("pre_xa"))
            rests(20)
            for h in range(XH):
                o = v3(wait_full(dve, f"xs{h}")[:, :], NMEM)
                mx = xmax[:, 2 * h:2 * h + 2]
                v.tensor_reduce(mx, o, AX.X, ALU.max, negate=True).then_inc(S["x_max"], 1)
                dve.wait_ge(S["x_max"], 2 * h + 1)
                v.tensor_scalar(mx, mx, XD ** -0.5, None, ALU.mult).then_inc(S["x_max"], 1)
            for h in range(XH):
                moved(dve, f"xs{h}")
                sm = xsum[:, 2 * h:2 * h + 2]
                v.reciprocal(sm, sm).then_inc(S["x_inv"], 1)
                dve.wait_ge(S["x_inv"], h + 1)
                v.tensor_tensor(px[:, h], px[:, h], spread(sm, NMEM), ALU.mult).then_inc(S["x_prob"], 1)
            for h in range(XH):
                rest_of_bank("xo", h, ox_split[1], ox_split[0])
            first = 2 * (S_FIN - S_SPLIT)
            rests(first + 3)
            post_norm(1, [(f"wo{i}", (256 * m, 256 * m + 256), m, i) for i in range(4) for m in range(2)], 4)
            pre_norm(1)
            for i in range(4):
                rest_of_bank("fft", i, h_split[1], h_split[0], prm("pre_ffn"))
            rests(first + 4)

            def act_rest(p):
                dve.wait_ge(S["high_ready"], HIGHS["act"] + p + 1)
                part = [flat(x[:, 2 * p:2 * p + 2, :]) for x in act_split]
                v.tensor_tensor(part[1], fft[:, p % 2, :], part[0].bitcast(F32), ALU.subtract).then_inc(S["act_rest"], 1)

            for p in range(NFF // 2):
                rests(first + 4 * p + 6)
                f = fft[:, p % 2, :]
                dve.wait_ge(S["f_exp"], p + 1)
                sigmoid_of_exp(f, "f_sig", 2 * p).then_inc(S["f_sig"], 1)
                dve.wait_ge(S["f_sig"], 2 * p + 2)
                o = wait_full(dve, f"g{p}")
                v.tensor_tensor(f, f, o[:, :], ALU.mult).then_inc(free_of(f"g{p}"), 1)
                if p > 0:
                    act_rest(p - 1)
                rests(first + 4 * p + 8)
                moved(dve, f"g{p}")
                o = wait_full(dve, f"u{p}")
                v.tensor_tensor(f, f, o[:, :], ALU.mult).then_inc(free_of(f"u{p}"), 1)
            act_rest(NFF // 2 - 1)
            rests(NHALF)
            post_norm(2, [(f"y{2 * m + i}", (0, 512), m, i) for m in range(2) for i in range(2)], 2)


def _constants():
    import numpy as np

    c = np.zeros((P, NCONST), np.float32)

    def put(name, a):
        c[:a.shape[0], CONST[name][0]:CONST[name][0] + a.shape[1]] = a

    i = np.arange(P)
    put("ident", np.eye(P))
    put("ones", np.ones((P, P)))
    put("pair_ones", (i[:, None] // HD == i[None, :] // HD) * 1.0)
    put("strict", (i[:, None] < i[None, :]) * 1.0)
    put("incl", (i[:, None] <= i[None, :]) * 1.0)
    diag = np.where(i[:, None] <= i[None, :], 0.0, NEG)
    put("causal_add", np.concatenate([diag, np.zeros((P, P)), diag], axis=1))
    levels = []
    for n in range(LEVELS):
        b = 1 << n
        levels.append(((i[:, None] // (2 * b) == i[None, :] // (2 * b)) & (i[:, None] // b % 2 == 0)
                       & (i[None, :] // b % 2 == 1)) * 1.0)
    put("levels", np.concatenate(levels, axis=1))
    put("level0_t", levels[0].T)
    put("time", np.tile(np.arange(T), (P, 1)))
    put("head_sel", np.repeat(np.eye(NH), P, axis=1))
    put("pair_sel", np.repeat(np.eye(NH), HD, axis=1))
    rel = T - 1 - np.arange(384)
    n = np.maximum(rel, 0)
    large = 16 + (np.log(np.maximum(n, 1).astype(np.float32) / 16) / math.log(128 / 16) * 16).astype(np.int32)
    bucket = np.where(n < 16, n, np.minimum(large, 31))
    hot = np.zeros((33, 384))
    hot[bucket, np.arange(384)] = rel >= 0
    hot[32] = np.where(rel < 0, NEG, 0.0)
    put("onehot", hot)
    for name, value in (("eps6", 1e-6), ("eps12", 1e-12), ("eps_gn", 64e-5), ("half_pi", math.pi / 2)):
        put(name, np.full((P, 1), value))
    return c


def _parameters(a):
    import numpy as np

    p = np.zeros((P, NPARAM), np.float32)

    def put(name, block, at=0):
        lo = PARAM[name][0] + at
        p[:block.shape[0], lo:lo + block.shape[1]] = block

    def channels(v):
        return v.reshape(-1, P).T

    mu = a["rw_mu"][0]
    put("mu", channels(np.concatenate([mu[768:1024], mu[256:512], mu[0:256], mu[512:768]])))
    for name, src in (("w0", "rw_w0"), ("a0", "rw_a0"), ("k_k", "rw_k_k"), ("k_a", "rw_k_a"), ("r_k", "rw_r_k"),
                      ("ln_w", "rw_ln_w"), ("ln_b", "rw_ln_b"), ("s5_d", "s5_d"), ("b_glu", "s5_b_glu"),
                      ("mix_gain", "mix_out_gain"), ("pre_mix", "norm_pre_mix"), ("pre_xa", "norm_pre_xa"),
                      ("pre_ffn", "norm_pre_ffn"), ("norm_mem", "norm_mem"), ("lam_re", "s5_lam_re"),
                      ("lam_im", "s5_lam_im")):
        put(name, channels(a[src][0]))
    put("conv", a["ml_conv"][0].reshape(4, 4, P).transpose(2, 1, 0).reshape(P, 16))
    put("log_step", channels(np.repeat(a["s5_log_step"][0], 64)))
    put("i_bias", a["ml_i_bias"][0].reshape(NH, 1))
    put("f_bias", a["ml_f_bias"][0].reshape(NH, 1))
    put("rel", a["rel_bias"])
    p[32, PARAM["rel"][0]:PARAM["rel"][1]] = 1.0
    gate = a["w_in"][0][:, 1280:1288]
    put("w_gate", gate.reshape(KD, P, 8).transpose(1, 0, 2).reshape(P, KD * 8))
    put("w2a2", np.concatenate([a["rw_w2"][0], a["rw_a2"][0]], axis=0))
    put("g2", a["rw_g2"][0])
    put("w_glu", a["s5_w_glu"][0].reshape(2, P, GW).transpose(1, 0, 2).reshape(P, 2 * GW))
    for name, src in (("b_re", "s5_b_re"), ("b_im", "s5_b_im")):
        b = np.zeros((4, 2, 16, 2, 2, 64), np.float32)
        w = a[src][0].reshape(2, 4, 2, 64, 16)
        for g in range(2):
            b[:, g, :, :, g, :] = w[:, :, g].transpose(1, 3, 0, 2)
        put(name, b.reshape(P, 256))
    for name, src in (("c_re", "s5_c_re"), ("c_im", "s5_c_im")):
        c = np.zeros((2, 64, 8, 2, 16), np.float32)
        w = a[src][0].reshape(8, 2, 16, 64)
        for g in range(2):
            c[g, :, :, g, :] = w[:, g].transpose(2, 0, 1)
        put(name, c.reshape(P, 256))
    return p


def _weight_slots(a):
    import numpy as np

    def columns_of(w):
        n = w.shape[1] // 256
        return w.reshape(KD, P, n, 256).transpose(2, 1, 0, 3).reshape(n, P, SLOT)

    w = a["w_in"][0]
    ml, rw, mb = GW, GW + 4 * GW + 8, GW + 4 * GW + 8 + 1024
    first = {"rw_wag": rw + 768, "rw_k": rw + 256, "rw_r": rw, "rw_v": rw + 512, "s5_u": 0, "ml_q": ml,
             "ml_k": ml + 256, "ml_v": ml + 512, "ml_o": ml + 768, "mb_q": mb, "mb_k": mb + 256, "mb_v": mb + 512}
    parts = [columns_of(w[:, first[n]:first[n] + 256]) for n in W_IN_ORDER]

    def halves_of(w, order):
        w = w.reshape(KD, P, 4, 256)[order].reshape(2, 4, P, 4, 256)
        halves = w.transpose(0, 3, 2, 1, 4).reshape(4, 2, P, HALF)
        return halves.transpose(0, 2, 1, 3).reshape(4, P, SLOT)

    parts += [columns_of(a["xa_wkv"][0]), halves_of(a["w_out"][0], Y_ORDER), columns_of(a["xa_wq"][0]),
              halves_of(a["xa_wo"][0], list(range(KD)))]
    gu = columns_of(a["ffn_w_in"][0])
    half = NFF // 2
    parts.append(np.stack([gu[:half], gu[half:]], axis=1).reshape(2 * half, P, SLOT))
    parts.append(a["ffn_w_out"][0].reshape(half, 2, P, D).transpose(0, 2, 1, 3).reshape(half, P, SLOT))
    return np.concatenate(parts, axis=0)


def kernel(**inputs):
    import numpy as np
    import concourse.bacc as bacc
    from concourse.bass_utils import run_bass_kernel_spmd

    a = {name: np.asarray(value) for name, value in inputs.items()}
    arrays = {
        "x_t": a["x"][0].T.reshape(KD, P, T).transpose(1, 0, 2).reshape(P, KD * T),
        "x_rows": a["x"][0],
        "mem_t": a["mem"][0].T.reshape(KD, P, NMEM).transpose(1, 0, 2).reshape(P, KD * NMEM),
        "consts": _constants(),
        "params": _parameters(a),
        "weights": _weight_slots(a),
        "gains": np.concatenate([a["norm_post_mix"], a["norm_post_xa"], a["norm_post_ffn"]], axis=0),
    }
    arrays = {name: np.ascontiguousarray(v) for name, v in arrays.items()}
    nc = bacc.Bacc("TRN2", target_bir_lowering=False, num_devices=1)
    aps = {name: nc.dram_tensor(name, v.shape, F32, kind="ExternalInput").ap() for name, v in arrays.items()}
    rel_scratch = nc.dram_tensor("rel_scratch", (P, NH * 384), F32)
    out = nc.dram_tensor("out", (1, T, D), F32, kind="ExternalOutput").ap()
    trunk_kernel(nc, aps["x_t"], aps["x_rows"], aps["mem_t"], aps["consts"], aps["params"], aps["weights"],
                 aps["gains"], rel_scratch, out)
    r = run_bass_kernel_spmd(nc, [arrays], core_ids=[0])
    return r.results[0]["out"]
```

```python
import concourse.bass as bass
from concourse import mybir
from contextlib import ExitStack
import math

F32 = mybir.dt.float32
F32R = mybir.dt.float32r
ALU = mybir.AluOpType
ACT = mybir.ActivationFunctionType
AX = mybir.AxisListType

P = 128
D = 1024
T = 256
NMEM = 256
KD = D // P
GW = 256
HD = 64
NH = GW // HD
C = 128
NC = T // C
DFF = 2816
NFF = DFF // P
XH, XD = 4, 256
NEG = -1e30
DECAY = math.exp(-0.5)
TAU = 6.2831850
ROUND = 12582912.0
GELU = 2.0 * math.sqrt(2.0 / math.pi)
LEVELS = 7


def columns(sizes):
    at, out = 0, {}
    for name, n in sizes:
        out[name] = (at, at + n)
        at += n
    return out, at


CONST, NCONST = columns([
    ("ones", P), ("eps6", 1), ("eps12", 1), ("eps_gn", 1), ("half_pi", 1), ("ident", P), ("pair_ones", P), ("strict", P), ("incl", P), ("causal_add", 384),
    ("levels", LEVELS * P), ("level0_t", P), ("time", T), ("head_sel", NH * P), ("pair_sel", 2 * P),
    ("onehot", 384),
])
CONST_FIRST = CONST["ident"][0]
PARAM, NPARAM = columns([
    ("mu", 8), ("w0", 2), ("a0", 2), ("k_k", 2), ("k_a", 2), ("r_k", 2), ("ln_w", 2), ("ln_b", 2),
    ("s5_d", 2), ("b_glu", 2), ("mix_gain", 8), ("conv", 16), ("pre_mix", 8), ("pre_xa", 8),
    ("pre_ffn", 8), ("norm_mem", 8), ("lam_re", 8), ("lam_im", 8), ("log_step", 8), ("i_bias", 1),
    ("f_bias", 1), ("rel", 4), ("w_gate", KD * 8), ("w2a2", GW), ("g2", GW), ("w_glu", 2 * GW),
    ("b_re", GW), ("b_im", GW), ("c_re", GW), ("c_im", GW),
])
PARAM_FIRST = PARAM["w_gate"][0]

W_IN_ORDER = ["rw_wag", "rw_k", "rw_r", "rw_v", "s5_u", "ml_q", "ml_k", "ml_v", "ml_o", "mb_q", "mb_k", "mb_v"]
SLOT = 2048
N_WIN, N_WKV, N_WOUT, N_WQ, N_WO = 12, 8, 4, 4, 4
N_FIN, N_FOUT = 2 * NFF // 2, NFF // 2
S_WKV = N_WIN
S_WOUT = S_WKV + N_WKV
S_WQ = S_WOUT + N_WOUT
S_WO = S_WQ + N_WQ
S_FIN = S_WO + N_WO
S_FOUT = S_FIN + N_FIN
NSLOTS = S_FOUT + N_FOUT
EARLY_RING, RING = 2, 3
HALF = SLOT // 2
NHALF = 2 * NSLOTS
H_MID = 2 * W_IN_ORDER.index("mb_q")
H_WKV, H_LATE = 2 * S_WKV, 2 * S_WOUT
HALF_BUFS, MID_BUFS = 4, 2
Y_ORDER = [2, 3, 6, 7, 4, 5, 0, 1]


def trunk_kernel(nc, x_t, x_rows, mem_t, consts_d, params_d, weights_d, gains_d, rel_scratch, out):
    ctx = ExitStack()
    with ctx:
        def sb(name, n):
            return ctx.enter_context(nc.sbuf_tensor(name, [P, n], F32))

        def v3(ap, n):
            return ap.rearrange("p (a b) -> p a b", b=n)

        def flat(ap):
            return ap.rearrange("p a b -> p (a b)")

        def v4(ap, m, n):
            return ap.rearrange("p (a b c) -> p a b c", b=m, c=n)

        def copies(ap, n):
            return ap.unsqueeze(1).to_broadcast([ap.shape[0], n, ap.shape[1]])

        def spread(ap, n):
            return ap.unsqueeze(2).to_broadcast([ap.shape[0], ap.shape[1], n])

        cst = sb("cst", NCONST)
        par = sb("par", NPARAM)
        with ExitStack() as stage:
            w_kx = [v3(stage.enter_context(nc.sbuf_tensor(name, [P, HALF], F32R))[:, :], 256)
                    for name in ("wk_high", "wk_rest")]
        kx = v3(sb("kx", KD * NMEM)[:, :], NMEM)
        vx = v3(sb("vx", 2 * D)[:, :], D)
        ring = sb("ring", EARLY_RING * SLOT)
        small = sb("small", 160)
        ARENA = 33000
        with ExitStack() as early:
            _, arena = (early.enter_context(nc.sbuf_tensor(name, [P, n], F32))
                        for name, n in (("below", 2 * KD * T + SLOT), ("arena", ARENA)))
        hT, mem_h = kx, v3(flat(vx), NMEM)
        bank = [ctx.enter_context(nc.psum_tensor(f"bank{i}", [P, 512], F32)) for i in range(8)]

        def const(name, rows=P):
            a, b = CONST[name]
            return cst[0:rows, a:b]

        def prm(name, rows=P):
            a, b = PARAM[name]
            return par[0:rows, a:b]

        def gain_rows(n):
            return bass.AP(gains_d.tensor, n * D, [[0, P], [1, D]])

        def carve(at, sizes):
            views = []
            for n in sizes:
                views.append(arena[:, at:at + n])
                at += n
            assert at <= ARENA, at
            return views, at

        (yT_, rwP_, rwM_, rwE_, KR_, Bh_, Kh_), at = carve(0, [8 * T, 8 * 257, 8 * T, 3 * 512, 1024, 512, 512])
        yT = v3(yT_, T)
        rwP = v3(rwP_, 257)
        rwM = v3(rwM_, T)
        kk, ab, G, Gp = (v3(rwP_[:, 512 * i:512 * i + 512], T) for i in range(4))
        rwE = rwE_.rearrange("p (e j t) -> p e j t", e=3, t=T)
        KR = KR_.rearrange("p (e j t) -> p e j t", e=2, t=T)
        Bh, Kh = v3(Bh_, T), v3(Kh_, T)
        rwg, bon = rwM[:, 0:2, :], rwM[:, 4:6, :]
        A_AT = at
        (A_, X_, XT_, Pm_, Mj_), at = carve(at, [4096, 1024, 1024, 1024, 1024])
        A = v3(A_, 512)
        X, XT, Pm, Mj = (a.rearrange("p (c h t) -> p c h t", c=NC, t=P) for a in (X_, XT_, Pm_, Mj_))
        (Vt_, BKt_, R_, U_, S0_), at = carve(at, [512, 512, 256, 512, 256])
        Vt, BKt, U, S0 = v3(Vt_, 256), v3(BKt_, 256), v3(U_, 256), v4(S0_, 2, HD)
        (cos_, sin_, bu_, t1_, t2_, pr_, s5u_), at = carve(at, [2048, 2048, 1024, 512, 512, 2048, 512])
        sq_x, sq_m = v3(pr_, T), v3(arena[:, at - 512 - 2048 - 2048:at - 512 - 2048], T)
        cos, sin, t1, t2, s5u = (v3(a, T) for a in (cos_, sin_, t1_, t2_, s5u_))
        bu, pr = v4(bu_, 2, T), v4(pr_, 2, T)
        (raw_cv, E_, c2n_), at = carve(at, [4 * 259 + 1024, 4 * 384, 256])
        raw, cv = v3(raw_cv[:, 0:1036], 259), v3(raw_cv[:, 1036:2060], T)
        mlo, mlv = v3(G.rearrange("p a b -> p (a b)"), T), v3(Gp.rearrange("p a b -> p (a b)"), 256)
        E = v3(E_, 384)
        rows = [yT[:, i, :] for i in (4, 5, 6, 7, 1)]
        c_re, c_im, c_nre = v3(prm("c_re"), 32), v3(prm("c_im"), 32), v3(c2n_, 32)
        mqk, mbv = v3(rwE_[:, 0:1024], T), v3(rwE_[:, 1024:1536], 256)
        Bz = v3(rwP_[:, 0:1024], T)
        Sm, PTm = E, v3(raw_cv[:, 0:1536], 384)

        Yrw, Ysq = v3(Mj_[:, 0:512], T), v3(Mj_[:, 512:1024], T)
        z5y, z5a, z5, z5b = v3(bu_[:, 0:512], T), v3(bu_[:, 512:1024], T), t1, t2
        gn_sq = [v3(pr_[:, 0:512], T), Bh, rwM[:, 2:4, :], Kh]
        rstd_x, rstd_m = s5u_[:, 0:T], yT_[:, 0:T]

        def pair(stack, name, n, width):
            return [v3(stack.enter_context(nc.sbuf_tensor(name + part, [P, n], F32R))[:, :], width)
                    for part in ("_high", "_rest")]

        def own(stack, name, n):
            return stack.enter_context(nc.sbuf_tensor(name, [P, n], F32))[:, :]

        h_split = pair(ctx, "h", KD * T, T)
        w_mid = [pair(ctx, "wm", HALF, 256)]
        w_mb = [w_mid[0], w_kx]
        with ExitStack() as stage:
            own(stage, "gap", A_AT)
            w_early = [pair(stage, f"we{i}", HALF, 256) for i in range(HALF_BUFS)]
        xtmp = v3(own(ctx, "xtmp", 2 * D), D)
        xres = v3(own(ctx, "xres", 2 * D), D)
        gain_ = own(ctx, "gain", D)
        px_ = own(ctx, "px", XH * 2 * NMEM)
        px = px_.rearrange("p (h t m) -> p h t m", t=2, m=NMEM)
        qx = v3(own(ctx, "qx", KD * T), T)
        own(ctx, "gap0", A_AT - 7 * D - 2 * D)
        w_late = [pair(ctx, f"w{i}", HALF, 256) for i in range(2)]
        with ExitStack() as stage:
            y_high = v3(stage.enter_context(nc.sbuf_tensor("y_high", [P, 8 * T], F32R))[:, :], T)
            ptx = own(stage, "ptx", XH * 2 * T).rearrange("p (h m t) -> p h m t", m=2, t=T)
            y_rest = v3(stage.enter_context(nc.sbuf_tensor("y_rest", [P, 8 * T], F32R))[:, :], T)
            y_split = [y_high, y_rest]
        act_high = v3(ctx.enter_context(nc.sbuf_tensor("act_high", [P, NFF * T], F32R))[:, :], T)
        own(ctx, "gap1", 3 * 8 * T - NFF * T)
        w_late += [pair(ctx, f"w{i}", HALF, 256) for i in range(2, HALF_BUFS)]
        with ExitStack() as stage:
            ox_split = pair(stage, "ox", KD * T, T)
        w_mid.append([w_late[2][0], w_late[3][0]])
        act_rest = v3(ctx.enter_context(nc.sbuf_tensor("act_rest", [P, NFF * T], F32R))[:, :], T)
        act_split = [act_high, act_rest]
        fft = v3(own(ctx, "fft", 1024), 512)
        third_slot = own(ctx, "third_slot", SLOT)

        taken = [0]

        def cols(n):
            taken[0] += n
            assert taken[0] <= 160
            return small[:, taken[0] - n:taken[0]]

        neg_w0a0, neg_bglu, one_ka = cols(4), cols(2), cols(2)
        mid, carry = cols(4), cols(2)
        step, mag, frac, frn, co_re, co_im, den8, s8a, s8b, s8c = (cols(8) for _ in range(10))
        gcol = cols(8)
        nmax, mb_sum = cols(8), cols(8)
        ssq, rst = cols(8), cols(2)
        xmax, xsum = cols(8), cols(8)

        S = {name: ctx.enter_context(nc.semaphore(name)) for name in """
            rotated_back s5_out_used rw_level_mask rw_x0 rw_xt0 ml_qk mb_prob consts_in params_in
            sq_ready h_ready sq_m_ready rw_lowrank rw_kx_sq rw_mix rw_tilde ml_rows mem_ready ml_em
            rw_bonus rw_ysq s5_z gn_done xn_ready x_prob first_in xres_in gain_in rel_stored
            rel_in x_new out_stored zeros_ready s5_co s5_c rotating scanned sincos x_in mem_in
            rstd_x s5_step s5_decay theta rstd_m rw_exp neg_ready rw_inv rw_G rw_kk rw_E ml_gate
            ml_log ml_conv ml_silu ml_E mb_max mb_exp rw_rstd s5_arg s5_exp rw_out s5_out post_sq post_root
            post_sum pre_root x_max f_exp rw_diff rw_low rw_kx rw_G0 rw_a rw_k2 s5_co_step
            ml_row_step ml_sig ml_den mb_inv s5_step2 rw_tail s5_sig x_inv f_sig s5_sq s5_root ml_sq
            ml_root rw_sq rw_root mb_sq mb_root
            w_high w_rest_even w_rest_odd w_rest_mid w_used high_ready act_rest y_rest h_high h_rest x_summed
            mem_summed
            """.split()}
        loaded = [ctx.enter_context(nc.semaphore(f"slot_loaded{i}")) for i in range(RING)]
        full = [ctx.enter_context(nc.semaphore(f"bank_full{i}")) for i in range(8)]
        free = [ctx.enter_context(nc.semaphore(f"bank_free{i}")) for i in range(8)]

        uses, count = {}, [0] * 8

        def pe_open(pe, name, b):
            uses[name] = (b, count[b])
            if count[b] > 0:
                pe.wait_ge(free[b], count[b])
            count[b] += 1
            return bank[b]

        def wait_full(eng, name):
            b, n = uses[name]
            eng.wait_ge(full[b], n + 1)
            return bank[b]

        def moved(eng, name):
            b, n = uses[name]
            eng.wait_ge(free[b], n + 1)

        def free_of(name):
            return free[uses[name][0]]

        def place(n):
            return n % EARLY_RING if n < S_WOUT else (n - S_WOUT) % RING

        def slot(n):
            i = place(n)
            return ring[:, i * SLOT:(i + 1) * SLOT] if i < EARLY_RING else third_slot

        def wait_slot(eng, n):
            eng.wait_ge(loaded[place(n)], 16 * sum(place(m) == place(n) for m in range(n + 1)))
            return slot(n)

        half_user = {}

        def split_half(i):
            if i < H_MID:
                return w_early[i % HALF_BUFS]
            if i < H_WKV:
                return w_mb[i % MID_BUFS]
            return w_mid[i % MID_BUFS] if i < H_LATE else w_late[(i - H_LATE) % HALF_BUFS]

        def raw_half(i):
            at = i % 2 * HALF
            return v3(slot(i // 2)[:, at:at + HALF], 256)

        def rest_done(i):
            if H_MID <= i < H_LATE:
                return S["w_rest_mid"], i - H_MID + 1
            return S[("w_rest_even", "w_rest_odd")[i % 2]], (i if i < H_MID else i - H_LATE + H_MID) // 2 + 1

        def wait_rest(eng, i):
            eng.wait_ge(*rest_done(i))

        HIGHS = {"y": 0, "xat": 4, "ox": 8, "fft": 12, "act": 16}

        def high_part(act, i):
            if i % 2 == 0:
                wait_slot(act, i // 2)
            start, bufs = (0, HALF_BUFS) if i < H_MID else (H_MID, MID_BUFS) if i < H_LATE else (H_LATE, HALF_BUFS)
            if i >= start + bufs:
                user = half_user[i - bufs]
                if isinstance(user, str):
                    wait_full(act, user)
                else:
                    act.wait_ge(S["w_used"], user)
            nc.scalar.activation(split_half(i)[0], raw_half(i), ACT.Copy).then_inc(S["w_high"], 1)

        def rest(eng, e, i):
            eng.wait_ge(S["w_high"], i + 1)
            high, rest_ = split_half(i)
            e.tensor_tensor(rest_, raw_half(i), high.bitcast(F32), ALU.subtract).then_inc(rest_done(i)[0], 1)

        def at(h):
            return slice(HD * (h % 2), HD * (h % 2) + HD), h // 2

        def sum_tiles(eng, e, sq, name, steps=0):
            for step in range(3):
                n = 4 >> step
                if step > 0:
                    eng.wait_ge(S[name], steps + step)
                e.tensor_tensor(sq[:, 0:n, :], sq[:, 0:n, :], sq[:, n:2 * n, :], ALU.add).then_inc(S[name], 1)

        block = ctx.enter_context(nc.Block())

        @block.tensor
        def _(pe):
            def mm(out_, lhsT, rhs, start=True, stop=True):
                return nc.tensor.matmul(out_, lhsT, rhs, start=start, stop=stop, skip_group_check=True)

            def mm3(out_, lhs, rhs, start, stop):
                mm(out_, lhs[0], rhs[0], start, False)
                mm(out_, lhs[0], rhs[1], False, False)
                return mm(out_, lhs[1], rhs[0], False, stop)

            def used(last, i, name=None):
                if name:
                    last.then_inc(full[uses[name][0]], 1)
                    half_user[i] = name
                else:
                    last.then_inc(S["w_used"], 1)
                    half_user[i] = sum(not isinstance(u, str) for u in half_user.values()) + 1

            def split_channel_major(n, name, b, act, arrive=None):
                o = v3(pe_open(pe, name, b)[:, :], T)
                for j in range(2):
                    i = 2 * n + j
                    wait_rest(pe, i)
                    if arrive:
                        arrive(j)
                    w = split_half(i)
                    for c in range(2):
                        for k in range(4):
                            last = mm3(o[:, c, :], [x[:, k, c * P:(c + 1) * P] for x in w],
                                       [x[:, 4 * j + k, :] for x in act], c + j + k == 0, 4 * j + k == KD - 1)
                    used(last, i, name if j else None)

            def split_values(n, name, b, act):
                o = v3(pe_open(pe, name, b)[:, :], 256)
                for j in range(2):
                    i = 2 * n + j
                    wait_rest(pe, i)
                    for m in range(2):
                        for k in range(4):
                            kt = 4 * j + k
                            last = mm3(o[:, m, :], [x[:, kt, m * P:(m + 1) * P] for x in act],
                                       [x[:, k, :] for x in split_half(i)], m + kt == 0, kt == KD - 1)
                    used(last, i, name if j else None)

            def split_token_major(n, q, name, b, act, order):
                o = v3((pe_open(pe, name, b) if q < 4 else bank[b])[:, :], 256)
                i = 2 * n + q
                wait_rest(pe, i)
                for m in range(2):
                    for k in range(4):
                        kt = 4 * (q // 4) + k
                        last = mm3(o[:, m, :], [x[:, order[kt], m * P:(m + 1) * P] for x in act],
                                   [x[:, k, :] for x in split_half(i)], m + kt == 0, kt == KD - 1)
                used(last, i, name if q >= 4 else None)

            def mem_arrives(j):
                pe.wait_ge(S["h_rest"], 3 + j)

            def wkv(i, b):
                if i < 4:
                    split_channel_major(S_WKV + i, f"wkv{i}", b, h_split, None if i else mem_arrives)
                else:
                    split_values(S_WKV + i, f"wkv{i}", b, h_split)

            def s5_in(i, b):
                o = pe_open(pe, f"bu{i}", b)
                r, j = slice(32 * (i % 4), 32 * (i % 4) + 32), i // 4
                for e, w in enumerate(("b_re", "b_im")):
                    last = mm(o[:, e * T:(e + 1) * T], v3(prm(w), P)[r, j, :], s5u[r, j, :])
                last.then_inc(full[b], 1)

            def s5_out(q, b):
                o = pe_open(pe, "s5_y", b) if q == 0 else bank[b]
                pe.wait_ge(S["rotated_back"], q + 1)
                for i in (2 * q, 2 * q + 1):
                    y = o[32 * (i % 4):32 * (i % 4) + 32, (i // 4) * T:(i // 4 + 1) * T]
                    for n, (w, x) in enumerate(((c_re, 0), (c_nre, 1), (c_im, 2), (c_im, 3))):
                        last = mm(y, w[:, i, :], pr[:, x, i % 2, :], n == 0, n == 3)
                last.then_inc(full[b] if q == 3 else S["s5_out_used"], 1)

            def level_p(n, c, b):
                o = v3(pe_open(pe, f"P{n}{c}", b)[:, :], P)
                pe.wait_ge(S["rw_level_mask"], 2 * (n - 1) + c + 1)
                if n == 1:
                    pe.wait_ge(S["rw_x0"], c + 1)
                else:
                    moved(pe, f"X{n - 1}{c}")
                for h in range(NH):
                    last = mm(o[:, h, :], Mj[:, c, h, :], X[:, c, h, :])
                last.then_inc(full[b], 1)

            def level_x(n, c):
                moved(pe, f"P{n}{c}")
                if n == 1:
                    pe.wait_ge(S["rw_xt0"], 2 * c + 2)
                else:
                    moved(pe, f"T{n - 1}{c}")
                if n < LEVELS - 1:
                    b = 5 + 2 * c
                    o = v3(pe_open(pe, f"X{n}{c}", b)[:, :], P)
                    for h in range(NH):
                        last = mm(o[:, h, :], XT[:, c, h, :], Pm[:, c, h, :])
                    last.then_inc(full[b], 1)
                b = 4 + 2 * c
                o = v3(pe_open(pe, f"T{n}{c}", b)[:, :], P)
                for h in range(NH):
                    last = mm(o[:, h, :], Pm[:, c, h, :], XT[:, c, h, :])
                last.then_inc(full[b], 1)

            def ml_qk(h, b):
                o = pe_open(pe, f"qk{h}", b)
                pe.wait_ge(S["ml_qk"], 1)
                r, j = at(h)
                mm(o[:, 0:T], cv[r, 2 + j, 0:P], cv[r, j, :])
                mm(o[:, T:T + P], cv[r, 2 + j, P:T], cv[r, j, P:T]).then_inc(full[b], 1)

            def attend(name, b, values, probs):
                o = pe_open(pe, name, b)
                for h in range(NH):
                    r, j = at(h)
                    v0 = values[:, 0, h * HD:(h + 1) * HD] if values is not None else const("ones")[:, 0:HD]
                    v1 = values[:, 1, h * HD:(h + 1) * HD] if values is not None else const("ones")[:, 0:HD]
                    mm(o[r, j * T:(j + 1) * T], v0, probs[:, h, 0:T], True, False)
                    last = mm(o[r, j * T + P:(j + 1) * T], v1, probs[:, h, T:T + P], False, True)
                last.then_inc(full[b], 1)

            def mb_scores(h, b):
                o = pe_open(pe, f"sc{h}", b)
                moved(pe, "mb_k")
                r, j = at(h)
                mm(o[:, 0:P], mqk[r, j, 0:P], mqk[r, 2 + j, 0:P])
                mm(o[:, P:P + T], mqk[r, j, P:T], mqk[r, 2 + j, :]).then_inc(full[b], 1)

            def mb_turn(h, b):
                o = pe_open(pe, f"pt{h}", b)
                pe.wait_ge(S["mb_prob"], 1)
                for i in range(3):
                    last = nc.tensor.transpose(o[:, i * P:(i + 1) * P], Sm[:, h, i * P:(i + 1) * P], const("ident"))
                last.then_inc(full[b], 1)

            def group_sumsq(name, g, b):
                o = pe_open(pe, name, b)
                pe.wait_ge(S[("s5", "ml", "rw", "mb")[g] + "_sq"], 1)
                for j in range(2):
                    last = mm(o[:, 0:T], const("ones"), gn_sq[g][:, j, :], j == 0, j == 1)
                last.then_inc(full[b], 1)

            def solve_r(c, b):
                o = v3(pe_open(pe, f"R{c}", b)[:, 0:GW], HD)
                for h in range(NH):
                    r, j = at(h)
                    last = mm(o[:, h, :], A[:, c * NH + h, T:T + P], Vt[:, c, h * HD:(h + 1) * HD], True, c == 0)
                    if c == 1:
                        last = mm(o[:, h, :], KR[:, 0, j, P:T], S0[:, j, h % 2, :], False, True)
                last.then_inc(full[b], 1)

            def solve_u(c, b):
                o = v3(pe_open(pe, f"U{c}", b)[:, 0:GW], HD)
                moved(pe, f"T{LEVELS - 1}{c}")
                moved(pe, f"R{c}")
                for h in range(NH):
                    last = mm(o[:, h, :], XT[:, c, h, :], v3(R_, HD)[:, h, :])
                last.then_inc(full[b], 1)

            pe.wait_ge(S["first_in"], 32)
            o = pe_open(pe, "x_sumsq", 0)
            pe.wait_ge(S["x_summed"], 4)
            mm(o[:, 0:T], const("ones"), sq_x[:, 0, :]).then_inc(full[0], 1)
            split_channel_major(0, "rw_wag", 1, h_split, lambda j: pe.wait_ge(S["h_rest"], j + 1))
            split_channel_major(1, "rw_k", 0, h_split)
            pe.wait_ge(S["consts_in"], 16)
            pe.wait_ge(S["params_in"], 16)
            for h in range(NH):
                o = pe_open(pe, f"rel{h}", 4 + h)
                mm(o[:, 0:384], prm("rel", 33)[:, h:h + 1].to_broadcast([33, P]), const("onehot", 33)).then_inc(full[4 + h], 1)
            split_channel_major(2, "rw_r", 1, h_split)
            o = pe_open(pe, "mem_sumsq", 3)
            pe.wait_ge(S["mem_summed"], 3)
            mm(o[:, 0:T], const("ones"), sq_m[:, 0, :]).then_inc(full[3], 1)
            split_channel_major(3, "rw_v", 0, h_split)
            split_channel_major(4, "s5_u", 1, h_split)
            o = v3(pe_open(pe, "rw_w", 2)[:, :], T)
            pe.wait_ge(S["rw_lowrank"], 1)
            for j in range(2):
                last = mm(o[:, j, :], prm("w2a2")[0:HD, j * P:(j + 1) * P], rwE[0:HD, 0, 0, :])
            last.then_inc(full[2], 1)
            o = v3(pe_open(pe, "rw_a", 3)[:, :], T)
            for j in range(2):
                last = mm(o[:, j, :], prm("w2a2")[HD:P, j * P:(j + 1) * P], rwM[HD:P, 0, :])
            last.then_inc(full[3], 1)
            o = v3(pe_open(pe, "rw_g", 2)[:, :], T)
            for j in range(2):
                last = mm(o[:, j, :], prm("g2")[:, j * P:(j + 1) * P], rwE[:, 0, 1, :])
            last.then_inc(full[2], 1)
            split_channel_major(5, "ml_q", 0, h_split)
            o = pe_open(pe, "rw_kk", 3)
            pe.wait_ge(S["rw_kx_sq"], 1)
            mm(o[:, :], const("pair_ones"), flat(rwE[:, 1])).then_inc(full[3], 1)
            split_channel_major(6, "ml_k", 1, h_split)
            o = pe_open(pe, "gates", 2)
            for e in range(2):
                for k in range(KD):
                    last = mm(o[0:NH, e * T:(e + 1) * T], v3(prm("w_gate"), 8)[:, k, 4 * e:4 * e + 4],
                              hT[:, k, :], k == 0, k == KD - 1)
            last.then_inc(full[2], 1)
            moved(pe, "s5_u")
            s5_in(0, 0)
            s5_in(1, 1)
            o = v4(pe_open(pe, "rw_vt", 3)[:, :], 2, P)
            pe.wait_ge(S["rw_mix"], 4)
            for c in range(NC):
                for j in range(2):
                    last = nc.tensor.transpose(o[:, c, j, :], rwM[:, 6 + j, c * P:(c + 1) * P], const("ident"))
            last.then_inc(full[3], 1)
            split_values(7, "ml_v", 0, h_split)
            split_channel_major(8, "ml_o", 1, h_split)
            pe.wait_ge(S["rw_tilde"], 4)
            for c in range(NC):
                for h in range(NH):
                    i = c * NH + h
                    r, j = at(h)
                    b = 4 + i % 4
                    o = v4(pe_open(pe, f"A{i}", b)[:, :], 2, P)
                    kr = KR[r, :, j, c * P:(c + 1) * P]
                    mm(o[:, 0], Bh[r, j, c * P:(c + 1) * P], kr)
                    mm(o[:, 1], Kh[r, j, c * P:(c + 1) * P], kr).then_inc(full[b], 1)
            for c in range(NC):
                for e in range(2):
                    b = 4 + 2 * c + e
                    o = v3(pe_open(pe, f"L{c}{e}", b)[:, 0:T], P)
                    r = slice(HD * e, HD * e + HD)
                    for j in range(2):
                        last = mm(o[:, j, :], KR[r, 0, j, c * P:(c + 1) * P], Bh[r, j, c * P:(c + 1) * P])
                    last.then_inc(full[b], 1)
            o = v4(pe_open(pe, "rw_bkt", 3)[:, :], 2, P)
            for e, src in enumerate((Bh, Kh)):
                for j in range(2):
                    last = nc.tensor.transpose(o[:, e, j, :], src[:, j, 0:P], const("ident"))
            last.then_inc(full[3], 1)

            level_p(1, 0, 4)
            level_p(1, 1, 6)
            s5_in(2, 0)
            s5_in(3, 2)
            split_channel_major(9, "mb_q", 1, h_split)
            s5_out(0, 3)
            level_x(1, 0)
            level_x(1, 1)

            level_p(2, 0, 4)
            level_p(2, 1, 6)
            split_channel_major(10, "mb_k", 0, h_split)
            o = v3(pe_open(pe, "g_col", 2)[:, 0:8], 4)
            pe.wait_ge(S["ml_rows"], 1)
            for c in range(NC):
                last = nc.tensor.transpose(o[:, c, :], rows[1][0:NH, c * P:(c + 1) * P], const("ident", NH)[:, 0:NH])
            last.then_inc(full[2], 1)
            pe.wait_ge(S["ml_rows"], 2)
            for m in range(2):
                b = 1 + m
                o = v3(pe_open(pe, f"m_row{m}", b)[:, :], T)
                for e in range(2):
                    h = 2 * m + e
                    last = mm(o[:, e, :], const("head_sel", NH)[:, h * P:(h + 1) * P], rows[2][0:NH, :])
                last.then_inc(full[b], 1)
            level_x(2, 0)
            level_x(2, 1)

            level_p(3, 0, 4)
            level_p(3, 1, 6)
            split_values(11, "mb_v", 0, h_split)
            level_x(3, 0)
            level_x(3, 1)
            s5_in(4, 2)
            s5_in(5, 1)

            ml_qk(0, 2)
            ml_qk(1, 0)
            level_p(4, 0, 4)
            level_p(4, 1, 6)
            s5_out(1, 3)
            wkv(0, 1)
            level_x(4, 0)
            level_x(4, 1)

            ml_qk(2, 2)
            ml_qk(3, 0)
            level_p(5, 0, 4)
            level_p(5, 1, 6)
            wkv(1, 1)
            level_x(5, 0)
            level_x(5, 1)

            moved(pe, "qk2")
            moved(pe, "qk3")
            moved(pe, "ml_v")
            attend("num", 2, mlv, E)
            attend("den", 0, None, E)
            o = v3(pe_open(pe, "em", 1)[:, :], T)
            pe.wait_ge(S["ml_em"], 1)
            for j in range(2):
                last = mm(o[:, j, :], const("pair_sel", NH)[:, j * P:(j + 1) * P], rows[4][0:NH, :])
            last.then_inc(full[1], 1)
            level_p(6, 0, 4)
            level_p(6, 1, 6)
            wkv(2, 1)
            s5_in(6, 2)
            s5_in(7, 0)
            level_x(6, 0)
            level_x(6, 1)

            moved(pe, "rw_vt")
            solve_r(0, 4)
            mb_scores(0, 2)
            mb_scores(1, 0)
            s5_out(2, 3)
            wkv(3, 1)
            solve_u(0, 5)
            mb_scores(2, 2)
            mb_scores(3, 0)
            wkv(4, 1)
            o = pe_open(pe, "S0", 4)
            moved(pe, "U0")
            moved(pe, "rw_bkt")
            for h in range(NH):
                r, j = at(h)
                hc = slice(h * HD, (h + 1) * HD)
                mm(o[r, j * HD:(j + 1) * HD], BKt[:, 0, hc], U[:, 0, hc], True, False)
                last = mm(o[r, j * HD:(j + 1) * HD], BKt[:, 1, hc], Vt[:, 0, hc], False, True)
            last.then_inc(full[4], 1)
            o = pe_open(pe, "bonus", 7)
            pe.wait_ge(S["rw_bonus"], 1)
            mm(o[:, :], const("pair_ones"), flat(bon)).then_inc(full[7], 1)
            moved(pe, "S0")
            solve_r(1, 5)
            wkv(5, 1)
            solve_u(1, 4)
            o = v3(pe_open(pe, "rw_y", 6)[:, :], T)
            moved(pe, "U1")
            for c in range(NC):
                for h in range(NH):
                    r, j = at(h)
                    hc = slice(h * HD, (h + 1) * HD)
                    y = o[r, j, c * P:(c + 1) * P]
                    mm(y, U[:, c, hc], A[:, c * NH + h, P:T], True, False)
                    last = mm(y, Vt[:, c, hc], A[:, c * NH + h, T + P:2 * T], False, c == 0)
                    if c == 1:
                        last = mm(y, S0[:, j, h % 2, :], KR[:, 1, j, P:T], False, True)
            last.then_inc(full[6], 1)
            wkv(6, 1)
            o = pe_open(pe, "mean", 4)
            moved(pe, "rw_y")
            mm(o[:, :], const("pair_ones"), flat(Yrw)).then_inc(full[4], 1)
            for h in range(NH):
                mb_turn(h, (2, 0, 6, 2)[h])
            s5_out(3, 3)
            o = pe_open(pe, "var", 5)
            pe.wait_ge(S["rw_ysq"], 1)
            mm(o[:, :], const("pair_ones"), flat(Ysq)).then_inc(full[5], 1)
            moved(pe, "pt3")
            moved(pe, "mb_v")
            attend("mb_o", 2, mbv, PTm)
            wkv(7, 1)
            group_sumsq("gn_ml", 1, 6)
            group_sumsq("gn_mb", 3, 0)
            o = v3(pe_open(pe, "glu", 3)[:, :], T)
            pe.wait_ge(S["s5_z"], 1)
            for j in range(2):
                for k in range(2):
                    last = mm(o[:, j, :], v3(prm("w_glu"), GW)[:, k, j * P:(j + 1) * P], z5[:, k, :], k == 0, k == 1)
            last.then_inc(full[3], 1)

            for q in range(8):
                if q == 2:
                    group_sumsq("gn_rw", 2, 3)
                if q == 3:
                    group_sumsq("gn_s5", 0, 1)
                if q in (0, 4):
                    pe.wait_ge(S["y_rest"], 2 * (q // 4) + 2)
                split_token_major(S_WOUT, q, f"wout{q % 4}", 4 + q % 4, y_split, Y_ORDER)

            def turn_stream(tag, n):
                for m in range(2):
                    pe.wait_ge(S["xn_ready"], 2 * n + m + 1)
                    for i in range(4):
                        if m == 0:
                            pe_open(pe, f"{tag}{i}", i)
                        o = v4(bank[i][:, :], 2, P)
                        for k in range(2):
                            last = nc.tensor.transpose(o[:, k, m, :], xtmp[:, m, (2 * i + k) * P:(2 * i + k + 1) * P],
                                                       const("ident"))
                        if m == 1:
                            last.then_inc(full[i], 1)

            def turned(tag):
                def arrive(j):
                    for i in (2 * j, 2 * j + 1):
                        moved(pe, f"{tag}{i}")
                return arrive

            turn_stream("xat", 0)

            def x_scores(h):
                o = v3(pe_open(pe, f"xs{h}", h)[:, :], NMEM)
                moved(pe, f"q{h}")
                for m in range(2):
                    for k in range(2):
                        last = mm(o[:, m, :], qx[:, 2 * h + k, m * P:(m + 1) * P], kx[:, 2 * h + k, :], k == 0, k == 1)
                last.then_inc(full[h], 1)

            for i in range(N_WQ):
                split_channel_major(S_WQ + i, f"q{i}", 4 + i, h_split, None if i else turned("xat"))
                if i > 0:
                    x_scores(i - 1)
            x_scores(XH - 1)
            for h in range(XH):
                o = v3(pe_open(pe, f"xp{h}", 4 + h)[:, :], T)
                pe.wait_ge(S["x_prob"], h + 1)
                for m in range(2):
                    for t in range(2):
                        last = nc.tensor.transpose(o[:, m, t * P:(t + 1) * P], px[:, h, t, m * P:(m + 1) * P],
                                                   const("ident"))
                last.then_inc(full[4 + h], 1)
            for h in range(XH):
                o = v3(pe_open(pe, f"xo{h}", h)[:, :], T)
                moved(pe, f"xp{h}")
                for d in range(2):
                    for m in range(2):
                        c0 = h * XD + d * P
                        last = mm(o[:, d, :], vx[:, m, c0:c0 + P], ptx[:, h, m, :], m == 0, m == 1)
                last.then_inc(full[h], 1)
            for q in range(8):
                if q in (0, 4):
                    for h in (q // 2, q // 2 + 1):
                        moved(pe, f"xo{h}")
                split_token_major(S_WO, q, f"wo{q % 4}", 4 + q % 4, ox_split, range(KD))

            turn_stream("fft", 1)
            for p in range(NFF // 2):
                split_channel_major(S_FIN + 2 * p, f"g{p}", 2 * (p % 2), h_split, None if p else turned("fft"))
                split_channel_major(S_FIN + 2 * p + 1, f"u{p}", 2 * (p % 2) + 1, h_split)
            ys = [pe_open(pe, f"y{i}", 4 + i) for i in range(4)]
            for kt in range(NFF):
                i = 2 * S_FOUT + kt
                wait_rest(pe, i)
                if kt % 2 == 0:
                    pe.wait_ge(S["act_rest"], kt // 2 + 1)
                w = [flat(x) for x in split_half(i)]
                for m in range(2):
                    for half in range(2):
                        last = mm3(ys[2 * m + half][:, :], [x[:, kt, m * P:(m + 1) * P] for x in act_split],
                                   [x[:, half * 512:(half + 1) * 512] for x in w], kt == 0, kt == NFF - 1)
                        if kt == NFF - 1:
                            last.then_inc(full[4 + 2 * m + half], 1)
                if kt < NFF - 1:
                    used(last, i)

        @block.sync
        def _(sp):
            sp.dma_start(hT, v3(x_t, T)).then_inc(S["x_in"], 16)
            sp.dma_start(cst[:, 0:CONST_FIRST], consts_d[:, 0:CONST_FIRST]).then_inc(S["first_in"], 16)
            sp.dma_start(par[:, 0:PARAM_FIRST], params_d[:, 0:PARAM_FIRST]).then_inc(S["first_in"], 16)
            for n in range(NSLOTS):
                if n == 2:
                    sp.dma_start(cst[:, CONST_FIRST:], consts_d[:, CONST_FIRST:]).then_inc(S["consts_in"], 16)
                    sp.dma_start(par[:, PARAM_FIRST:], params_d[:, PARAM_FIRST:]).then_inc(S["params_in"], 16)
                if n == 3:
                    sp.dma_start(mem_h, v3(mem_t, NMEM)).then_inc(S["mem_in"], 16)
                if n == S_WQ:
                    sp.wait_ge(S["gn_done"], 4)
                    sp.dma_start(gain_, gain_rows(0)).then_inc(S["gain_in"], 16)
                    sp.dma_start(xres, x_rows.rearrange("(m p) c -> p m c", p=P)).then_inc(S["xres_in"], 16)
                if n in (S_WO, S_FIN + 8):
                    g = 1 if n == S_WO else 2
                    sp.wait_ge(S["x_new"], 2 * g - 1)
                    sp.dma_start(gain_, gain_rows(g)).then_inc(S["gain_in"], 16)
                before = max((m for m in range(n) if place(m) == place(n)), default=None)
                if before is None:
                    if n >= EARLY_RING:
                        wait_full(sp, "pt3")
                        wait_full(sp, "s5_y")
                else:
                    for i in range(2):
                        wait_rest(sp, 2 * before + i)
                sp.dma_start(slot(n), weights_d[n]).then_inc(loaded[place(n)], 16)
                if n == 5:
                    for h in range(NH):
                        moved(sp, f"rel{h}")
                    sp.dma_start(rel_scratch.ap(), E_).then_inc(S["rel_stored"], 16)
                if n == 9:
                    sp.wait_ge(S["rel_stored"], 16)
                    sp.wait_ge(S["rw_tilde"], 4)
                    skew = bass.AP(rel_scratch, P - 1, [[NH * 384 - 1, P], [384, NH], [1, T]])
                    sp.dma_start(Bz, skew).then_inc(S["rel_in"], 16)
            for m in range(2):
                sp.wait_ge(S["x_new"], 5 + m)
                sp.dma_start(out[0, m * P:(m + 1) * P, :], xres[:, m, :]).then_inc(S["out_stored"], 16)
            sp.wait_ge(S["out_stored"], 32)

        @block.gpsimd
        def _(pool):
            g = nc.gpsimd
            g.memset(rwP[:, :, 0:1], 0.0).then_inc(S["zeros_ready"], 1)
            g.memset(raw[:, :, 0:3], 0.0).then_inc(S["zeros_ready"], 1)
            g.memset(S0_, 0.0).then_inc(S["zeros_ready"], 1)
            for i in range(1, H_MID, 2):
                rest(pool, g, i)
                if i == 3:
                    pool.wait_ge(S["sq_m_ready"], 1)
                    sum_tiles(pool, g, sq_m, "mem_summed")
            pool.wait_ge(S["s5_co"], 1)
            wr, wi, xr, xi = (v3(pr_[:, 256 * i:256 * i + 256], 32) for i in range(4))
            g.tensor_tensor(wr, c_re, spread(co_re, 32), ALU.mult)
            g.tensor_tensor(wi, c_im, spread(co_im, 32), ALU.mult)
            g.tensor_tensor(xr, c_re, spread(co_im, 32), ALU.mult)
            g.tensor_tensor(xi, c_im, spread(co_re, 32), ALU.mult).then_inc(S["s5_c"], 1)
            pool.wait_ge(S["s5_c"], 1)
            g.tensor_tensor(c_nre, wi, wr, ALU.subtract)
            g.tensor_tensor(c_re, wr, wi, ALU.subtract)
            g.tensor_tensor(xr, xr, xi, ALU.add).then_inc(S["s5_c"], 1)
            pool.wait_ge(S["s5_c"], 2)
            g.tensor_scalar(c_im, xr, -1.0, None, ALU.mult).then_inc(S["s5_c"], 1)

            def rotate(q):
                cq, sq = cos[:, 2 * q:2 * q + 2, :], sin[:, 2 * q:2 * q + 2, :]
                moved(pool, f"bu{2 * q}")
                moved(pool, f"bu{2 * q + 1}")
                if q > 0:
                    pool.wait_ge(S["rotated_back"], q)
                g.tensor_tensor(t1, cq, bu[:, 0], ALU.mult)
                g.tensor_tensor(t2, cq, bu[:, 1], ALU.mult).then_inc(S["rotating"], 1)
                pool.wait_ge(S["rotating"], 3 * q + 1)
                g.tensor_tensor(bu[:, 1], sq, bu[:, 1], ALU.mult)
                g.tensor_tensor(bu[:, 0], sq, bu[:, 0], ALU.mult).then_inc(S["rotating"], 1)
                pool.wait_ge(S["rotating"], 3 * q + 2)
                g.tensor_tensor(t1, t1, bu[:, 1], ALU.add)
                g.tensor_tensor(t2, t2, bu[:, 0], ALU.subtract).then_inc(S["rotating"], 1)

            def rotate_back(q):
                cq, sq = cos[:, 2 * q:2 * q + 2, :], sin[:, 2 * q:2 * q + 2, :]
                pool.wait_ge(S["scanned"], q + 1)
                if q > 0:
                    pool.wait_ge(S["s5_out_used"], q)
                for x, (a_, b_) in enumerate(((cq, t1), (sq, t2), (cq, t2), (sq, t1))):
                    last = g.tensor_tensor(pr[:, x], a_, b_, ALU.mult)
                last.then_inc(S["rotated_back"], 1)

            def level_mask(n):
                for c in range(NC):
                    if n > 1:
                        wait_full(pool, f"P{n - 1}{c}")
                    else:
                        for i in range(NH * c, NH * (c + 1)):
                            moved(pool, f"A{i}")
                    g.tensor_tensor(Mj[:, c], A[:, NH * c:NH * (c + 1), 0:P],
                                    copies(const("levels")[:, n * P:(n + 1) * P], NH),
                                    ALU.mult).then_inc(S["rw_level_mask"], 1)

            pool.wait_ge(S["sincos"], 3)
            rotate(0)
            level_mask(1)
            rotate_back(0)
            level_mask(2)
            rotate(1)
            level_mask(3)
            rotate_back(1)
            level_mask(4)
            rotate(2)
            level_mask(5)
            rotate_back(2)
            level_mask(6)
            rotate(3)
            rotate_back(3)
            for i in range(H_LATE + 1, NHALF, 2):
                rest(pool, g, i)

        @block.scalar
        def _(act):
            a = nc.scalar
            LN_EXP = "natural_log_exp_and_others"
            a.preload_act_table_set(LN_EXP)

            def project(name, out_):
                o = wait_full(act, name)
                a.activation(out_, v3(o[:, :], 256), ACT.Copy).then_inc(free_of(name), 1)

            def inv_root(name, out_, width, scale, eps):
                o = wait_full(act, name)
                a.activation(out_, o[:, 0:width], ACT.Ln, bias=const(eps), scale=scale).then_inc(free_of(name), 1)
                moved(act, name)
                return a.activation(out_, out_, ACT.Exp, scale=-0.5)

            def s5_driving(i):
                if i in (2, 4, 6):
                    act.wait_ge(S["rotating"], 3 * (i // 2))
                project(f"bu{i}", bu[:, :, i % 2, :])

            def level_evac(n):
                for c in range(NC):
                    o = wait_full(act, f"P{n}{c}")
                    a.activation(Pm[:, c], v3(o[:, :], P), ACT.Copy).then_inc(free_of(f"P{n}{c}"), 1)

            def wkv_evac(i):
                project(f"wkv{i}", kx[:, 2 * i:2 * i + 2, :] if i < 4 else vx[:, :, (i - 4) * 256:(i - 3) * 256])

            split = [0]

            def highs(upto):
                while split[0] < min(upto, NHALF):
                    high_part(act, split[0])
                    split[0] += 1

            act.wait_ge(S["x_in"], 16)
            a.activation(sq_x[:, 0:4, :], hT[:, 0:4, :], ACT.Square).then_inc(S["sq_ready"], 1)
            act.wait_ge(S["first_in"], 32)
            highs(2)
            inv_root("x_sumsq", rstd_x, T, 1.0 / D, "eps6").then_inc(S["rstd_x"], 1)
            for j in range(2):
                act.wait_ge(S["h_ready"], j + 1)
                a.activation(h_split[0][:, 4 * j:4 * j + 4, :], hT[:, 4 * j:4 * j + 4, :], ACT.Copy).then_inc(S["h_high"], 1)
            highs(4)
            a.activation(step, prm("log_step"), ACT.Exp).then_inc(S["s5_step"], 1)
            act.wait_ge(S["s5_decay"], 1)
            a.activation(mag, s8a, ACT.Exp).then_inc(S["s5_step"], 1)
            act.wait_ge(S["mem_in"], 16)
            a.activation(sq_m, mem_h, ACT.Square).then_inc(S["sq_m_ready"], 1)
            act.wait_ge(S["zeros_ready"], 1)
            project("rw_wag", rwP[:, 0:2, 1:257])
            highs(6)
            project("rw_k", rwP[:, 2:4, 1:257])
            highs(8)
            act.wait_ge(S["theta"], 6)
            a.activation(cos, sin, ACT.Abs).then_inc(S["sincos"], 1)
            act.wait_ge(S["sincos"], 1)
            a.activation(cos, cos, ACT.Sin, bias=const("half_pi"), scale=-TAU).then_inc(S["sincos"], 1)
            highs(9)
            a.activation(sin, sin, ACT.Sin, scale=TAU).then_inc(S["sincos"], 1)
            a.preload_act_table_set(LN_EXP)
            project("rw_r", rwP[:, 4:6, 1:257])
            highs(10)
            act.wait_ge(S["rw_mix"], 1)
            a.activation(rwE[0:HD, 0, 0, :], rwM[0:HD, 0, :], ACT.Exp, scale=-2.0)
            a.activation(rwE[:, 0, 1, :], rwM[:, 1, :], ACT.Exp, scale=-1.0).then_inc(S["rw_exp"], 1)
            project("rw_v", rwP[:, 6:8, 1:257])
            highs(12)
            inv_root("mem_sumsq", rstd_m, T, 1.0 / D, "eps6").then_inc(S["rstd_m"], 1)
            act.wait_ge(S["rw_mix"], 4)
            act.wait_ge(S["neg_ready"], 1)
            for name, out_, b in (("rw_w", G, 0), ("rw_a", ab, 2)):
                o = v3(wait_full(act, name)[:, :], T)
                for j in range(2):
                    e = a.activation(out_[:, j, :], o[:, j, :], ACT.Exp, bias=neg_w0a0[:, b + j:b + j + 1], scale=-1.0)
                e.then_inc(free_of(name), 1)
            project("s5_u", s5u)
            highs(14)
            project("rw_g", rwg)
            act.wait_ge(S["zeros_ready"], 2)
            project("ml_q", raw[:, 0:2, 3:259])
            highs(16)
            inv_root("rw_kk", flat(rwE[:, 2]), 512, 1.0, "eps12").then_inc(S["rw_inv"], 1)
            project("ml_k", raw[:, 2:4, 3:259])
            highs(18)
            act.wait_ge(S["rw_G"], 4)
            a.activation(rwE[:, 0], Gp, ACT.Exp)
            a.activation(rwE[:, 1], G, ACT.Exp)
            a.activation(carry, carry, ACT.Exp)
            act.wait_ge(S["rw_kk"], 1)
            a.activation(rwE[:, 2], Gp, ACT.Exp, scale=-1.0).then_inc(S["rw_E"], 1)
            s5_driving(0)
            s5_driving(1)
            wait_full(act, "gates")
            highs(H_MID + 2)
            project("rw_vt", Vt)
            act.wait_ge(S["rw_E"], 1)
            project("ml_v", mlv)
            o = wait_full(act, "ml_o")
            a.activation(mlo, v3(o[:, :], T), ACT.Exp, scale=-1.0).then_inc(free_of("ml_o"), 1)
            project("rw_bkt", BKt)

            level_evac(1)
            s5_driving(2)
            s5_driving(3)
            act.wait_ge(S["rw_tilde"], 4)
            highs(H_MID + 3)
            project("mb_q", mqk[:, 0:2, :])
            highs(H_MID + 4)
            act.wait_ge(S["ml_gate"], 1)
            a.activation(rows[3][0:NH, :], rows[0][0:NH, :], ACT.Abs).then_inc(S["ml_log"], 1)
            act.wait_ge(S["ml_log"], 1)
            a.activation(rows[3][0:NH, :], rows[3][0:NH, :], ACT.Exp, scale=-1.0).then_inc(S["ml_log"], 1)
            act.wait_ge(S["ml_log"], 2)
            a.activation(rows[3][0:NH, :], rows[3][0:NH, :], ACT.Ln, bias=const("ones", NH)[:, 0:1]).then_inc(S["ml_log"], 1)
            act.wait_ge(S["ml_conv"], 4)
            act.wait_ge(S["rel_stored"], 16)
            a.activation(E_[:, 0:1024], flat(cv), ACT.Exp, scale=-1.0).then_inc(S["ml_silu"], 1)
            level_evac(2)
            highs(H_MID + 5)
            project("mb_k", mqk[:, 2:4, :])
            o = wait_full(act, "g_col")
            a.activation(gcol, o[:, 0:8], ACT.Copy).then_inc(free_of("g_col"), 1)
            highs(H_MID + 6)
            act.wait_ge(S["ml_rows"], 3)
            a.activation(rows[4][0:NH, :], rows[4][0:NH, :], ACT.Exp).then_inc(S["ml_em"], 1)
            level_evac(3)
            project("mb_v", mbv)
            act.wait_ge(S["mem_ready"], 1)
            for j in range(2):
                ks = slice(4 * j, 4 * j + 4)
                a.activation(h_split[0][:, ks, :], mem_h[:, ks, :], ACT.Copy).then_inc(S["h_high"], 1)
            moved(act, "m_row0")
            moved(act, "m_row1")
            a.activation(E_, E_, ACT.Exp).then_inc(S["ml_E"], 1)
            s5_driving(4)
            s5_driving(5)
            act.wait_ge(S["rotated_back"], 2)
            highs(H_WKV + 2)

            def wkv_done(i):
                highs(H_WKV + 2 * i + 3)
                wkv_evac(i)
                highs(H_WKV + 2 * i + 4)

            level_evac(4)
            wkv_done(0)
            level_evac(5)
            wkv_done(1)
            level_evac(6)
            wkv_done(2)
            s5_driving(6)
            s5_driving(7)
            wkv_done(3)
            wkv_done(4)
            act.wait_ge(S["mb_max"], 1)
            for h in range(NH):
                for m, (lo, hi) in enumerate(((0, P), (P, P + T))):
                    e = a.activation(Sm[:, h, lo:hi], Sm[:, h, lo:hi], ACT.Exp, bias=nmax[:, 4 * m + h:4 * m + h + 1],
                                     accum_out=mb_sum[:, 4 * m + h:4 * m + h + 1])
            e.then_inc(S["mb_exp"], 1)
            wkv_done(5)
            wkv_done(6)
            moved(act, "mean")
            a.activation(Ysq, Yrw, ACT.Square).then_inc(S["rw_ysq"], 1)
            for h in range(NH):
                o = wait_full(act, f"pt{h}")
                a.activation(PTm[:, h, :], o[:, 0:384], ACT.Copy).then_inc(free_of(f"pt{h}"), 1)
            inv_root("var", Pm_[:, 0:512], 512, 1.0 / HD, "eps_gn").then_inc(S["rw_rstd"], 1)
            def group_square(g_, name):
                a.activation(gn_sq[g_], yT[:, 2 * g_:2 * g_ + 2, :], ACT.Square).then_inc(S[name + "_sq"], 1)

            def group_root(g_, name):
                inv_root("gn_" + name, gn_sq[g_][:, 0, :], T, 1.0 / GW, "eps6").then_inc(S[name + "_root"], 1)

            def y_high(turn, g_):
                act.wait_ge(S["gn_done"], turn + 1)
                a.activation(y_split[0][:, 2 * g_:2 * g_ + 2, :], yT[:, 2 * g_:2 * g_ + 2, :],
                             ACT.Copy).then_inc(S["high_ready"], 1)

            moved(act, "num")
            group_square(1, "ml")
            act.wait_ge(S["s5_arg"], 1)
            a.activation(z5b, z5a, ACT.Exp, scale=-GELU).then_inc(S["s5_exp"], 1)
            moved(act, "mb_o")
            group_square(3, "mb")
            wait_full(act, "rw_y")
            act.wait_ge(S["rotated_back"], 4)
            highs(H_LATE + 2)
            wkv_evac(7)
            group_root(1, "ml")
            group_root(3, "mb")
            y_high(0, 1)
            y_high(1, 3)
            o = v3(wait_full(act, "glu")[:, :], T)
            for j in range(2):
                e = a.activation(z5b[:, j, :], o[:, j, :], ACT.Exp, bias=neg_bglu[:, j:j + 1], scale=-1.0)
            e.then_inc(free_of("glu"), 1)
            highs(H_LATE + 3)
            act.wait_ge(S["rw_out"], 1)
            group_square(2, "rw")
            highs(H_LATE + 4)
            group_root(2, "rw")
            y_high(2, 2)
            act.wait_ge(S["s5_out"], 1)
            group_square(0, "s5")
            highs(H_LATE + 6)
            group_root(0, "s5")
            y_high(3, 0)

            def post_square(name, src, m, part):
                o = wait_full(act, name)
                w = src[1] - src[0]
                return a.activation(px_[:, m * D + part * w:m * D + (part + 1) * w], o[:, src[0]:src[1]], ACT.Square,
                                    accum_out=ssq[:, 4 * m + part:4 * m + part + 1])

            def post_root(n):
                act.wait_ge(S["post_sum"], n + 1)
                a.activation(rst, rst, ACT.Ln, bias=const("eps6"), scale=1.0 / D).then_inc(S["post_root"], 1)
                act.wait_ge(S["post_root"], 2 * n + 1)
                a.activation(rst, rst, ACT.Exp, scale=-0.5).then_inc(S["post_root"], 1)

            def pre_root(n):
                for m in range(2):
                    at = 6 * n + 3 * m
                    r = rst[:, m:m + 1]
                    act.wait_ge(S["x_new"], 2 * n + m + 1)
                    a.activation(px_[:, m * D:(m + 1) * D], xres[:, m, :], ACT.Square, accum_out=r).then_inc(S["pre_root"], 1)
                    act.wait_ge(S["pre_root"], at + 1)
                    a.activation(r, r, ACT.Ln, bias=const("eps6"), scale=1.0 / D).then_inc(S["pre_root"], 1)
                    act.wait_ge(S["pre_root"], at + 2)
                    a.activation(r, r, ACT.Exp, scale=-0.5).then_inc(S["pre_root"], 1)

            def projected(tag, first):
                for i in range(4):
                    for m in range(2):
                        e = post_square(f"{tag}{i}", (256 * m, 256 * m + 256), m, i)
                    e.then_inc(S["post_sq"], 1)
                    if i < 2:
                        highs(first + i + 1)

            def high_of_bank(name, out_, scale=1.0):
                o = v3(wait_full(act, name)[:, :], T)
                if isinstance(scale, float):
                    return a.activation(out_, o, ACT.Copy, scale=scale)
                for k in range(2):
                    e = a.activation(out_[:, k, :], o[:, k, :], ACT.Copy, scale=scale[:, k:k + 1])
                return e

            def turned(tag, gain):
                for i in range(4):
                    high_of_bank(f"{tag}{i}", h_split[0][:, 2 * i:2 * i + 2, :],
                                 prm(gain)[:, 2 * i:2 * i + 2]).then_inc(S["high_ready"], 1)

            highs(H_LATE + 8)
            projected("wout", H_LATE + 8)
            post_root(0)
            pre_root(0)
            turned("xat", "pre_xa")
            highs(H_LATE + 12)

            def x_exp(h):
                o = v3(wait_full(act, f"xs{h}")[:, :], NMEM)
                act.wait_ge(S["x_max"], 2 * (h + 1))
                for m in range(2):
                    e = a.activation(px[:, h, m, :], o[:, m, :], ACT.Exp, bias=xmax[:, 2 * h + m:2 * h + m + 1],
                                     scale=XD ** -0.5, accum_out=xsum[:, 2 * h + m:2 * h + m + 1])
                e.then_inc(free_of(f"xs{h}"), 1)

            for i in range(N_WQ):
                highs(H_LATE + 14 + 2 * i)
                project(f"q{i}", qx[:, 2 * i:2 * i + 2, :])
                if i > 1:
                    x_exp(i - 2)
            x_exp(XH - 2)
            x_exp(XH - 1)
            for h in range(XH):
                project(f"xp{h}", ptx[:, h])
            for h in range(XH):
                high_of_bank(f"xo{h}", ox_split[0][:, 2 * h:2 * h + 2, :]).then_inc(S["high_ready"], 1)
            first = 2 * S_FIN
            highs(first)
            projected("wo", first)
            post_root(1)
            pre_root(1)
            turned("fft", "pre_ffn")
            highs(first + 4)

            def act_high(p):
                moved(act, f"u{p}")
                a.activation(flat(act_split[0][:, 2 * p:2 * p + 2, :]), fft[:, p % 2, :],
                             ACT.Copy).then_inc(S["high_ready"], 1)

            for p in range(NFF // 2):
                highs(first + 4 * p + 6)
                o = wait_full(act, f"g{p}")
                if p > 1:
                    act.wait_ge(S["act_rest"], p - 1)
                a.activation(fft[:, p % 2, :], o[:, :], ACT.Exp, scale=-1.0).then_inc(S["f_exp"], 1)
                if p > 0:
                    act_high(p - 1)
                highs(first + 4 * p + 8)
            act_high(NFF // 2 - 1)
            highs(NHALF)
            for m in range(2):
                for i in range(2):
                    post_square(f"y{2 * m + i}", (0, 512), m, i).then_inc(S["post_sq"], 1)
            post_root(2)

        @block.vector
        def _(dve):
            v = nc.vector

            def sigmoid_of_exp(x, name, n):
                v.tensor_scalar(x, x, 1.0, None, ALU.add).then_inc(S[name], 1)
                dve.wait_ge(S[name], n + 1)
                return v.reciprocal(x, x)

            split = [0]

            def rests(upto):
                while split[0] < min(upto, NHALF):
                    if split[0] % 2 == 0 or H_MID <= split[0] < H_LATE:
                        rest(dve, v, split[0])
                    split[0] += 1

            dve.wait_ge(S["x_in"], 16)
            v.tensor_tensor(sq_x[:, 4:8, :], hT[:, 4:8, :], hT[:, 4:8, :], ALU.mult).then_inc(S["x_summed"], 1)
            dve.wait_ge(S["sq_ready"], 1)
            dve.wait_ge(S["x_summed"], 1)
            sum_tiles(dve, v, sq_x, "x_summed", 1)
            dve.wait_ge(S["first_in"], 32)
            a, b = PARAM["w0"][0], PARAM["a0"][1]
            v.tensor_scalar(neg_w0a0, par[:, a:b], -1.0, None, ALU.mult)
            v.tensor_scalar(neg_bglu, prm("b_glu"), -1.0, None, ALU.mult)
            v.tensor_scalar(one_ka, prm("k_a"), -1.0, 1.0, ALU.mult, ALU.add).then_inc(S["neg_ready"], 1)
            rests(2)
            dve.wait_ge(S["rstd_x"], 1)

            def h_rest(n, h):
                dve.wait_ge(S["h_high"], n + 1)
                ks = slice(4 * (n % 2), 4 * (n % 2) + 4)
                v.tensor_tensor(h_split[1][:, ks, :], h[:, ks, :], h_split[0][:, ks, :].bitcast(F32),
                                ALU.subtract).then_inc(S["h_rest"], 1)

            for k in range(KD):
                last = v.scalar_tensor_tensor(hT[:, k, :], hT[:, k, :], prm("pre_mix")[:, k:k + 1], rstd_x,
                                              ALU.mult, ALU.mult)
                if k % 4 == 3:
                    last.then_inc(S["h_ready"], 1)
                if k == 5:
                    h_rest(0, hT)
            h_rest(1, hT)
            rests(4)
            dve.wait_ge(S["consts_in"], 16)
            dve.wait_ge(S["params_in"], 16)
            dve.wait_ge(S["s5_step"], 1)
            v.tensor_tensor(s8a, prm("lam_re"), step, ALU.mult).then_inc(S["s5_decay"], 1)
            v.scalar_tensor_tensor(frac, prm("lam_im"), 1.0 / (2.0 * math.pi), step, ALU.mult, ALU.mult).then_inc(S["theta"], 1)
            dve.wait_ge(S["theta"], 1)
            v.tensor_scalar(frn, frac, ROUND, None, ALU.add).then_inc(S["theta"], 1)
            dve.wait_ge(S["theta"], 2)
            v.scalar_tensor_tensor(frac, frn, ROUND, frac, ALU.subtract, ALU.subtract).then_inc(S["theta"], 1)
            dve.wait_ge(S["theta"], 3)
            for i in range(8):
                last = v.tensor_scalar(sin[:, i, :], const("time"), frac[:, i:i + 1], None, ALU.mult)
            last.then_inc(S["theta"], 1)
            dve.wait_ge(S["theta"], 4)
            v.tensor_scalar(cos, sin, ROUND, None, ALU.add).then_inc(S["theta"], 1)
            dve.wait_ge(S["theta"], 5)
            v.scalar_tensor_tensor(sin, cos, ROUND, sin, ALU.subtract, ALU.subtract).then_inc(S["theta"], 1)

            def mix(n, name):
                moved(dve, name)
                v.tensor_tensor(rwM[:, 2 * n:2 * n + 2, :], rwP[:, 2 * n:2 * n + 2, 0:T], rwP[:, 2 * n:2 * n + 2, 1:T + 1],
                                ALU.subtract).then_inc(S["rw_diff"], 1)
                dve.wait_ge(S["rw_diff"], n + 1)
                for i in (2 * n, 2 * n + 1):
                    last = v.scalar_tensor_tensor(rwM[:, i, :], rwM[:, i, :], prm("mu")[:, i:i + 1], rwP[:, i, 1:T + 1],
                                                  ALU.mult, ALU.add)
                last.then_inc(S["rw_mix"], 1)

            dve.wait_ge(S["zeros_ready"], 1)
            mix(0, "rw_wag")
            rests(6)
            mix(1, "rw_k")
            rests(8)
            for h in range(NH):
                o = wait_full(dve, f"rel{h}")
                v.tensor_copy(E[:, h, :], o[:, 0:384]).then_inc(free_of(f"rel{h}"), 1)
            rests(9)
            mix(2, "rw_r")
            rests(10)
            dve.wait_ge(S["rw_exp"], 1)
            v.tensor_scalar(rwE[0:HD, 0, 0, :], rwE[0:HD, 0, 0, :], 1.0, None, ALU.add)
            v.tensor_scalar(rwE[:, 0, 1, :], rwE[:, 0, 1, :], 1.0, None, ALU.add).then_inc(S["rw_low"], 1)
            dve.wait_ge(S["rw_low"], 1)
            v.reciprocal(rwE[0:HD, 0, 0, :], rwE[0:HD, 0, 0, :])
            v.reciprocal(rwE[:, 0, 1, :], rwE[:, 0, 1, :]).then_inc(S["rw_low"], 1)
            dve.wait_ge(S["rw_low"], 2)
            v.tensor_scalar(rwE[0:HD, 0, 0, :], rwE[0:HD, 0, 0, :], 2.0, -1.0, ALU.mult, ALU.add).then_inc(S["rw_lowrank"], 1)
            mix(3, "rw_v")
            rests(12)
            dve.wait_ge(S["rw_mix"], 4)
            for j in range(2):
                last = v.tensor_scalar(kk[:, j, :], rwM[:, 2 + j, :], prm("k_k")[:, j:j + 1], None, ALU.mult)
            last.then_inc(S["rw_kx"], 1)
            dve.wait_ge(S["rw_kx"], 1)
            v.tensor_tensor(rwE[:, 1], kk, kk, ALU.mult).then_inc(S["rw_kx_sq"], 1)
            moved(dve, "rw_w")
            sigmoid_of_exp(G, "rw_G0", 0).then_inc(S["rw_G0"], 1)
            dve.wait_ge(S["rw_G0"], 2)
            v.tensor_scalar(G, G, -DECAY, None, ALU.mult).then_inc(S["rw_G0"], 1)
            dve.wait_ge(S["rw_G0"], 3)
            for j in range(2):
                for c in range(NC):
                    cs = slice(c * C, (c + 1) * C)
                    last = v.tensor_tensor_scan(Gp[:, j, cs], const("ones"), G[:, j, cs], 0.0, ALU.mult, ALU.add)
            last.then_inc(S["rw_G"], 1)
            dve.wait_ge(S["rw_G"], 1)
            Gpc, Gc = v3(flat(Gp), C), v3(flat(G), C)
            v.tensor_copy(mid, Gpc[:, :, C // 2 - 1]).then_inc(S["rw_G"], 1)
            dve.wait_ge(S["rw_G"], 2)
            v.tensor_tensor(Gpc, Gpc, spread(mid, C), ALU.subtract).then_inc(S["rw_G"], 1)
            dve.wait_ge(S["rw_G"], 3)
            v.tensor_tensor(carry, Gp[:, :, C - 1], mid[:, 1:4:2], ALU.add)
            v.tensor_tensor(G, Gp, G, ALU.subtract).then_inc(S["rw_G"], 1)
            rests(14)
            moved(dve, "rw_a")
            sigmoid_of_exp(ab, "rw_a", 0).then_inc(S["rw_a"], 1)
            dve.wait_ge(S["rw_inv"], 1)
            v.tensor_tensor(kk, kk, rwE[:, 2], ALU.mult).then_inc(S["rw_kk"], 1)
            dve.wait_ge(S["rw_a"], 2)
            k2 = rwM[:, 2:4, :]
            for j in range(2):
                last = v.tensor_scalar(Kh[:, j, :], ab[:, j, :], prm("k_a")[:, j:j + 1], one_ka[:, j:j + 1], ALU.mult, ALU.add)
            last.then_inc(S["rw_k2"], 1)
            dve.wait_ge(S["rw_kk"], 1)
            dve.wait_ge(S["rw_k2"], 1)
            v.tensor_tensor(ab, kk, ab, ALU.mult).then_inc(S["rw_k2"], 1)
            v.tensor_tensor(k2, k2, Kh, ALU.mult).then_inc(S["rw_k2"], 1)
            rests(16)
            dve.wait_ge(S["rw_k2"], 3)
            dve.wait_ge(S["rw_E"], 1)
            v.tensor_tensor(KR[:, 0], kk, rwE[:, 1], ALU.mult).then_inc(S["rw_tilde"], 1)
            v.tensor_tensor(KR[:, 1], rwM[:, 4:6, :], rwE[:, 0], ALU.mult).then_inc(S["rw_tilde"], 1)
            v.tensor_tensor(Bh, ab, rwE[:, 2], ALU.mult).then_inc(S["rw_tilde"], 1)
            v.tensor_tensor(Kh, k2, rwE[:, 2], ALU.mult).then_inc(S["rw_tilde"], 1)
            dve.wait_ge(S["rw_tilde"], 2)
            for j in range(2):
                last = v.scalar_tensor_tensor(bon[:, j, :], bon[:, j, :], prm("r_k")[:, j:j + 1], k2[:, j, :],
                                              ALU.mult, ALU.mult)
            last.then_inc(S["rw_bonus"], 1)
            rests(18)
            dve.wait_ge(S["sincos"], 3)
            cos1, sin1, lr, li = cos[:, :, 1], sin[:, :, 1], prm("lam_re"), prm("lam_im")
            v.tensor_tensor(s8b, mag, cos1, ALU.mult)
            v.tensor_tensor(s8c, mag, sin1, ALU.mult)
            v.tensor_tensor(den8, lr, lr, ALU.mult)
            v.tensor_tensor(s8a, li, li, ALU.mult).then_inc(S["s5_co_step"], 1)
            dve.wait_ge(S["s5_co_step"], 1)
            v.tensor_tensor(den8, den8, s8a, ALU.add)
            v.tensor_scalar(s8b, s8b, -1.0, None, ALU.add).then_inc(S["s5_co_step"], 1)
            dve.wait_ge(S["s5_co_step"], 2)
            v.reciprocal(den8, den8)
            v.tensor_tensor(co_re, s8b, lr, ALU.mult)
            v.tensor_tensor(s8a, s8c, li, ALU.mult)
            v.tensor_tensor(co_im, s8c, lr, ALU.mult)
            v.tensor_tensor(frn, s8b, li, ALU.mult).then_inc(S["s5_co_step"], 1)
            dve.wait_ge(S["s5_co_step"], 3)
            v.tensor_tensor(co_re, co_re, s8a, ALU.add)
            v.tensor_tensor(co_im, co_im, frn, ALU.subtract).then_inc(S["s5_co_step"], 1)
            dve.wait_ge(S["s5_co_step"], 4)
            v.tensor_tensor(co_re, co_re, den8, ALU.mult)
            v.tensor_tensor(co_im, co_im, den8, ALU.mult).then_inc(S["s5_co"], 1)

            rests(H_MID + 2)

            def scan(q):
                dve.wait_ge(S["rotating"], 3 * (q + 1))
                for i in range(2):
                    decay = mag[:, 2 * q + i:2 * q + i + 1].to_broadcast([P, T])
                    v.tensor_tensor_scan(t1[:, i, :], decay, t1[:, i, :], 0.0, ALU.mult, ALU.add)
                    last = v.tensor_tensor_scan(t2[:, i, :], decay, t2[:, i, :], 0.0, ALU.mult, ALU.add)
                last.then_inc(S["scanned"], 1)

            o = wait_full(dve, "gates")
            v.tensor_scalar(rows[0][0:NH, :], o[0:NH, T:2 * T], prm("f_bias", NH), None, ALU.add).then_inc(S["ml_gate"], 1)
            v.tensor_scalar(rows[1][0:NH, :], o[0:NH, 0:T], prm("i_bias", NH), None, ALU.add).then_inc(free_of("gates"), 1)
            dve.wait_ge(S["rstd_m"], 1)
            for k in range(KD):
                last = v.scalar_tensor_tensor(mem_h[:, k, :], mem_h[:, k, :], prm("norm_mem")[:, k:k + 1], rstd_m,
                                              ALU.mult, ALU.mult)
            last.then_inc(S["mem_ready"], 1)
            mask2 = cst[:, CONST["strict"][0]:CONST["incl"][1]]
            for i in range(8):
                o = wait_full(dve, f"A{i}")
                v.tensor_tensor(v3(A[:, i, :], 256), v3(o[:, :], 256), copies(mask2, 2), ALU.mult).then_inc(free_of(f"A{i}"), 1)
            for c in range(NC):
                for e in range(2):
                    o = wait_full(dve, f"L{c}{e}")
                    v.tensor_tensor(X[:, c, e:NH:2], v3(o[:, 0:T], P), copies(const("level0_t"), 2),
                                    ALU.mult).then_inc(free_of(f"L{c}{e}"), 1)
                moved(dve, f"L{c}0")
                moved(dve, f"L{c}1")
                v.tensor_tensor(X[:, c], copies(const("ident"), NH), X[:, c], ALU.subtract).then_inc(S["rw_x0"], 1)
            for c in range(NC):
                for i in range(NH * c, NH * (c + 1)):
                    moved(dve, f"A{i}")
                v.tensor_tensor(XT[:, c], A[:, NH * c:NH * (c + 1), 0:P], copies(const("levels")[:, 0:P], NH),
                                ALU.mult).then_inc(S["rw_xt0"], 1)
                dve.wait_ge(S["rw_xt0"], 2 * c + 1)
                v.tensor_tensor(XT[:, c], copies(const("ident"), NH), XT[:, c], ALU.subtract).then_inc(S["rw_xt0"], 1)
            scan(0)
            moved(dve, "ml_q")
            moved(dve, "ml_k")
            dve.wait_ge(S["zeros_ready"], 2)
            cw = v3(prm("conv"), 4)
            for tap in range(4):
                if tap > 0:
                    dve.wait_ge(S["ml_conv"], tap)
                for i in range(4):
                    w, x = cw[:, i, tap:tap + 1], raw[:, i, tap:tap + T]
                    if tap == 0:
                        last = v.tensor_scalar(cv[:, i, :], x, w, None, ALU.mult)
                    else:
                        last = v.scalar_tensor_tensor(cv[:, i, :], x, w, cv[:, i, :], ALU.mult, ALU.add)
                last.then_inc(S["ml_conv"], 1)

            def level_update(n):
                for c in range(NC):
                    if n < LEVELS - 1:
                        o = wait_full(dve, f"X{n}{c}")
                        v.tensor_tensor(X[:, c], X[:, c], v3(o[:, :], P), ALU.subtract).then_inc(free_of(f"X{n}{c}"), 1)
                    o = wait_full(dve, f"T{n}{c}")
                    v.tensor_tensor(XT[:, c], XT[:, c], v3(o[:, :], P), ALU.subtract).then_inc(free_of(f"T{n}{c}"), 1)

            rests(H_MID + 3)
            level_update(1)
            rests(H_MID + 4)
            scan(1)
            dve.wait_ge(S["ml_log"], 3)
            lf, g_, nM, F, em = (rows[i][0:NH, :] for i in (0, 1, 2, 3, 4))
            v.scalar_tensor_tensor(lf, lf, 0.0, F, ALU.min, ALU.subtract).then_inc(S["ml_row_step"], 1)
            dve.wait_ge(S["ml_row_step"], 1)
            one = const("ones", NH)[:, 0:1].to_broadcast([NH, T])
            v.tensor_tensor_scan(F, one, lf, 0.0, ALU.mult, ALU.add).then_inc(S["ml_row_step"], 1)
            dve.wait_ge(S["ml_row_step"], 2)
            v.tensor_tensor(g_, g_, F, ALU.subtract).then_inc(S["ml_rows"], 1)
            dve.wait_ge(S["ml_rows"], 1)
            v.tensor_tensor_scan(lf, g_, g_, 0.0, ALU.max, ALU.max).then_inc(S["ml_row_step"], 1)
            dve.wait_ge(S["ml_row_step"], 3)
            v.tensor_scalar(nM, lf, -1.0, None, ALU.mult).then_inc(S["ml_rows"], 1)
            v.scalar_tensor_tensor(em, F, -1.0, lf, ALU.mult, ALU.subtract).then_inc(S["ml_rows"], 1)
            dve.wait_ge(S["ml_silu"], 1)
            ex = v3(E_[:, 0:1024], T)
            v.tensor_scalar(ex, ex, 1.0, None, ALU.add).then_inc(S["ml_sig"], 1)
            dve.wait_ge(S["ml_sig"], 1)
            v.reciprocal(ex[:, 0:2, :], ex[:, 0:2, :])
            rests(H_MID + 5)
            level_update(2)
            rests(H_MID + 6)
            v.reciprocal(ex[:, 2:4, :], ex[:, 2:4, :]).then_inc(S["ml_sig"], 1)
            dve.wait_ge(S["ml_sig"], 2)
            v.tensor_tensor(cv, cv, ex, ALU.mult).then_inc(S["ml_qk"], 1)
            moved(dve, "g_col")
            dve.wait_ge(S["ml_qk"], 1)
            ca = const("causal_add")
            for m in range(2):
                o = v3(wait_full(dve, f"m_row{m}")[:, :], T)
                for e in range(2):
                    h = 2 * m + e
                    v.scalar_tensor_tensor(E[:, h, 0:T], o[:, e, :], gcol[:, h:h + 1], ca[:, 0:T], ALU.add, ALU.add)
                    last = v.scalar_tensor_tensor(E[:, h, T:T + P], o[:, e, P:T], gcol[:, 4 + h:5 + h], ca[:, T:T + P],
                                                  ALU.add, ALU.add)
                last.then_inc(free_of(f"m_row{m}"), 1)
            level_update(3)
            for j in range(2):
                h_rest(2 + j, mem_h)

            def ml_weight(h):
                o = wait_full(dve, f"qk{h}")
                dve.wait_ge(S["ml_E"], 1)
                v.scalar_tensor_tensor(E[:, h, :], o[:, 0:384], HD ** -0.5, E[:, h, :], ALU.mult,
                                       ALU.mult).then_inc(free_of(f"qk{h}"), 1)

            ml_weight(0)
            ml_weight(1)
            rests(H_WKV + 3)
            level_update(4)
            rests(H_WKV + 4)
            scan(2)
            ml_weight(2)
            ml_weight(3)
            rests(H_WKV + 5)
            level_update(5)
            rests(H_WKV + 6)
            o = wait_full(dve, "den")
            den = v3(raw_cv[:, 0:512], T)
            v.tensor_scalar(den, v3(o[:, :], T), -1.0, None, ALU.mult).then_inc(S["ml_den"], 1)
            dve.wait_ge(S["ml_den"], 1)
            e = wait_full(dve, "em")
            v.tensor_tensor(den, den, v3(e[:, :], T), ALU.max).then_inc(free_of("em"), 1)
            moved(dve, "em")
            v.tensor_tensor(den, den, v3(o[:, :], T), ALU.max).then_inc(free_of("den"), 1)
            moved(dve, "den")
            moved(dve, "ml_o")
            v.scalar_tensor_tensor(den, mlo, 1.0, den, ALU.add, ALU.mult).then_inc(S["ml_den"], 1)
            dve.wait_ge(S["ml_den"], 2)
            v.reciprocal(den, den).then_inc(S["ml_den"], 1)
            dve.wait_ge(S["ml_den"], 3)
            o = wait_full(dve, "num")
            v.tensor_tensor(yT[:, 2:4, :], v3(o[:, :], T), den, ALU.mult).then_inc(free_of("num"), 1)
            rests(H_WKV + 7)
            level_update(6)
            rests(H_WKV + 8)

            def solve_rhs(c):
                o = wait_full(dve, f"R{c}")
                v.tensor_scalar(R_, o[:, 0:GW], -1.0, None, ALU.mult).then_inc(free_of(f"R{c}"), 1)

            def solution(c):
                o = wait_full(dve, f"U{c}")
                v.tensor_copy(U[:, c, :], o[:, 0:GW]).then_inc(free_of(f"U{c}"), 1)

            def mb_biased(h):
                o = wait_full(dve, f"sc{h}")
                dve.wait_ge(S["rel_in"], 16)
                v.scalar_tensor_tensor(Sm[:, h, 0:P], o[:, 0:P], HD ** -0.5, Bz[:, h, P:T], ALU.mult, ALU.add)
                v.scalar_tensor_tensor(Sm[:, h, P:P + T], o[:, P:P + T], HD ** -0.5, Bz[:, h, :], ALU.mult,
                                       ALU.add).then_inc(free_of(f"sc{h}"), 1)

            solve_rhs(0)
            mb_biased(0)
            mb_biased(1)
            rests(H_WKV + 9)
            solution(0)
            rests(H_WKV + 10)
            mb_biased(2)
            mb_biased(3)
            for h in range(NH):
                moved(dve, f"sc{h}")
            v.tensor_reduce(nmax[:, 0:4], Sm[:, :, 0:P], AX.X, ALU.max, negate=True)
            v.tensor_reduce(nmax[:, 4:8], Sm[:, :, P:P + T], AX.X, ALU.max, negate=True).then_inc(S["mb_max"], 1)
            rests(H_WKV + 11)
            o = wait_full(dve, "S0")
            dve.wait_ge(S["zeros_ready"], 3)
            for h in range(NH):
                r, j = at(h)
                last = v.tensor_scalar(S0[r, j, h % 2, :], o[r, j * HD:(j + 1) * HD], carry[r, j:j + 1], None, ALU.mult)
            last.then_inc(free_of("S0"), 1)
            rests(H_WKV + 12)
            solve_rhs(1)
            rests(H_WKV + 13)
            solution(1)
            rests(H_WKV + 14)
            scan(3)
            dve.wait_ge(S["mb_exp"], 1)
            v.reciprocal(mb_sum, mb_sum).then_inc(S["mb_inv"], 1)
            o = wait_full(dve, "rw_y")
            v.tensor_copy(Yrw, v3(o[:, :], T)).then_inc(free_of("rw_y"), 1)
            dve.wait_ge(S["mb_inv"], 1)
            v.tensor_tensor(Sm[:, :, 0:P], Sm[:, :, 0:P], spread(mb_sum[:, 0:4], P), ALU.mult)
            v.tensor_tensor(Sm[:, :, P:P + T], Sm[:, :, P:P + T], spread(mb_sum[:, 4:8], T), ALU.mult).then_inc(S["mb_prob"], 1)
            rests(H_WKV + 15)
            o = wait_full(dve, "mean")
            moved(dve, "rw_y")
            v.scalar_tensor_tensor(flat(Yrw), o[:, :], -1.0 / HD, flat(Yrw), ALU.mult, ALU.add).then_inc(free_of("mean"), 1)
            moved(dve, "mean")
            rests(H_LATE)
            o = v3(wait_full(dve, "s5_y")[:, :], T)
            for j in range(2):
                last = v.scalar_tensor_tensor(z5y[:, j, :], s5u[:, j, :], prm("s5_d")[:, j:j + 1], o[:, j, :],
                                              ALU.mult, ALU.add)
            last.then_inc(free_of("s5_y"), 1)
            moved(dve, "s5_y")
            v.tensor_tensor(z5a, z5y, z5y, ALU.mult).then_inc(S["s5_step2"], 1)
            dve.wait_ge(S["s5_step2"], 1)
            v.tensor_scalar(z5a, z5a, 0.044715, 1.0, ALU.mult, ALU.add).then_inc(S["s5_step2"], 1)
            dve.wait_ge(S["s5_step2"], 2)
            v.tensor_tensor(z5a, z5a, z5y, ALU.mult).then_inc(S["s5_arg"], 1)
            o = wait_full(dve, "mb_o")
            v.tensor_copy(yT[:, 6:8, :], v3(o[:, :], T)).then_inc(free_of("mb_o"), 1)
            dve.wait_ge(S["s5_exp"], 1)
            sigmoid_of_exp(z5b, "s5_sig", 0).then_inc(S["s5_sig"], 1)
            dve.wait_ge(S["s5_sig"], 2)
            v.tensor_tensor(z5, z5y, z5b, ALU.mult).then_inc(S["s5_z"], 1)
            rests(H_LATE + 1)

            def y_rest(turn, g_):
                dve.wait_ge(S["high_ready"], HIGHS["y"] + turn + 1)
                tiles = slice(2 * g_, 2 * g_ + 2)
                v.tensor_tensor(y_split[1][:, tiles, :], yT[:, tiles, :], y_split[0][:, tiles, :].bitcast(F32),
                                ALU.subtract).then_inc(S["y_rest"], 1)

            def group_gain(g_, name):
                dve.wait_ge(S[name + "_root"], 1)
                for j in range(2):
                    k = 2 * g_ + j
                    last = v.scalar_tensor_tensor(yT[:, k, :], yT[:, k, :], prm("mix_gain")[:, k:k + 1],
                                                  gn_sq[g_][:, 0, :], ALU.mult, ALU.mult)
                last.then_inc(S["gn_done"], 1)

            dve.wait_ge(S["rw_rstd"], 1)
            v.tensor_tensor(flat(Yrw), flat(Yrw), Pm_[:, 0:512], ALU.mult).then_inc(S["rw_tail"], 1)
            group_gain(1, "ml")
            group_gain(3, "mb")
            o = v3(wait_full(dve, "bonus")[:, :], T)
            v.tensor_tensor(Ysq, o, rwM[:, 6:8, :], ALU.mult).then_inc(free_of("bonus"), 1)
            y_rest(0, 1)
            y_rest(1, 3)
            dve.wait_ge(S["rw_tail"], 1)
            for j in range(2):
                last = v.tensor_scalar(Yrw[:, j, :], Yrw[:, j, :], prm("ln_w")[:, j:j + 1], prm("ln_b")[:, j:j + 1],
                                       ALU.mult, ALU.add)
            last.then_inc(S["rw_tail"], 1)
            moved(dve, "bonus")
            dve.wait_ge(S["rw_tail"], 2)
            v.tensor_tensor(Yrw, Yrw, Ysq, ALU.add).then_inc(S["rw_tail"], 1)
            dve.wait_ge(S["rw_tail"], 3)
            moved(dve, "rw_g")
            v.tensor_tensor(yT[:, 4:6, :], Yrw, rwg, ALU.mult).then_inc(S["rw_out"], 1)
            rests(H_LATE + 3)
            moved(dve, "glu")
            sigmoid_of_exp(z5b, "s5_sig", 2).then_inc(S["s5_sig"], 1)
            dve.wait_ge(S["s5_sig"], 4)
            v.tensor_tensor(yT[:, 0:2, :], z5, z5b, ALU.mult).then_inc(S["s5_out"], 1)
            rests(H_LATE + 4)
            group_gain(2, "rw")
            y_rest(2, 2)
            rests(H_LATE + 6)
            group_gain(0, "s5")
            y_rest(3, 0)
            rests(H_LATE + 8)

            def post_gain(name, src, m, part):
                w = src[1] - src[0]
                cols = slice(part * w, (part + 1) * w)
                return v.tensor_tensor(xtmp[:, m, cols], wait_full(dve, name)[:, src[0]:src[1]], gain_[:, cols], ALU.mult)

            def post_sum(n, parts):
                v.tensor_reduce(rst, v3(ssq, 4)[:, :, 0:parts], AX.X, ALU.add).then_inc(S["post_sum"], 1)

            def post_norm(n, last):
                dve.wait_ge(S["post_root"], 2 * n + 2)
                moved(dve, last)
                if n == 0:
                    dve.wait_ge(S["xres_in"], 16)
                for m in range(2):
                    v.scalar_tensor_tensor(xres[:, m, :], xtmp[:, m, :], rst[:, m:m + 1], xres[:, m, :], ALU.mult,
                                           ALU.add).then_inc(S["x_new"], 1)

            def projected(n, tag, first):
                dve.wait_ge(S["gain_in"], 16 * (n + 1))
                for i in range(4):
                    dve.wait_ge(S["post_sq"], 4 * n + i + 1)
                    if i == 3:
                        post_sum(n, 4)
                    for m in range(2):
                        e = post_gain(f"{tag}{i}", (256 * m, 256 * m + 256), m, i)
                    e.then_inc(free_of(f"{tag}{i}"), 1)
                    if i < 2:
                        rests(first + i + 1)
                post_norm(n, f"{tag}3")

            def pre_norm(n):
                for m in range(2):
                    dve.wait_ge(S["pre_root"], 6 * n + 3 * (m + 1))
                    v.tensor_scalar(xtmp[:, m, :], xres[:, m, :], rst[:, m:m + 1], None, ALU.mult).then_inc(S["xn_ready"], 1)

            def rest_of_bank(tag, i, out, high, scale=None):
                o = v3(wait_full(dve, f"{tag}{i}")[:, :], T)
                dve.wait_ge(S["high_ready"], HIGHS[tag.replace("xo", "ox")] + i + 1)
                for k in range(2):
                    c = 2 * i + k
                    if scale is None:
                        e = v.tensor_tensor(out[:, c, :], o[:, k, :], high[:, c, :].bitcast(F32), ALU.subtract)
                    else:
                        e = v.scalar_tensor_tensor(out[:, c, :], o[:, k, :], scale[:, c:c + 1],
                                                   high[:, c, :].bitcast(F32), ALU.mult, ALU.subtract)
                e.then_inc(free_of(f"{tag}{i}"), 1)

            projected(0, "wout", H_LATE + 8)
            pre_norm(0)
            for i in range(4):
                rest_of_bank("xat", i, h_split[1], h_split[0], prm("pre_xa"))

            def x_max(h):
                o = v3(wait_full(dve, f"xs{h}")[:, :], NMEM)
                mx = xmax[:, 2 * h:2 * h + 2]
                v.tensor_reduce(mx, o, AX.X, ALU.max, negate=True).then_inc(S["x_max"], 1)
                dve.wait_ge(S["x_max"], 2 * h + 1)
                v.tensor_scalar(mx, mx, XD ** -0.5, None, ALU.mult).then_inc(S["x_max"], 1)

            def x_prob(h):
                moved(dve, f"xs{h}")
                sm = xsum[:, 2 * h:2 * h + 2]
                v.reciprocal(sm, sm).then_inc(S["x_inv"], 1)
                dve.wait_ge(S["x_inv"], h + 1)
                v.tensor_tensor(px[:, h], px[:, h], spread(sm, NMEM), ALU.mult).then_inc(S["x_prob"], 1)

            rests(H_LATE + 14)
            for h in range(XH):
                rests(min(H_LATE + 16 + 2 * h, H_LATE + 20))
                x_max(h)
                if h > 0:
                    x_prob(h - 1)
            x_prob(XH - 1)
            for h in range(XH):
                rest_of_bank("xo", h, ox_split[1], ox_split[0])
            first = 2 * S_FIN
            rests(first)
            projected(1, "wo", first)
            pre_norm(1)
            for i in range(4):
                rest_of_bank("fft", i, h_split[1], h_split[0], prm("pre_ffn"))
            rests(first + 4)

            def act_rest(p):
                dve.wait_ge(S["high_ready"], HIGHS["act"] + p + 1)
                part = [flat(x[:, 2 * p:2 * p + 2, :]) for x in act_split]
                v.tensor_tensor(part[1], fft[:, p % 2, :], part[0].bitcast(F32), ALU.subtract).then_inc(S["act_rest"], 1)

            for p in range(NFF // 2):
                rests(first + 4 * p + 6)
                f = fft[:, p % 2, :]
                dve.wait_ge(S["f_exp"], p + 1)
                sigmoid_of_exp(f, "f_sig", 2 * p).then_inc(S["f_sig"], 1)
                dve.wait_ge(S["f_sig"], 2 * p + 2)
                o = wait_full(dve, f"g{p}")
                v.tensor_tensor(f, f, o[:, :], ALU.mult).then_inc(free_of(f"g{p}"), 1)
                if p > 0:
                    act_rest(p - 1)
                rests(first + 4 * p + 8)
                moved(dve, f"g{p}")
                o = wait_full(dve, f"u{p}")
                v.tensor_tensor(f, f, o[:, :], ALU.mult).then_inc(free_of(f"u{p}"), 1)
            act_rest(NFF // 2 - 1)
            rests(NHALF)
            dve.wait_ge(S["gain_in"], 48)
            for m in range(2):
                for i in range(2):
                    dve.wait_ge(S["post_sq"], 9 + 2 * m + i)
                    if m + i == 2:
                        post_sum(2, 2)
                    post_gain(f"y{2 * m + i}", (0, 512), m, i).then_inc(free_of(f"y{2 * m + i}"), 1)
            for i in range(3):
                moved(dve, f"y{i}")
            post_norm(2, "y3")


def _constants():
    import numpy as np

    c = np.zeros((P, NCONST), np.float32)

    def put(name, a):
        c[:a.shape[0], CONST[name][0]:CONST[name][0] + a.shape[1]] = a

    i = np.arange(P)
    put("ident", np.eye(P))
    put("ones", np.ones((P, P)))
    put("pair_ones", (i[:, None] // HD == i[None, :] // HD) * 1.0)
    put("strict", (i[:, None] < i[None, :]) * 1.0)
    put("incl", (i[:, None] <= i[None, :]) * 1.0)
    diag = np.where(i[:, None] <= i[None, :], 0.0, NEG)
    put("causal_add", np.concatenate([diag, np.zeros((P, P)), diag], axis=1))
    levels = []
    for n in range(LEVELS):
        b = 1 << n
        levels.append(((i[:, None] // (2 * b) == i[None, :] // (2 * b)) & (i[:, None] // b % 2 == 0)
                       & (i[None, :] // b % 2 == 1)) * 1.0)
    put("levels", np.concatenate(levels, axis=1))
    put("level0_t", levels[0].T)
    put("time", np.tile(np.arange(T), (P, 1)))
    put("head_sel", np.repeat(np.eye(NH), P, axis=1))
    put("pair_sel", np.repeat(np.eye(NH), HD, axis=1))
    rel = T - 1 - np.arange(384)
    n = np.maximum(rel, 0)
    large = 16 + (np.log(np.maximum(n, 1).astype(np.float32) / 16) / math.log(128 / 16) * 16).astype(np.int32)
    bucket = np.where(n < 16, n, np.minimum(large, 31))
    hot = np.zeros((33, 384))
    hot[bucket, np.arange(384)] = rel >= 0
    hot[32] = np.where(rel < 0, NEG, 0.0)
    put("onehot", hot)
    for name, value in (("eps6", 1e-6), ("eps12", 1e-12), ("eps_gn", 64e-5), ("half_pi", math.pi / 2)):
        put(name, np.full((P, 1), value))
    return c


def _parameters(a):
    import numpy as np

    p = np.zeros((P, NPARAM), np.float32)

    def put(name, block, at=0):
        lo = PARAM[name][0] + at
        p[:block.shape[0], lo:lo + block.shape[1]] = block

    def channels(v):
        return v.reshape(-1, P).T

    mu = a["rw_mu"][0]
    put("mu", channels(np.concatenate([mu[768:1024], mu[256:512], mu[0:256], mu[512:768]])))
    for name, src in (("w0", "rw_w0"), ("a0", "rw_a0"), ("k_k", "rw_k_k"), ("k_a", "rw_k_a"), ("r_k", "rw_r_k"),
                      ("ln_w", "rw_ln_w"), ("ln_b", "rw_ln_b"), ("s5_d", "s5_d"), ("b_glu", "s5_b_glu"),
                      ("mix_gain", "mix_out_gain"), ("pre_mix", "norm_pre_mix"), ("pre_xa", "norm_pre_xa"),
                      ("pre_ffn", "norm_pre_ffn"), ("norm_mem", "norm_mem"), ("lam_re", "s5_lam_re"),
                      ("lam_im", "s5_lam_im")):
        put(name, channels(a[src][0]))
    put("conv", a["ml_conv"][0].reshape(4, 4, P).transpose(2, 1, 0).reshape(P, 16))
    put("log_step", channels(np.repeat(a["s5_log_step"][0], 64)))
    put("i_bias", a["ml_i_bias"][0].reshape(NH, 1))
    put("f_bias", a["ml_f_bias"][0].reshape(NH, 1))
    put("rel", a["rel_bias"])
    p[32, PARAM["rel"][0]:PARAM["rel"][1]] = 1.0
    gate = a["w_in"][0][:, 1280:1288]
    put("w_gate", gate.reshape(KD, P, 8).transpose(1, 0, 2).reshape(P, KD * 8))
    put("w2a2", np.concatenate([a["rw_w2"][0], a["rw_a2"][0]], axis=0))
    put("g2", a["rw_g2"][0])
    put("w_glu", a["s5_w_glu"][0].reshape(2, P, GW).transpose(1, 0, 2).reshape(P, 2 * GW))
    for name, src in (("b_re", "s5_b_re"), ("b_im", "s5_b_im")):
        b = np.zeros((4, 2, 16, 2, 2, 64), np.float32)
        w = a[src][0].reshape(2, 4, 2, 64, 16)
        for g in range(2):
            b[:, g, :, :, g, :] = w[:, :, g].transpose(1, 3, 0, 2)
        put(name, b.reshape(P, 256))
    for name, src in (("c_re", "s5_c_re"), ("c_im", "s5_c_im")):
        c = np.zeros((2, 64, 8, 2, 16), np.float32)
        w = a[src][0].reshape(8, 2, 16, 64)
        for g in range(2):
            c[g, :, :, g, :] = w[:, g].transpose(2, 0, 1)
        put(name, c.reshape(P, 256))
    return p


def _weight_slots(a):
    import numpy as np

    def columns_of(w):
        n = w.shape[1] // 256
        return w.reshape(KD, P, n, 256).transpose(2, 1, 0, 3).reshape(n, P, SLOT)

    w = a["w_in"][0]
    ml, rw, mb = GW, GW + 4 * GW + 8, GW + 4 * GW + 8 + 1024
    first = {"rw_wag": rw + 768, "rw_k": rw + 256, "rw_r": rw, "rw_v": rw + 512, "s5_u": 0, "ml_q": ml,
             "ml_k": ml + 256, "ml_v": ml + 512, "ml_o": ml + 768, "mb_q": mb, "mb_k": mb + 256, "mb_v": mb + 512}
    parts = [columns_of(w[:, first[n]:first[n] + 256]) for n in W_IN_ORDER]

    def halves_of(w, order):
        w = w.reshape(KD, P, 4, 256)[order].reshape(2, 4, P, 4, 256)
        halves = w.transpose(0, 3, 2, 1, 4).reshape(4, 2, P, HALF)
        return halves.transpose(0, 2, 1, 3).reshape(4, P, SLOT)

    parts += [columns_of(a["xa_wkv"][0]), halves_of(a["w_out"][0], Y_ORDER), columns_of(a["xa_wq"][0]),
              halves_of(a["xa_wo"][0], list(range(KD)))]
    gu = columns_of(a["ffn_w_in"][0])
    half = NFF // 2
    parts.append(np.stack([gu[:half], gu[half:]], axis=1).reshape(2 * half, P, SLOT))
    parts.append(a["ffn_w_out"][0].reshape(half, 2, P, D).transpose(0, 2, 1, 3).reshape(half, P, SLOT))
    return np.concatenate(parts, axis=0)


def kernel(**inputs):
    import numpy as np
    import concourse.bacc as bacc
    from concourse.bass_utils import run_bass_kernel_spmd

    a = {name: np.asarray(value) for name, value in inputs.items()}
    arrays = {
        "x_t": a["x"][0].T.reshape(KD, P, T).transpose(1, 0, 2).reshape(P, KD * T),
        "x_rows": a["x"][0],
        "mem_t": a["mem"][0].T.reshape(KD, P, NMEM).transpose(1, 0, 2).reshape(P, KD * NMEM),
        "consts": _constants(),
        "params": _parameters(a),
        "weights": _weight_slots(a),
        "gains": np.concatenate([a["norm_post_mix"], a["norm_post_xa"], a["norm_post_ffn"]], axis=0),
    }
    arrays = {name: np.ascontiguousarray(v) for name, v in arrays.items()}
    nc = bacc.Bacc("TRN2", target_bir_lowering=False, num_devices=1)
    aps = {name: nc.dram_tensor(name, v.shape, F32, kind="ExternalInput").ap() for name, v in arrays.items()}
    rel_scratch = nc.dram_tensor("rel_scratch", (P, NH * 384), F32)
    out = nc.dram_tensor("out", (1, T, D), F32, kind="ExternalOutput").ap()
    trunk_kernel(nc, aps["x_t"], aps["x_rows"], aps["mem_t"], aps["consts"], aps["params"], aps["weights"],
                 aps["gains"], rel_scratch, out)
    r = run_bass_kernel_spmd(nc, [arrays], core_ids=[0])
    return r.results[0]["out"]
```
